# Optimizing a Trainium2 kernel written in Bass

```python
import jax, jax.numpy as jnp
from jax import lax
import numpy as np
import math

D_MODEL = 1024
BATCH = 1
SEQ = 256
DEPTH = 2

N_A_LAYERS = DEPTH // 2
N_B_LAYERS = DEPTH - N_A_LAYERS
D_FF = 2816
CHUNK = 128
GMLP_HALF = 2 * D_MODEL
GMLP_GROUPS = 16
GMLP_GROUP_DIM = GMLP_HALF // GMLP_GROUPS
N_HEADS = 8
QK_NOPE = 128
QK_ROPE = 64
V_DIM = 128
KV_RANK = 256
Q_RANK = 512
Q_BLOCK = 128
ROPE_THETA = 10000.0
RMS_EPS = 1e-6
LN_EPS = 1e-5
NEG_INF = -1e30


def rms_norm(x, g):
    x32 = x.astype(jnp.float32)
    y = x32 * lax.rsqrt(jnp.mean(x32 * x32, axis=-1, keepdims=True) + RMS_EPS) * g.astype(jnp.float32)
    return y.astype(x.dtype)

def layer_norm(x, g, b):
    x32 = x.astype(jnp.float32)
    mu = jnp.mean(x32, axis=-1, keepdims=True)
    xc = x32 - mu
    y = xc * lax.rsqrt(jnp.mean(xc * xc, axis=-1, keepdims=True) + LN_EPS)
    return (y * g.astype(jnp.float32) + b.astype(jnp.float32)).astype(x.dtype)

def swiglu(n, w_gate, w_up, w_down):
    return (jax.nn.silu(n @ w_gate) * (n @ w_up)) @ w_down

def rope_tables(positions):
    inv_freq = ROPE_THETA ** (-jnp.arange(0, QK_ROPE, 2, dtype=jnp.float32) / QK_ROPE)
    ang = positions.astype(jnp.float32)[..., None] * inv_freq
    return jnp.cos(ang), jnp.sin(ang)

def apply_rope(x, cos, sin):
    cos = cos.astype(x.dtype)
    sin = sin.astype(x.dtype)
    x1, x2 = jnp.split(x, 2, axis=-1)
    return jnp.concatenate([x1 * cos - x2 * sin, x2 * cos + x1 * sin], axis=-1)

def gmlp_mixer(n, w_in, ln_g, ln_b, w_s, b_s, w_out):
    b, s, _ = n.shape
    z = jax.nn.gelu(n @ w_in)
    u, v = jnp.split(z, 2, axis=-1)
    v = layer_norm(v, ln_g, ln_b)
    v = v.reshape(b, s // CHUNK, CHUNK, GMLP_GROUPS, GMLP_GROUP_DIM)
    causal = jnp.tril(jnp.ones((CHUNK, CHUNK), dtype=w_s.dtype))
    w = w_s * causal
    sv = jnp.einsum('gtc,bncgd->bntgd', w, v) + jnp.transpose(b_s)[None, None, :, :, None]
    return (u * sv.reshape(b, s, GMLP_HALF)) @ w_out

def shared_kv(h, kv_norm_g, w_dkv, kv_a_norm_g, w_ukv, cos, sin):
    b, s, _ = h.shape
    n = rms_norm(h, kv_norm_g)
    ckv = n @ w_dkv
    c, k_rope = ckv[..., :KV_RANK], ckv[..., KV_RANK:]
    c = rms_norm(c, kv_a_norm_g)
    k_rope = apply_rope(k_rope, cos, sin)
    kv = (c @ w_ukv).reshape(b, s, N_HEADS, QK_NOPE + V_DIM)
    return kv[..., :QK_NOPE], k_rope, kv[..., QK_NOPE:]

def mla_mixer(n, k_nope, k_rope, v, w_dq, q_norm_g, w_uq, w_o, cos, sin):
    b, s, _ = n.shape
    q = (rms_norm(n @ w_dq, q_norm_g) @ w_uq).reshape(b, s, N_HEADS, QK_NOPE + QK_ROPE)
    q_nope = q[..., :QK_NOPE]
    q_rope = apply_rope(q[..., QK_NOPE:], cos[:, :, None, :], sin[:, :, None, :])
    scale = (QK_NOPE + QK_ROPE) ** -0.5
    outs = []
    for blk in range(s // Q_BLOCK):
        q0, q1 = blk * Q_BLOCK, (blk + 1) * Q_BLOCK
        sc = (jnp.einsum('bqhd,bkhd->bhqk', q_nope[:, q0:q1], k_nope[:, :q1])
              + jnp.einsum('bqhr,bkr->bhqk', q_rope[:, q0:q1], k_rope[:, :q1]))
        sc = sc.astype(jnp.float32) * scale
        q_idx = q0 + jnp.arange(Q_BLOCK)
        k_idx = jnp.arange(q1)
        sc = jnp.where(k_idx[None, :] <= q_idx[:, None], sc, NEG_INF)
        p = jax.nn.softmax(sc, axis=-1).astype(v.dtype)
        outs.append(jnp.einsum('bhqk,bkhd->bqhd', p, v[:, :q1]))
    o = jnp.concatenate(outs, axis=1).reshape(b, s, N_HEADS * V_DIM)
    return o @ w_o

def first_inputs(seed: int = 0) -> dict:
    key = jax.random.key(seed)
    ks = iter(jax.random.split(key, 40))

    def w(shape, fan_in):
        return jax.random.normal(next(ks), shape, jnp.float32) * (fan_in ** -0.5)

    def g(shape):
        return 1.0 + 0.02 * jax.random.normal(next(ks), shape, jnp.float32)

    x = jax.random.normal(next(ks), (BATCH, SEQ, D_MODEL), jnp.float32)
    offs = jax.random.randint(next(ks), (BATCH, 1), 0, 1024, dtype=jnp.int32)
    positions = (jnp.arange(SEQ, dtype=jnp.int32)[None, :] + offs).astype(jnp.int32)
    return {
        "x": x,
        "positions": positions,
        "ffn_pre_g": g((DEPTH, 2, D_MODEL)),
        "ffn_post_g": g((DEPTH, 2, D_MODEL)),
        "ffn_w_gate": w((DEPTH, 2, D_MODEL, D_FF), D_MODEL),
        "ffn_w_up": w((DEPTH, 2, D_MODEL, D_FF), D_MODEL),
        "ffn_w_down": w((DEPTH, 2, D_FF, D_MODEL), D_FF),
        "mix_pre_g": g((DEPTH, D_MODEL)),
        "mix_post_g": g((DEPTH, D_MODEL)),
        "gmlp_w_in": w((N_A_LAYERS, D_MODEL, 2 * GMLP_HALF), D_MODEL),
        "gmlp_ln_g": g((N_A_LAYERS, GMLP_HALF)),
        "gmlp_ln_b": 0.02 * jax.random.normal(next(ks), (N_A_LAYERS, GMLP_HALF), jnp.float32),
        "gmlp_w_s": w((N_A_LAYERS, GMLP_GROUPS, CHUNK, CHUNK), CHUNK),
        "gmlp_b_s": g((N_A_LAYERS, GMLP_GROUPS, CHUNK)),
        "gmlp_w_out": w((N_A_LAYERS, GMLP_HALF, D_MODEL), GMLP_HALF),
        "kv_norm_g": g((D_MODEL,)),
        "w_dkv": w((D_MODEL, KV_RANK + QK_ROPE), D_MODEL),
        "kv_a_norm_g": g((KV_RANK,)),
        "w_ukv": w((KV_RANK, N_HEADS * (QK_NOPE + V_DIM)), KV_RANK),
        "mla_w_dq": w((N_B_LAYERS, D_MODEL, Q_RANK), D_MODEL),
        "mla_q_norm_g": g((N_B_LAYERS, Q_RANK)),
        "mla_w_uq": w((N_B_LAYERS, Q_RANK, N_HEADS * (QK_NOPE + QK_ROPE)), Q_RANK),
        "mla_w_o": w((N_B_LAYERS, N_HEADS * V_DIM, D_MODEL), N_HEADS * V_DIM),
    }

def first_block(x, positions, ffn_pre_g, ffn_post_g, ffn_w_gate, ffn_w_up, ffn_w_down,
              mix_pre_g, mix_post_g, gmlp_w_in, gmlp_ln_g, gmlp_ln_b, gmlp_w_s, gmlp_b_s,
              gmlp_w_out, kv_norm_g, w_dkv, kv_a_norm_g, w_ukv, mla_w_dq, mla_q_norm_g,
              mla_w_uq, mla_w_o):
    cos, sin = rope_tables(positions)
    h = x
    k_nope = k_rope = v = None
    for layer in range(DEPTH):
        f = swiglu(rms_norm(h, ffn_pre_g[layer, 0]), ffn_w_gate[layer, 0], ffn_w_up[layer, 0], ffn_w_down[layer, 0])
        h = h + 0.5 * rms_norm(f, ffn_post_g[layer, 0])
        n = rms_norm(h, mix_pre_g[layer])
        if layer < N_A_LAYERS:
            m = gmlp_mixer(n, gmlp_w_in[layer], gmlp_ln_g[layer], gmlp_ln_b[layer],
                           gmlp_w_s[layer], gmlp_b_s[layer], gmlp_w_out[layer])
        else:
            j = layer - N_A_LAYERS
            m = mla_mixer(n, k_nope, k_rope, v, mla_w_dq[j], mla_q_norm_g[j], mla_w_uq[j], mla_w_o[j], cos, sin)
        h = h + rms_norm(m, mix_post_g[layer])
        f = swiglu(rms_norm(h, ffn_pre_g[layer, 1]), ffn_w_gate[layer, 1], ffn_w_up[layer, 1], ffn_w_down[layer, 1])
        h = h + 0.5 * rms_norm(f, ffn_post_g[layer, 1])
        if layer == N_A_LAYERS - 1:
            k_nope, k_rope, v = shared_kv(h, kv_norm_g, w_dkv, kv_a_norm_g, w_ukv, cos, sin)
    return h


DEPTH_2 = 1

RET_HEADS = 4
RET_DK = 64
RET_DV = 128
RET_QK = RET_HEADS * RET_DK
RET_V = RET_HEADS * RET_DV
FOX_HEADS = 8
FOX_DH = 64
FOX_W = FOX_HEADS * FOX_DH
D_FF_2 = -(-8 * D_MODEL // (3 * 256)) * 256
ROPE_BASE = 10000.0
EPS = 1e-6
IN_SIZES = (RET_QK, RET_QK, RET_V, RET_V, FOX_W, FOX_W, FOX_W, FOX_HEADS, D_MODEL, D_MODEL)
IN_COLS = sum(IN_SIZES)


def rmsnorm(x, g):
    xf = x.astype(jnp.float32)
    y = xf * lax.rsqrt(jnp.mean(xf * xf, axis=-1, keepdims=True) + EPS)
    return (y * g.astype(jnp.float32)).astype(x.dtype)

def rotary(x, pos):
    half = x.shape[-1] // 2
    inv_freq = 1.0 / (ROPE_BASE ** (jnp.arange(half, dtype=jnp.float32) / half))
    ang = pos[:, None] * inv_freq[None, :]
    cos = jnp.cos(ang)[None, :, None, :]
    sin = jnp.sin(ang)[None, :, None, :]
    xf = x.astype(jnp.float32)
    x1, x2 = xf[..., :half], xf[..., half:]
    return jnp.concatenate([x1 * cos - x2 * sin, x1 * sin + x2 * cos], axis=-1)

def retention_chunkwise(q, k, v):
    B, S, H, dk = q.shape
    dv = v.shape[-1]
    n = S // CHUNK
    log_g = jnp.log1p(-(2.0 ** (-5.0 - jnp.arange(H, dtype=jnp.float32))))
    qc = q.astype(jnp.float32).reshape(B, n, CHUNK, H, dk)
    kc = k.astype(jnp.float32).reshape(B, n, CHUNK, H, dk)
    vc = v.astype(jnp.float32).reshape(B, n, CHUNK, H, dv)
    idx = jnp.arange(CHUNK, dtype=jnp.float32)
    diff = idx[:, None] - idx[None, :]
    decay = jnp.where(diff[None] >= 0, jnp.exp(jnp.maximum(diff, 0.0)[None] * log_g[:, None, None]), 0.0)
    scores = jnp.einsum('bnihd,bnjhd->bnhij', qc, kc) * decay[None, None]
    intra = jnp.einsum('bnhij,bnjhe->bnihe', scores, vc)
    zeta = jnp.exp((CHUNK - 1.0 - idx)[None, :] * log_g[:, None])
    chunk_kv = jnp.einsum('bnjhd,hj,bnjhe->bnhde', kc, zeta, vc)
    g_chunk = jnp.exp(CHUNK * log_g)[:, None, None]

    def step(r_prev, kv):
        return g_chunk * r_prev + kv, r_prev

    r0 = jnp.zeros((B, H, dk, dv), jnp.float32)
    _, states = lax.scan(step, r0, jnp.moveaxis(chunk_kv, 1, 0))
    states = jnp.moveaxis(states, 0, 1)
    xi = jnp.exp((idx + 1.0)[None, :] * log_g[:, None]).T
    inter = jnp.einsum('bnihd,bnhde->bnihe', qc, states) * xi[None, None, :, :, None]
    return (intra + inter).reshape(B, S, H, dv)

def forgetting_attention(q, k, v, log_f):
    B, S, H, d = q.shape
    nb = S // Q_BLOCK
    scale = 1.0 / math.sqrt(d)
    c = jnp.cumsum(log_f, axis=1).transpose(0, 2, 1)
    qh = q.transpose(0, 2, 1, 3)
    kh = k.transpose(0, 2, 1, 3)
    vh = v.transpose(0, 2, 1, 3)
    qb = qh.reshape(B, H, nb, Q_BLOCK, d).transpose(2, 0, 1, 3, 4)
    cb = c.reshape(B, H, nb, Q_BLOCK).transpose(2, 0, 1, 3)
    pos_k = jnp.arange(S)

    def block(args):
        i, q_blk, c_blk = args
        s = jnp.einsum('bhqd,bhkd->bhqk', q_blk, kh).astype(jnp.float32) * scale
        s = s + c_blk[..., None] - c[:, :, None, :]
        pos_q = i * Q_BLOCK + jnp.arange(Q_BLOCK)
        mask = pos_k[None, :] <= pos_q[:, None]
        s = jnp.where(mask[None, None], s, -jnp.inf)
        p = jax.nn.softmax(s, axis=-1)
        return jnp.einsum('bhqk,bhkd->bhqd', p.astype(vh.dtype), vh)

    out = lax.map(block, (jnp.arange(nb), qb, cb))
    return out.transpose(1, 2, 0, 3, 4).reshape(B, H, S, d).transpose(0, 2, 1, 3)

def split_cols(z):
    offs = np.cumsum(np.array(IN_SIZES))[:-1].tolist()
    return jnp.split(z, offs, axis=-1)

def second_inputs(seed: int = 0) -> dict:
    key = jax.random.key(seed)
    ks = jax.random.split(key, 16)
    f32 = jnp.float32
    nrm = lambda k, shp: jax.random.normal(k, shp, f32)
    L = DEPTH_2
    return {
        "x": nrm(ks[0], (BATCH, SEQ, D_MODEL)),
        "g_mix": 1.0 + 0.02 * nrm(ks[1], (L, D_MODEL)),
        "w_in": nrm(ks[2], (L, D_MODEL, IN_COLS)) * D_MODEL ** -0.5,
        "b_forget": 1.0 + 0.5 * nrm(ks[3], (L, FOX_HEADS)),
        "g_ret_norm": 1.0 + 0.02 * nrm(ks[4], (L, RET_V)),
        "w_ret_o": nrm(ks[5], (L, RET_V, D_MODEL)) * RET_V ** -0.5,
        "g_fox_q": 1.0 + 0.02 * nrm(ks[6], (L, FOX_DH)),
        "g_fox_k": 1.0 + 0.02 * nrm(ks[7], (L, FOX_DH)),
        "w_fox_o": nrm(ks[8], (L, FOX_W, D_MODEL)) * FOX_W ** -0.5,
        "w_out": nrm(ks[9], (L, D_MODEL, D_MODEL)) * D_MODEL ** -0.5,
        "g_ffn": 1.0 + 0.02 * nrm(ks[10], (L, D_MODEL)),
        "w_gate": nrm(ks[11], (L, D_MODEL, D_FF_2)) * D_MODEL ** -0.5,
        "w_up": nrm(ks[12], (L, D_MODEL, D_FF_2)) * D_MODEL ** -0.5,
        "w_down": nrm(ks[13], (L, D_FF_2, D_MODEL)) * D_FF_2 ** -0.5,
    }

def second_block(x, g_mix, w_in, b_forget, g_ret_norm, w_ret_o, g_fox_q, g_fox_k, w_fox_o,
              w_out, g_ffn, w_gate, w_up, w_down):
    B, S, _ = x.shape
    pos = jnp.arange(S, dtype=jnp.float32)
    for l in range(DEPTH_2):
        h = rmsnorm(x, g_mix[l])
        z = h @ w_in[l]
        q_r, k_r, v_r, gt_r, q_f, k_f, v_f, f_f, a_r, a_f = split_cols(z)

        q_r = rotary(q_r.reshape(B, S, RET_HEADS, RET_DK), pos)
        k_r = rotary(k_r.reshape(B, S, RET_HEADS, RET_DK), pos) * (RET_DK ** -0.5)
        v_r = v_r.reshape(B, S, RET_HEADS, RET_DV)
        o_r = retention_chunkwise(q_r, k_r, v_r)
        mu = jnp.mean(o_r, axis=-1, keepdims=True)
        var = jnp.mean(jnp.square(o_r - mu), axis=-1, keepdims=True)
        o_r = ((o_r - mu) * lax.rsqrt(var + EPS)).reshape(B, S, RET_V) * g_ret_norm[l].astype(jnp.float32)
        o_r = (jax.nn.silu(gt_r.astype(jnp.float32)) * o_r).astype(x.dtype)
        y_r = o_r @ w_ret_o[l]

        q_f = rmsnorm(q_f.reshape(B, S, FOX_HEADS, FOX_DH), g_fox_q[l])
        k_f = rmsnorm(k_f.reshape(B, S, FOX_HEADS, FOX_DH), g_fox_k[l])
        v_f = v_f.reshape(B, S, FOX_HEADS, FOX_DH)
        log_f = jax.nn.log_sigmoid(f_f.astype(jnp.float32) + b_forget[l].astype(jnp.float32))
        o_f = forgetting_attention(q_f, k_f, v_f, log_f).reshape(B, S, FOX_W).astype(x.dtype)
        y_f = o_f @ w_fox_o[l]

        merged = (jax.nn.sigmoid(a_r.astype(jnp.float32)) * y_r.astype(jnp.float32)
                  + jax.nn.sigmoid(a_f.astype(jnp.float32)) * y_f.astype(jnp.float32)).astype(x.dtype)
        x = x + merged @ w_out[l]

        h2 = rmsnorm(x, g_ffn[l])
        ff = (jax.nn.silu(h2 @ w_gate[l]) * (h2 @ w_up[l])) @ w_down[l]
        x = x + ff
    return x


def setup_inputs(seed=0):
    out = dict(first_inputs(seed))
    for name, value in second_inputs(seed + 1).items():
        if name != "x":
            out[name + "_2"] = value
    return out


def reference(
    x, positions, ffn_pre_g, ffn_post_g, ffn_w_gate, ffn_w_up, ffn_w_down, mix_pre_g,
    mix_post_g, gmlp_w_in, gmlp_ln_g, gmlp_ln_b, gmlp_w_s, gmlp_b_s, gmlp_w_out, kv_norm_g,
    w_dkv, kv_a_norm_g, w_ukv, mla_w_dq, mla_q_norm_g, mla_w_uq, mla_w_o, g_mix_2, w_in_2,
    b_forget_2, g_ret_norm_2, w_ret_o_2, g_fox_q_2, g_fox_k_2, w_fox_o_2, w_out_2, g_ffn_2,
    w_gate_2, w_up_2, w_down_2,
):
    x = first_block(
        x, positions, ffn_pre_g, ffn_post_g, ffn_w_gate, ffn_w_up, ffn_w_down, mix_pre_g,
        mix_post_g, gmlp_w_in, gmlp_ln_g, gmlp_ln_b, gmlp_w_s, gmlp_b_s, gmlp_w_out, kv_norm_g,
        w_dkv, kv_a_norm_g, w_ukv, mla_w_dq, mla_q_norm_g, mla_w_uq, mla_w_o,
    )
    return second_block(
        x, g_mix_2, w_in_2, b_forget_2, g_ret_norm_2, w_ret_o_2, g_fox_q_2, g_fox_k_2,
        w_fox_o_2, w_out_2, g_ffn_2, w_gate_2, w_up_2, w_down_2,
    )


_drawn_inputs = setup_inputs


def setup_inputs(seed=0):
    import zlib

    import numpy as np

    out = dict(_drawn_inputs(seed))
    spreads = {}
    factors = {'ffn_post_g': 3.545,
     'mix_pre_g': 2.775,
     'gmlp_ln_g': 6.568,
     'gmlp_ln_b': 6.641,
     'gmlp_b_s': 4.179,
     'kv_norm_g': 4.416,
     'kv_a_norm_g': 4.601,
     'mla_q_norm_g': 8.0,
     'g_mix_2': 6.411,
     'g_ret_norm_2': 8.0,
     'g_fox_q_2': 8.0,
     'g_fox_k_2': 8.0,
     'g_ffn_2': 7.154}
    for name, (base, spread) in spreads.items():
        noise = np.random.default_rng([zlib.crc32(name.encode()), seed]).standard_normal(out[name].shape)
        drawn = base * np.exp(spread * noise) if base else spread * noise
        out[name] = __import__('jax').numpy.asarray(drawn.astype(out[name].dtype))
    for name, factor in factors.items():
        out[name] = (out[name] * factor).astype(out[name].dtype)
    return out
```

```python
from contextlib import ExitStack
import math

import numpy as np

import concourse.bass as bass
from concourse import mybir

ALU = mybir.AluOpType
ACT = mybir.ActivationFunctionType
AX_X = mybir.AxisListType.X
F32 = mybir.dt.float32
F32R = mybir.dt.float32r
I32 = mybir.dt.int32

P = 128
BANK = 512
SLOTS = 6
UNIT = 1024
RMS_EPS = 1e-6
LN_EPS = 1e-5
ROPE_BASE = 10000.0
NEG = -1e30
TWO_PI = (6.28125, 0.0019350051879882812, 3.0199159819567926e-07)
PI_DOWN = 3.141592502593994
ROUND = 1.5 * 2.0 ** 23


def shape_constants(s, rope, heads_r):
    f = np.float32
    i = np.arange(P)
    causal = np.where(i[None, :] <= i[:, None], 0.0, NEG)
    out = {
        "c_ident": np.eye(P),
        "c_mask": np.concatenate([causal, np.zeros((P, P)), causal], 1),
        "c_upto": (i[:, None] <= i[None, :]).astype(f),
        "c_ones": np.ones((P, P)),
    }
    sel = np.zeros((8, 8, P))
    for h in range(8):
        sel[h, h] = 1.0
    out["c_sel"] = sel.reshape(8, 8 * P)
    half = rope // 2
    out["c_freq"] = np.broadcast_to(ROPE_BASE ** (-np.arange(half) / half), (P, half))
    freq = (1.0 / (ROPE_BASE ** (np.arange(half, dtype=f) / f(half))).astype(f)).astype(f)
    ang = (np.arange(s, dtype=f)[:, None] * freq[None, :]).astype(f).astype(np.float64)
    out["c_cos"], out["c_sin"] = np.cos(ang), np.sin(ang)
    log_g = np.log1p(-(2.0 ** (-5.0 - np.arange(heads_r))))
    diff = np.arange(2 * P)[None, :] - i[:, None]
    d = np.where(diff[None] >= 0, np.exp(np.maximum(diff, 0)[None] * log_g[:, None, None]), 0.0) * rope ** -0.5
    d = np.concatenate([d, d[:, :, :P]], 2)
    out["c_decay"] = np.transpose(d, (1, 0, 2)).reshape(P, heads_r * 3 * P)
    return {k: np.ascontiguousarray(v, dtype=f) for k, v in out.items()}


def build(nc, a, out):
    S, D = a["x"].shape[1:]
    TT = S // P
    KC = D // P
    F = a["ffn_w_gate"].shape[-1]
    FT = 256
    NF = F // FT
    HALF = a["gmlp_ln_g"].shape[-1]
    GROUPS = a["gmlp_w_s"].shape[1]
    GD = HALF // GROUPS
    R_KV = a["kv_a_norm_g"].shape[0]
    R_Q = a["mla_q_norm_g"].shape[1]
    ROPE = a["w_dkv"].shape[1] - R_KV
    H = 8
    NOPE = P
    QW = NOPE + ROPE
    KVW = 2 * P
    HR = 4
    ZW = a["w_in_2"].shape[-1]
    RH = ROPE // 2
    assert TT == 2 and KC == 8 and F % FT == 0 and GD == P and ROPE == 64 and a["w_ukv"].shape[1] == H * KVW
    assert a["mla_w_uq"].shape[2] == H * QW
    Z_QR, Z_KR, Z_VR, Z_GT, Z_QF, Z_KF, Z_VF, Z_F, Z_AR, Z_AF = 0, 256, 512, 1024, 1536, 2048, 2560, 3072, 3080, 4104
    assert ZW == Z_AF + D
    MLA_SCALE = float(QW) ** -0.5

    ctx = ExitStack()
    with ctx:
        def sb(name, shape, dt=F32):
            return ctx.enter_context(nc.sbuf_tensor(name, shape, dt))

        sems = {}

        def sem(name):
            if name not in sems:
                sems[name] = ctx.enter_context(nc.semaphore(name))
            return sems[name]

        raw = sb("raw", [P, SLOTS, UNIT])
        whi = sb("whi", [P, SLOTS, UNIT], F32R)
        wlo = sb("wlo", [P, SLOTS, UNIT], F32R)
        kthi = sb("kthi", [P, 16, S], F32R)
        ktlo = sb("ktlo", [P, 16, S], F32R)
        hthi = sb("hthi", [P, 2, S], F32R)
        htlo = sb("htlo", [P, 2, S], F32R)
        zero = sb("zero", [P, P], F32R)
        h = sb("h", [P, TT, D])
        fg = sb("fg", [P, TT, D])
        gpost = sb("gpost", [P, 2, D])
        hid = sb("hid", [P, TT, FT])
        ident = sb("ident", [P, P])
        mask = sb("mask", [P, 3 * P])
        gcol = sb("gcol", [P, P])
        half_neg = sb("half_neg", [P, 40])
        stat = sb("stat", [P, 400])
        rcos = sb("rcos", [P, TT, RH])
        rsin = sb("rsin", [P, TT, RH])
        arena = sb("arena", [P, 16384])
        sq_out = sb("sq_out", [P, TT, D], mybir.dt.bfloat16)
        ps = ctx.enter_context(nc.psum_tensor("ps", [P, 8, BANK], F32))

        def view(at, *dims):
            n = math.prod(dims)
            v = arena[:, at:at + n]
            names = "abcd"[:len(dims)]
            if len(dims) == 1:
                return v
            return v.rearrange(f"p ({' '.join(names)}) -> p {' '.join(names)}", **dict(zip(names[1:], dims[1:])))

        u_sb, v_sb = view(0, TT, HALF), view(4096, TT, HALF)
        ws_sb, wst = view(8192, GROUPS, P), view(10240, GROUPS, P)
        ln_g, ln_b = view(12288, HALF), view(14336, HALF)
        grow = view(0, P)
        freq = view(256, RH)
        posf = view(320, TT)
        ang, turns, red, whole = view(384, TT, RH), view(448, TT, RH), view(512, TT, RH), view(576, TT, RH)
        pos_i = sb("pos_i", [P, TT], I32)
        ckv = view(0, TT, R_KV + ROPE)
        krope2 = view(640, TT, 2, ROPE)
        krt = view(896, S)
        knt = view(1152, H, S)
        v_mla = view(3200, TT, H * P)
        qlat = view(5248, TT, R_Q)
        qnt = view(6272, H, S)
        qrope = view(8320, TT, H, ROPE)
        qrt = view(9344, H // 2, S)
        rope_t = view(10368, 2, H * RH)
        p_sb = view(10880, 2, 3 * P)
        pt_sb = view(11648, 2, 3 * P)
        z = view(0, TT, ZW)
        o = TT * ZW
        turned = view(o, 8, S)
        ro_t = view(o + 2048, 2, 512)
        st_sb = view(o + 3072, 2, 3 * P)
        pt2_sb = view(o + 3840, 2, 3 * P)
        decay = view(o + 3840, HR, 3 * P)
        assert o + 5952 <= 16384
        gfox = gpost
        upto = view(o + 2048, P)
        ones = view(o + 2048 + P, P)
        sel = view(o + 4608, 8, P)
        cos2, sin2 = sb("cos2", [P, TT, RH]), sb("sin2", [P, TT, RH])
        bfor = sb("bfor", [P, 8])
        logf, cum = view(o + 5888, 3, TT * 8), view(o + 5936, TT, 8)
        ncumt = view(o + 5632, S)[0:8]

        gain_col = {}
        gain_rows = []
        row = 0
        for name, ap in (
            ("ffn00", a["ffn_pre_g"][0, 0]), ("mix0", a["mix_pre_g"][0]), ("ffn01", a["ffn_pre_g"][0, 1]),
            ("kv", a["kv_norm_g"]), ("ffn10", a["ffn_pre_g"][1, 0]), ("mix1", a["mix_pre_g"][1]),
            ("ffn11", a["ffn_pre_g"][1, 1]), ("mix2", a["g_mix_2"][0]), ("ffn2", a["g_ffn_2"][0]),
            ("kva", a["kv_a_norm_g"]), ("q", a["mla_q_norm_g"][0]), ("bs", a["gmlp_b_s"][0]),
        ):
            n = math.prod(ap.shape) // P
            gain_col[name] = row
            gain_rows.append((row, n, ap.rearrange("(c p) -> c p", p=P) if len(ap.shape) == 1 else ap))
            row += n
        assert row <= P

        cols = {}
        at = [0]

        def st(name, n=1):
            if name not in cols:
                cols[name] = (at[0], n)
                at[0] += n
                assert at[0] <= 400
            c, n = cols[name]
            return stat[:, c:c + n]

        FFNS = [("00", 0, 0), ("01", 0, 1), ("10", 1, 0), ("11", 1, 1)]
        roots = []

        def root(name, n, scale, eps, signals):
            st("s_" + name, n)
            st("r_" + name, n)
            roots.append((name, n, scale, eps, signals))

        pre = lambda k: root("pre_" + k, TT, 1.0 / D, RMS_EPS, TT)
        post = lambda k, half: root("post_" + k, TT, (4.0 if half else 1.0) / D, (4.0 if half else 1.0) * RMS_EPS, TT)
        pre("ffn00"); post("ffn00", True)
        pre("mix0"); root("ln", TT, 1.0, LN_EPS, 1); post("mix0", False)
        pre("ffn01"); post("ffn01", True)
        pre("kv"); root("kva", TT, 1.0 / R_KV, RMS_EPS, 1); post("ffn10", True)
        pre("mix1"); root("q", TT, 1.0 / R_Q, RMS_EPS, 1); post("mix1", False)
        pre("ffn11"); post("ffn11", True)
        pre("mix2")
        root("ret", TT * HR, 1.0, RMS_EPS, 1)
        root("foxq", TT * H, 1.0, 64 * RMS_EPS, 1)
        root("foxk", TT * H, 1.0 / 64, RMS_EPS, 1)
        pre("ffn2")

        sum_before, root_number = {}, {}
        for number, (name, _, _, _, signals) in enumerate(roots):
            sum_before[name] = sum(r[4] for r in roots[:number])
            root_number[name] = number + 1

        def sums(name, signals):
            return sem("sum_ready"), sum_before[name] + signals

        def rooted(name):
            return sem("root_ready"), root_number[name]

        raw_in = [sem(f"raw_in{i}") for i in range(SLOTS)]
        hi_done = [sem(f"hi_done{i}") for i in range(SLOTS)]
        lo_done = [sem(f"lo_done{i}") for i in range(SLOTS)]
        slot_used = [sem(f"slot_used{i}") for i in range(SLOTS)]

        W_OUT = [0, 1, 2, 3, 4, 5] + [i % SLOTS for i in range(10)]
        DKV = [0, 1, 2, 3]
        UKV = [4, 5, 0, 1]
        DQ = [0, 1, 2, 3]
        UQ = [4, 5, 0, 1, 2, 3, 4, 5]
        WO = [0, 1, 2, 3, 4, 5, 0, 1]
        RET_O = [4, 5, 0, 1]
        FOX_O = [2, 3, 4, 5]
        OUT2 = [0, 1, 2, 3, 4, 5, 0, 1]

        block = ctx.enter_context(nc.Block())

        @block.sync
        def _(sp):
            use = [0] * SLOTS

            def load(s, n, first, second):
                if not (isinstance(n, int) and n == 0):
                    sp.wait_ge(lo_done[s], n)
                for dst, src in (first, second):
                    sp.dma_start(dst, src).then_inc(raw_in[s], 16)

            def pair(s):
                return raw[:, s, :].rearrange("p (c n) -> p c n", c=2)

            def gate_up(s, n, gate, up, col):
                load(s, n, (pair(s)[:, :, 0:FT], gate[:, 2 * s:2 * s + 2, bass.ds(col, FT)]),
                     (pair(s)[:, :, FT:2 * FT], up[:, 2 * s:2 * s + 2, bass.ds(col, FT)]))

            def rows(s, n, w, c):
                wc = w[:, bass.ds(c, 1), :].rearrange("p c n -> p (c n)")
                load(s, n, (raw[:, s, 0:512], wc[:, 0:512]), (raw[:, s, 512:1024], wc[:, 512:1024]))

            def chunked(w):
                return w.rearrange("(c p) n -> p c n", p=P)

            def ffn(w_gate, w_up, w_down):
                gate, up, down = chunked(w_gate), chunked(w_up), chunked(w_down)
                base = list(use)
                for s in range(4):
                    gate_up(s, base[s], gate, up, 0)
                for f in range(2):
                    rows(4 + f, base[4 + f], down, f)
                with sp.Fori(1, NF) as j:
                    for s in range(4):
                        gate_up(s, j + base[s], gate, up, j * FT)
                    for f in range(2):
                        rows(4 + f, j + base[4 + f], down, j * 2 + f)
                for s in range(SLOTS):
                    use[s] += NF

            def tile512(s, n, w, col):
                load(s, n, (pair(s)[:, 0, :], w[:, 2 * s, bass.ds(col, BANK)]),
                     (pair(s)[:, 1, :], w[:, 2 * s + 1, bass.ds(col, BANK)]))

            def wide(w, col0, pairs):
                base = list(use)
                with sp.Fori(0, pairs) as i:
                    for par in range(2):
                        for s in range(4):
                            tile512(s, i * 2 + (base[s] + par), w, i * 1024 + (col0 + par * BANK))
                for s in range(4):
                    use[s] += 2 * pairs

            def take(s):
                use[s] += 1
                return use[s] - 1

            def all_rows(slots, w):
                for c, s in enumerate(slots):
                    rows(s, take(s), w, c)

            for r, n, ap in gain_rows:
                sp.dma_start(grow[r:r + n, :], ap).then_inc(sem("grow_in"), 16)
            sp.dma_start(ident[:], a["c_ident"]).then_inc(sem("ident_in"), 16)
            sp.dma_start(h[:], a["x"][0].rearrange("(t p) d -> p t d", p=P)).then_inc(sem("x_in"), 16)
            sp.dma_start(mask[:], a["c_mask"]).then_inc(sem("mask_in"), 16)
            sp.dma_start(freq, a["c_freq"]).then_inc(sem("pos_in"), 16)
            with nc.allow_non_contiguous_dma(reason="256 positions"):
                sp.dma_start(pos_i[:], a["positions"][0].rearrange("(t p) -> p t", p=P)).then_inc(sem("pos_in"), 16)
            sp.dma_start(cos2[:], a["c_cos"].rearrange("(t p) d -> p t d", p=P)).then_inc(sem("rope2_in"), 16)
            sp.dma_start(sin2[:], a["c_sin"].rearrange("(t p) d -> p t d", p=P)).then_inc(sem("rope2_in"), 16)
            sp.dma_start(bfor[:], a["b_forget_2"][0].partition_broadcast(P)).then_inc(sem("bfor_in"), 16)

            posts = [0]

            def load_post(g):
                k = posts[0]
                if k >= 2:
                    sp.wait_ge(sem("h_new"), k - 1)
                sp.dma_start(gpost[:, k % 2, :], g.partition_broadcast(P)).then_inc(sem(f"gpost_in{k % 2}"), 16)
                posts[0] += 1

            load_post(a["ffn_post_g"][0, 0])
            load_post(a["mix_post_g"][0])
            ffn(a["ffn_w_gate"][0, 0], a["ffn_w_up"][0, 0], a["ffn_w_down"][0, 0])
            w_in = chunked(a["gmlp_w_in"][0])
            sp.wait_ge(sem("gcol_ready"), 1)
            sp.wait_ge(sem("rope_ready"), 1)
            sp.dma_start(ws_sb, a["gmlp_w_s"][0].rearrange("g t c -> t g c")).then_inc(sem("ws_in"), 16)
            sp.dma_start(ln_g, a["gmlp_ln_g"][0].partition_broadcast(P)).then_inc(sem("ln_in"), 16)
            sp.dma_start(ln_b, a["gmlp_ln_b"][0].partition_broadcast(P)).then_inc(sem("ln_in"), 16)
            wide(w_in, HALF, 2)
            wide(w_in, 0, 2)
            all_rows(W_OUT, chunked(a["gmlp_w_out"][0]))
            load_post(a["ffn_post_g"][0, 1])
            ffn(a["ffn_w_gate"][0, 1], a["ffn_w_up"][0, 1], a["ffn_w_down"][0, 1])
            load_post(a["ffn_post_g"][1, 0])
            dkv = chunked(a["w_dkv"])
            for c, s in enumerate(DKV):
                load(s, take(s), (pair(s)[:, 0, 0:R_KV + ROPE], dkv[:, 2 * c, :]),
                     (pair(s)[:, 1, 0:R_KV + ROPE], dkv[:, 2 * c + 1, :]))
            ukv = chunked(a["w_ukv"])
            for i, s in enumerate(UKV):
                w = ukv[:, i % 2, (i // 2) * UNIT:(i // 2 + 1) * UNIT]
                load(s, take(s), (raw[:, s, 0:512], w[:, 0:512]), (raw[:, s, 512:1024], w[:, 512:1024]))
            ffn(a["ffn_w_gate"][1, 0], a["ffn_w_up"][1, 0], a["ffn_w_down"][1, 0])
            load_post(a["mix_post_g"][1])
            dq = chunked(a["mla_w_dq"][0])
            for s in DQ:
                tile512(s, take(s), dq, 0)
            uq = chunked(a["mla_w_uq"][0])
            for i, s in enumerate(UQ):
                w = uq[:, i % 4, (i // 4) * 768:(i // 4 + 1) * 768]
                load(s, take(s), (raw[:, s, 0:384], w[:, 0:384]), (raw[:, s, 384:768], w[:, 384:768]))
            all_rows(WO, chunked(a["mla_w_o"][0]))
            load_post(a["ffn_post_g"][1, 1])
            ffn(a["ffn_w_gate"][1, 1], a["ffn_w_up"][1, 1], a["ffn_w_down"][1, 1])
            w_in2 = chunked(a["w_in_2"][0])
            s = 4
            load(s, take(s), (raw[:, s, 0:32].rearrange("p (c n) -> p c n", c=4), w_in2[:, 0:4, Z_F:Z_F + 8]),
                 (raw[:, s, 32:64].rearrange("p (c n) -> p c n", c=4), w_in2[:, 4:8, Z_F:Z_F + 8]))
            wide(w_in2, 0, 3)
            wide(w_in2, Z_AR, 2)
            sp.wait_ge(sem("h_new"), 6)
            sp.dma_start(decay, a["c_decay"].rearrange("p (h n) -> p h n", h=HR)).then_inc(sem("decay_in"), 16)
            sp.dma_start(gfox[:, 1, 0:512], a["g_ret_norm_2"][0].partition_broadcast(P)).then_inc(sem("gret_in"), 16)
            for qk, g in ((0, a["g_fox_q_2"]), (1, a["g_fox_k_2"])):
                for head in range(H):
                    sp.dma_start(gfox[:, 0, qk * 512 + head * 64:qk * 512 + head * 64 + 64],
                                 g[0].partition_broadcast(P)).then_inc(sem("gfox_in"), 16)
            all_rows(RET_O, chunked(a["w_ret_o_2"][0]))
            ret_done = slot_used[RET_O[-1]], use[RET_O[-1]]
            all_rows(FOX_O, chunked(a["w_fox_o_2"][0]))
            sp.wait_ge(*ret_done)
            sp.dma_start(upto, a["c_upto"]).then_inc(sem("fox_c_in"), 16)
            sp.dma_start(ones, a["c_ones"]).then_inc(sem("fox_c_in"), 16)
            sp.dma_start(sel[0:8], a["c_sel"].rearrange("k (h q) -> k h q", h=8)).then_inc(sem("fox_c_in"), 16)
            all_rows(OUT2, chunked(a["w_out_2"][0]))
            ffn(a["w_gate_2"][0], a["w_up_2"][0], a["w_down_2"][0])
            sp.wait_ge(sem("h_new"), 8)
            sp.dma_start(out[0].rearrange("(t p) d -> p t d", p=P), h[:]).then_inc(sem("out_done"), 16)
            sp.wait_ge(sem("out_done"), 16)

        @block.gpsimd
        def _(pool):
            own = [0]

            def step(ins):
                own[0] += 1
                ins.then_inc(sem("pool_own"), 1)
                pool.wait_ge(sem("pool_own"), own[0])

            step(nc.gpsimd.memset(half_neg[:], -0.5))
            for name, n, scale, eps, signals in roots:
                if name == "post_ffn00":
                    pool.wait_ge(sem("ws_in"), 16)
                    nc.gpsimd.affine_select(out=ws_sb, in_=ws_sb, compare_op=ALU.is_ge, fill=0.0, base=0,
                                            pattern=[[0, GROUPS], [-1, P]], channel_multiplier=1
                                            ).then_inc(sem("ws_masked"), 1)
                pool.wait_ge(*sums(name, signals))
                step(nc.gpsimd.tensor_scalar(st("s_" + name), st("s_" + name), scale, eps, ALU.mult, ALU.add))
                nc.gpsimd.tensor_tensor(st("r_" + name), st("s_" + name), half_neg[:, 0:n],
                                        ALU.pow).then_inc(sem("root_ready"), 1)
                if name == "ln":
                    pool.wait_ge(sem("ln_in"), 32)
                    for t in range(TT):
                        pool.wait_ge(sem("v_normed"), t + 1)
                        step(nc.gpsimd.tensor_tensor(v_sb[:, t, :], v_sb[:, t, :], ln_g, ALU.mult))
                        nc.gpsimd.tensor_tensor(v_sb[:, t, :], v_sb[:, t, :], ln_b, ALU.add
                                                ).then_inc(sem("v_ready"), 1)

        @block.scalar
        def _(act):
            use = [0] * SLOTS
            seen = {}
            own = [0]

            def count(name, by=1):
                seen[name] = seen.get(name, 0) + by
                return seen[name]

            def high(s, n, dst=None, src=None):
                act.wait_ge(raw_in[s], n * 32 + 32)
                if not (isinstance(n, int) and n == 0):
                    act.wait_ge(slot_used[s], n)
                nc.scalar.copy(whi[:, s, :] if dst is None else dst, raw[:, s, :] if src is None else src
                               ).then_inc(hi_done[s], 1)

            def take(s):
                use[s] += 1
                return use[s] - 1

            def highs(slots, width=UNIT):
                for s in slots:
                    high(s, take(s), whi[:, s, 0:width], raw[:, s, 0:width])

            def ffn():
                base, b = list(use), seen.get("hid_full", 0)

                def gated(j):
                    act.wait_ge(slot_used[3], j + base[3])
                    for t in range(TT):
                        nc.scalar.activation(hid[:, t, :], ps[:, 4 + t, 0:FT], ACT.Silu, scale=pre_root[:, t:t + 1]
                                             ).then_inc(sem("silu_done"), 1)

                def turned_hidden(j):
                    act.wait_ge(sem("hid_full"), j + (b + 1))
                    nc.scalar.copy(hthi[:].rearrange("p c n -> p (c n)"), ps[:, 6, :]).then_inc(sem("ht_high"), 1)

                pre_root = act_pre[0]
                for s in range(3):
                    high(s, base[s])
                gated(0)
                high(3, base[3])
                turned_hidden(0)
                with act.Fori(1, NF - 1) as j:
                    for s in range(3):
                        high(s, j + base[s])
                    gated(j)
                    high(3, j + base[3])
                    for s in (4, 5):
                        high(s, j + (base[s] - 1))
                    turned_hidden(j)
                gated(NF - 1)
                for s in (4, 5):
                    high(s, base[s] + NF - 2)
                turned_hidden(NF - 1)
                for s in range(4):
                    use[s] += NF - 1
                for s in (4, 5):
                    use[s] += NF - 1
                count("hid_full", NF)

            act_pre = [None]

            def latest(s):
                return slot_used[s], use[s]

            def squares_free(name):
                if sum_before[name]:
                    act.wait_ge(sem("sum_ready"), sum_before[name])

            def post_squares(name, done):
                act.wait_ge(*done)
                squares_free(name)
                k = count("post")
                for t in range(TT):
                    if t == 1:
                        act.wait_ge(sem("acc_read1"), k)
                    nc.scalar.activation(sq_out[:, t, :], ps[:, 2 * t:2 * t + 2, :].rearrange("p a b -> p (a b)"),
                                         ACT.Square, accum_out=st("s_" + name)[:, t:t + 1]
                                         ).then_inc(sem("sum_ready"), 1)

            def pre_squares(name):
                squares_free(name)
                act.wait_ge(sem("h_new"), count("h_new"))
                for t in range(TT):
                    nc.scalar.activation(sq_out[:, t, :], h[:, t, :], ACT.Square,
                                         accum_out=st("s_" + name)[:, t:t + 1]).then_inc(sem("sum_ready"), 1)

            def flip_high(chunks, at=0, gain=None):
                for r in range(chunks // 2):
                    act.wait_ge(sem("flip_full"), count("flip_full"))
                    bank = flip_bank(r)
                    for c in range(2):
                        k = 2 * r + c
                        scale = 1.0 if gain is None else gcol[:, gain_col[gain] + k:gain_col[gain] + k + 1]
                        ins = nc.scalar.activation(kthi[:, at + k, :], ps[:, bank, c * S:c * S + S], ACT.Copy, scale=scale)
                    ins.then_inc(sem("flip_high"), 1)

            flip_bank = lambda r: 4 + r % 4

            def wide(pairs, name, func, dst):
                base = list(use)
                with act.Fori(0, pairs) as i:
                    for par in range(2):
                        for s in range(3):
                            high(s, i * 2 + (base[s] + par))
                        act.wait_ge(slot_used[3], i * 2 + (base[3] + par))
                        for t in range(TT):
                            ins = nc.scalar.activation(dst(t, i * 1024 + par * BANK), ps[:, 4 + 2 * par + t, :], func,
                                                       scale=st("r_" + name)[:, t:t + 1])
                        ins.then_inc(sem("wide_read"), 1)
                        high(3, i * 2 + (base[3] + par))
                for s in range(4):
                    use[s] += 2 * pairs

            highs([0, 1, 2, 3, 4, 5])
            act.wait_ge(sem("ang_ready"), 2)
            nc.scalar.activation(rcos[:], turns, ACT.Sin)
            nc.scalar.activation(rsin[:], red, ACT.Sin).then_inc(sem("rope_ready"), 1)
            act.wait_ge(sem("x_in"), 16)
            for t in range(TT):
                nc.scalar.activation(sq_out[:, t, :], h[:, t, :], ACT.Square,
                                     accum_out=st("s_pre_ffn00")[:, t:t + 1]).then_inc(sem("sum_ready"), 1)
            flip_high(KC, gain="ffn00")

            def run_ffn(name):
                act_pre[0] = st("r_pre_" + name)
                act.wait_ge(*rooted("pre_" + name))
                ffn()

            run_ffn("ffn00")
            done = latest(5)
            highs([0, 1, 2, 3])
            post_squares("post_ffn00", done)
            for r in range(GROUPS // 4):
                act.wait_ge(sem("wst_full"), r + 1)
                nc.scalar.copy(wst[:, 4 * r:4 * r + 4, :].rearrange("p g t -> p (g t)"), ps[:, 4 + r, :]
                               ).then_inc(sem("wst_ready"), 1)
            pre_squares("pre_mix0")
            flip_high(KC, gain="mix0")
            act.wait_ge(*rooted("pre_mix0"))
            wide(2, "pre_mix0", ACT.Gelu_apprx_tanh, lambda t, c: v_sb[:, t, bass.ds(c, BANK)])
            wide(2, "pre_mix0", ACT.Gelu_apprx_tanh, lambda t, c: u_sb[:, t, bass.ds(c, BANK)])
            highs([4, 5])
            for r in range(GROUPS // 2):
                act.wait_ge(sem("flip_full"), count("flip_full"))
                nc.scalar.copy(kthi[:, 2 * r:2 * r + 2, :].rearrange("p c n -> p (c n)"), ps[:, 6 + r % 2, :]
                               ).then_inc(sem("flip_high"), 1)
                if r >= 2 and r < 7:
                    highs(W_OUT[2 * r + 2:2 * r + 4])
            done = latest(W_OUT[-1])
            highs([4, 5, 0, 1])
            post_squares("post_mix0", done)
            highs([2, 3])
            pre_squares("pre_ffn01")
            flip_high(KC, gain="ffn01")
            run_ffn("ffn01")
            done = latest(5)
            for s in DKV:
                high(s, take(s), whi[:, s, :].rearrange("p (c n) -> p c n", c=2)[:, :, 0:R_KV + ROPE],
                     raw[:, s, :].rearrange("p (c n) -> p c n", c=2)[:, :, 0:R_KV + ROPE])
            ckv_done = latest(DKV[-1])
            highs([4, 5])
            post_squares("post_ffn01", done)
            pre_squares("pre_kv")
            flip_high(KC, gain="kv")
            act.wait_ge(*rooted("pre_kv"))
            act.wait_ge(*ckv_done)
            for t in range(TT):
                nc.scalar.activation(ckv[:, t, :], ps[:, 4 + t, 0:R_KV + ROPE], ACT.Copy,
                                     scale=st("r_pre_kv")[:, t:t + 1]).then_inc(sem("ckv_ready"), 1)
            highs([0, 1])
            act.wait_ge(sem("flip_full"), count("flip_full"))
            for c in range(2):
                k = gain_col["kva"] + c
                ins = nc.scalar.activation(kthi[:, 8 + c, :], ps[:, 6, c * S:c * S + S], ACT.Copy, scale=gcol[:, k:k + 1])
            ins.then_inc(sem("flip_high"), 1)
            act.wait_ge(sem("krt_full"), 1)
            nc.scalar.copy(krt, ps[:, 7, 0:S]).then_inc(sem("krt_ready"), 1)
            for half in range(2):
                for b in range(2):
                    act.wait_ge(sem("knt_full"), 2 * half + b + 1)
                    nc.scalar.copy(knt[:, 4 * half + 2 * b:4 * half + 2 * b + 2, :].rearrange("p c n -> p (c n)"),
                                   ps[:, 4 + b, :]).then_inc(sem("knt_ready"), 1)
            highs([2, 3])
            highs([0, 1, 4, 5])
            flip_high(KC, gain="ffn10")
            act_pre[0] = st("r_pre_kv")
            ffn()
            done = latest(5)
            highs(DQ)
            dq_done = latest(DQ[-1])
            highs(UQ[0:2], 768)
            post_squares("post_ffn10", done)
            pre_squares("pre_mix1")
            flip_high(KC, gain="mix1")
            act.wait_ge(*rooted("pre_mix1"))
            act.wait_ge(*dq_done)
            for t in range(TT):
                nc.scalar.activation(qlat[:, t, :], ps[:, 4 + t, :], ACT.Copy,
                                     scale=st("r_pre_mix1")[:, t:t + 1]).then_inc(sem("qlat_ready"), 1)
            act.wait_ge(sem("qlat_ready"), TT)
            squares_free("q")
            for t in range(TT):
                ins = nc.scalar.activation(sq_out[:, t, 0:R_Q], qlat[:, t, :], ACT.Square, accum_out=st("s_q")[:, t:t + 1])
            ins.then_inc(sem("sum_ready"), 1)
            highs(UQ[2:6], 768)
            flip_high(R_Q // P, gain="q")
            for half in range(2):
                for b in range(2):
                    act.wait_ge(sem("qnt_full"), 2 * half + b + 1)
                    nc.scalar.copy(qnt[:, 4 * half + 2 * b:4 * half + 2 * b + 2, :].rearrange("p c n -> p (c n)"),
                                   ps[:, 4 + b, :]).then_inc(sem("qnt_ready"), 1)
                if half == 0:
                    highs(UQ[6:8], 768)
            for r in range(2):
                act.wait_ge(sem("qrt_full"), r + 1)
                nc.scalar.copy(qrt[:, 2 * r:2 * r + 2, :].rearrange("p c n -> p (c n)"), ps[:, r, :]
                               ).then_inc(sem("qrt_ready"), 1)
            highs(WO[0:4])

            def exponentials(kind, scale, probs, turned_probs, after=None):
                for i in range(H + 1):
                    if i < H:
                        act.wait_ge(sem(kind + "_max_ready"), i + 1)
                        for t in range(TT):
                            blk = probs[:, i % 2, 0:P] if t == 0 else probs[:, i % 2, P:3 * P]
                            ins = nc.scalar.activation(blk, blk, ACT.Exp, bias=st(f"{kind}_nmax{i}", TT)[:, t:t + 1],
                                                       scale=scale, accum_out=st(f"{kind}_sum{i % 2}", TT)[:, t:t + 1])
                        ins.then_inc(sem(kind + "_exp_done"), 1)
                    if i >= 1:
                        act.wait_ge(sem(kind + "_pt_full"), i)
                        nc.scalar.copy(turned_probs[:, (i - 1) % 2, :], ps[:, 6, 0:3 * P]
                                       ).then_inc(sem(kind + "_pt_ready"), 1)
                        if after:
                            after(i - 1)

            def output_high(i):
                if i % 2:
                    act.wait_ge(sem("flip_full"), count("flip_full"))
                    nc.scalar.copy(kthi[:, i - 1:i + 1, :].rearrange("p c n -> p (c n)"), ps[:, i // 2, :]
                                   ).then_inc(sem("flip_high"), 1)

            exponentials("mla", MLA_SCALE, p_sb, pt_sb, output_high)
            highs(WO[4:6])
            highs(WO[6:8])
            done = latest(WO[-1])
            highs([2, 3])
            post_squares("post_mix1", done)
            highs([4, 5, 0, 1])
            pre_squares("pre_ffn11")
            flip_high(KC, gain="ffn11")
            run_ffn("ffn11")
            done = latest(5)
            highs([0, 1, 2, 3])
            highs([4], 64)
            f_done = latest(4)
            post_squares("post_ffn11", done)
            pre_squares("pre_mix2")
            flip_high(KC, gain="mix2")
            act.wait_ge(*rooted("pre_mix2"))
            wide(3, "pre_mix2", ACT.Copy, lambda t, c: z[:, t, bass.ds(c, BANK)])
            act.wait_ge(*f_done)
            for t in range(TT):
                ins = nc.scalar.activation(z[:, t, Z_F:Z_F + 8], ps[:, t, 0:8], ACT.Copy,
                                           scale=st("r_pre_mix2")[:, t:t + 1])
            ins.then_inc(sem("f_ready"), 1)
            wide(2, "pre_mix2", ACT.Sigmoid, lambda t, c: z[:, t, bass.ds(c + Z_AR, BANK)])
            highs(RET_O[0:2])
            act.wait_ge(sem("wide_read"), 20)
            for t in range(TT):
                ins = nc.scalar.activation(z[:, t, Z_GT:Z_GT + 512], z[:, t, Z_GT:Z_GT + 512], ACT.Silu)
            ins.then_inc(sem("gate_ready"), 1)
            for r in range(2):
                act.wait_ge(sem("rqk_full"), r + 1)
                nc.scalar.copy(turned[:, 2 * r:2 * r + 2, :].rearrange("p c n -> p (c n)"), ps[:, 6 + r, :]
                               ).then_inc(sem("rqk_ready"), 1)
            flip_high(4)
            act.wait_ge(sem("logf_x"), 1)
            nc.scalar.activation(logf[:, 1, :], logf[:, 1, :], ACT.Exp, scale=-1.0).then_inc(sem("logf_e"), 1)
            act.wait_ge(sem("logf_e"), 1)
            nc.scalar.activation(logf[:, 1, :], logf[:, 1, :], ACT.Ln, bias=1.0).then_inc(sem("logf_l"), 1)
            for r in range(4):
                act.wait_ge(sem("fqk_full"), r + 1)
                nc.scalar.copy(turned[:, 2 * r:2 * r + 2, :].rearrange("p c n -> p (c n)"), ps[:, 4 + r, :]
                               ).then_inc(sem("fqk_ready"), 1)
            highs(FOX_O[2:4])
            highs(OUT2[0:2])
            exponentials("fox", 1.0, st_sb, pt2_sb)
            flip_high(4)
            highs(OUT2[2:6])
            flip_high(KC)
            highs(OUT2[6:8])
            highs([2, 3, 4, 5, 0, 1])
            pre_squares("pre_ffn2")
            flip_high(KC, gain="ffn2")
            run_ffn("ffn2")

        @block.vector
        def _(dve):
            use = [0] * SLOTS
            seen = {}
            own = [0]

            def count(name, by=1):
                seen[name] = seen.get(name, 0) + by
                return seen[name]

            def mark(ins):
                own[0] += 1
                ins.then_inc(sem("dve_own"), 1)

            def settle():
                dve.wait_ge(sem("dve_own"), own[0])

            def f32(x):
                return x.bitcast(F32)

            def low(s, n, part=lambda x: x):
                dve.wait_ge(hi_done[s], n + 1)
                nc.vector.tensor_tensor(part(wlo[:, s, :]), part(raw[:, s, :]), f32(part(whi[:, s, :])),
                                        ALU.subtract).then_inc(lo_done[s], 1)

            def take(s):
                use[s] += 1
                return use[s] - 1

            def lows(slots, width=UNIT):
                for s in slots:
                    low(s, take(s), lambda x: x[:, 0:width])

            def ffn(pre):
                base, b = list(use), seen.get("silu_done", 0)
                root_ = st("r_" + pre)

                def gated(j):
                    for t in range(TT):
                        dve.wait_ge(sem("silu_done"), j * 2 + (b + t + 1))
                        ins = nc.vector.scalar_tensor_tensor(out=hid[:, t, :], in0=ps[:, 4 + t, FT:2 * FT],
                                                             scalar=root_[:, t:t + 1], in1=hid[:, t, :],
                                                             op0=ALU.mult, op1=ALU.mult)
                    ins.then_inc(sem("hid_ready"), 1)

                def turned_hidden(j):
                    dve.wait_ge(sem("ht_high"), j + (b // 2 + 1))
                    nc.vector.tensor_tensor(htlo[:].rearrange("p c n -> p (c n)"), ps[:, 6, :],
                                            f32(hthi[:]).rearrange("p c n -> p (c n)"), ALU.subtract
                                            ).then_inc(sem("ht_low"), 1)

                for s in range(3):
                    low(s, base[s])
                gated(0)
                low(3, base[3])
                turned_hidden(0)
                with dve.Fori(1, NF - 1) as j:
                    for s in range(3):
                        low(s, j + base[s])
                    gated(j)
                    low(3, j + base[3])
                    for s in (4, 5):
                        low(s, j + (base[s] - 1))
                    turned_hidden(j)
                gated(NF - 1)
                for s in (4, 5):
                    low(s, base[s] + NF - 2)
                turned_hidden(NF - 1)
                for s in range(SLOTS):
                    use[s] += NF - 1
                count("silu_done", 2 * NF)

            def acc(t):
                return ps[:, 2 * t:2 * t + 2, :].rearrange("p a b -> p (a b)")

            def latest(s):
                return slot_used[s], use[s]

            def residual(name, k, done):
                dve.wait_ge(*done)
                dve.wait_ge(sem(f"gpost_in{k % 2}"), 16 * (k // 2 + 1))
                g = gpost[:, k % 2, :]
                nc.vector.tensor_tensor(fg[:, 1, :], acc(1), g, ALU.mult).then_inc(sem("acc_read1"), 1)
                dve.wait_ge(*sums(name, 1))
                mark(nc.vector.tensor_tensor(fg[:, 0, :], acc(0), g, ALU.mult))
                dve.wait_ge(*rooted(name))
                settle()
                for t in range(TT):
                    if t == 1:
                        dve.wait_ge(sem("acc_read1"), k + 1)
                    ins = nc.vector.scalar_tensor_tensor(out=h[:, t, :], in0=fg[:, t, :],
                                                         scalar=st("r_" + name)[:, t:t + 1], in1=h[:, t, :],
                                                         op0=ALU.mult, op1=ALU.add)
                ins.then_inc(sem("h_new"), 1)

            def flip_low(chunks, at=0, gain=None, bank=lambda r: 4 + r % 4):
                for r in range(chunks // 2):
                    flip_low_pair(r, at, gain, bank(r))

            def flip_low_pair(r, at, gain, bank):
                dve.wait_ge(sem("flip_high"), count("flip_high"))
                if gain is None:
                    ins = nc.vector.tensor_tensor(ktlo[:, at + 2 * r:at + 2 * r + 2, :].rearrange("p c n -> p (c n)"),
                                                  ps[:, bank, :],
                                                  f32(kthi[:, at + 2 * r:at + 2 * r + 2, :]).rearrange("p c n -> p (c n)"),
                                                  ALU.subtract)
                else:
                    for c in range(2):
                        k = 2 * r + c
                        g = gcol[:, gain_col[gain] + k:gain_col[gain] + k + 1]
                        ins = nc.vector.scalar_tensor_tensor(out=ktlo[:, at + k, :], in0=ps[:, bank, c * S:c * S + S],
                                                             scalar=g, in1=f32(kthi[:, at + k, :]),
                                                             op0=ALU.mult, op1=ALU.subtract)
                ins.then_inc(sem("kt_ready"), 1)

            def wide(pairs):
                base = list(use)
                with dve.Fori(0, pairs) as i:
                    for par in range(2):
                        for s in range(4):
                            low(s, i * 2 + (base[s] + par))
                for s in range(4):
                    use[s] += 2 * pairs

            def over_heads(x, heads):
                return x.unsqueeze(1).to_broadcast([P, heads, RH])

            def rotate(dst, x, cos, sin, heads, tmp):
                x1, x2 = x[:, :, 0:RH], x[:, :, RH:2 * RH]
                c, s = over_heads(cos, heads), over_heads(sin, heads)
                t0 = tmp[:, 0, 0:heads * RH].rearrange("p (h r) -> p h r", h=heads)
                t1 = tmp[:, 1, 0:heads * RH].rearrange("p (h r) -> p h r", h=heads)
                settle()
                mark(nc.vector.tensor_tensor(t0, x1, c, ALU.mult))
                mark(nc.vector.tensor_tensor(t1, x2, s, ALU.mult))
                settle()
                mark(nc.vector.tensor_tensor(dst[:, :, 0:RH], t0, t1, ALU.subtract))
                settle()
                mark(nc.vector.tensor_tensor(t0, x2, c, ALU.mult))
                mark(nc.vector.tensor_tensor(t1, x1, s, ALU.mult))
                settle()
                mark(nc.vector.tensor_tensor(dst[:, :, RH:2 * RH], t0, t1, ALU.add))

            nc.vector.memset(zero[:].bitcast(F32), 0.0).then_inc(sem("zero_ready"), 1)
            nc.vector.memset(hthi[:].bitcast(F32), 0.0).then_inc(sem("zero_ready"), 1)
            for pair in range(2):
                nc.vector.memset(st(f"free{pair}"), 0.0).then_inc(sem("wide_read"), 1)
            dve.wait_ge(sem("gcol_full"), 1)
            nc.vector.tensor_copy(gcol[:, 0:row], ps[:, 4, 0:row]).then_inc(sem("gcol_ready"), 1)
            dve.wait_ge(sem("pos_in"), 32)
            mark(nc.vector.tensor_copy(posf, pos_i[:]))
            settle()
            for t in range(TT):
                mark(nc.vector.tensor_scalar(ang[:, t, :], freq, posf[:, t:t + 1], None, ALU.mult))
            settle()
            for quarter, dst in ((0.25, turns), (0.0, red)):
                mark(nc.vector.tensor_scalar(whole, ang, 1.0 / (2.0 * math.pi), quarter, ALU.mult, ALU.add))
                settle()
                mark(nc.vector.tensor_scalar(whole, whole, ROUND, -ROUND, ALU.add, ALU.add))
                settle()
                src = ang
                for part in TWO_PI:
                    for t in range(TT):
                        mark(nc.vector.scalar_tensor_tensor(out=dst[:, t, :], in0=whole[:, t, :], scalar=-part,
                                                            in1=src[:, t, :], op0=ALU.mult, op1=ALU.add))
                    settle()
                    src = dst
                mark(nc.vector.tensor_scalar(dst, dst, quarter * 2.0 * math.pi, PI_DOWN, ALU.add, ALU.min))
                settle()
                nc.vector.tensor_scalar(dst, dst, -PI_DOWN, None, ALU.max).then_inc(sem("ang_ready"), 1)
            lows([0, 1, 2, 3, 4, 5])
            flip_low(KC, gain="ffn00")

            dve.wait_ge(*rooted("pre_ffn00"))
            ffn("pre_ffn00")
            done = latest(5)
            lows([0, 1, 2, 3])
            residual("post_ffn00", 0, done)
            flip_low(KC, gain="mix0")
            wide(2)
            dve.wait_ge(sem("wide_read"), 2 + 4)
            for t in range(TT):
                for c in range(HALF // BANK):
                    mark(nc.vector.bn_stats(st("bn", 48)[:, (4 * t + c) * 6:(4 * t + c) * 6 + 6],
                                            v_sb[:, t, c * BANK:(c + 1) * BANK]))
            settle()
            for t in range(TT):
                mark(nc.vector.bn_aggr(st("mv", 16)[:, 2 * t:2 * t + 2], st("bn", 48)[:, 24 * t:24 * t + 24]))
            settle()
            mv = st("mv", 16).rearrange("p (k two) -> p k two", two=2)
            nc.vector.tensor_copy(st("s_ln"), mv[:, 0:TT, 1]).then_inc(sem("sum_ready"), 1)
            dve.wait_ge(*rooted("ln"))
            for t in range(TT):
                nc.vector.tensor_scalar(v_sb[:, t, :], v_sb[:, t, :], mv[:, t, 0:1], st("r_ln")[:, t:t + 1],
                                        ALU.subtract, ALU.mult).then_inc(sem("v_normed"), 1)
            wide(2)
            lows([4, 5])

            def mix(r):
                dve.wait_ge(sem("spatial_full"), r + 1)
                for g in (2 * r, 2 * r + 1):
                    k = gain_col["bs"] + g
                    ug = u_sb[:, :, g * GD:(g + 1) * GD]
                    ins = nc.vector.scalar_tensor_tensor(
                        out=ug, in0=ps[:, 4 + r % 2, (g % 2) * S:(g % 2) * S + S].rearrange("p (n d) -> p n d", n=TT),
                        scalar=gcol[:, k:k + 1], in1=ug, op0=ALU.add, op1=ALU.mult)
                ins.then_inc(sem("mixed"), 1)

            dve.wait_ge(sem("wide_read"), 2 + 8)
            mix(0)
            for r in range(GROUPS // 2):
                if r + 1 < GROUPS // 2:
                    mix(r + 1)
                flip_low_pair(r, 0, None, 6 + r % 2)
                if r >= 2 and r < 7:
                    lows(W_OUT[2 * r + 2:2 * r + 4])
            done = latest(W_OUT[-1])
            lows([4, 5, 0, 1])
            residual("post_mix0", 1, done)
            lows([2, 3])
            flip_low(KC, gain="ffn01")
            dve.wait_ge(*rooted("pre_ffn01"))
            ffn("pre_ffn01")
            done = latest(5)
            for s in DKV:
                low(s, take(s), lambda x: x.rearrange("p (c n) -> p c n", c=2)[:, :, 0:R_KV + ROPE])
            lows([4, 5])
            residual("post_ffn01", 2, done)
            flip_low(KC, gain="kv")
            dve.wait_ge(sem("ckv_ready"), TT)
            for t in range(TT):
                ins = nc.vector.tensor_tensor_reduce(out=fg[:, t, 0:R_KV], in0=ckv[:, t, 0:R_KV], in1=ckv[:, t, 0:R_KV],
                                                     scale=1.0, scalar=0.0, op0=ALU.mult, op1=ALU.add,
                                                     accum_out=st("s_kva")[:, t:t + 1])
            ins.then_inc(sem("sum_ready"), 1)
            dve.wait_ge(sem("rope_ready"), 1)
            for t in range(TT):
                rotate(krope2[:, t, 0:1, :], ckv[:, t:t + 1, R_KV:R_KV + ROPE], rcos[:, t, :], rsin[:, t, :], 1, rope_t)
            settle()
            nc.vector.tensor_copy(krope2[:, :, 1, :], krope2[:, :, 0, :]).then_inc(sem("krope_ready"), 1)
            dve.wait_ge(*rooted("kva"))
            for t in range(TT):
                ins = nc.vector.tensor_scalar(ckv[:, t, 0:R_KV], ckv[:, t, 0:R_KV], st("r_kva")[:, t:t + 1], None, ALU.mult)
            ins.then_inc(sem("ckv_normed"), 1)
            v_done = [latest(UKV[1])]
            lows([0, 1])
            v_done.append(latest(UKV[3]))
            flip_low_pair(0, 8, "kva", 6)
            for half in range(2):
                dve.wait_ge(*v_done[half])
                nc.vector.tensor_copy(v_mla[:, :, half * 512:(half + 1) * 512], ps[:, 6:8, :]).then_inc(sem("v_read"), 1)
            lows([2, 3])
            lows([0, 1, 4, 5])
            flip_low(KC, gain="ffn10")
            ffn("pre_kv")
            done = latest(5)
            lows(DQ)
            lows(UQ[0:2], 768)
            residual("post_ffn10", 3, done)
            flip_low(KC, gain="mix1")
            dve.wait_ge(*rooted("q"))
            for t in range(TT):
                ins = nc.vector.tensor_scalar(qlat[:, t, :], qlat[:, t, :], st("r_q")[:, t:t + 1], None, ALU.mult)
            ins.then_inc(sem("q_normed"), 1)
            lows(UQ[2:6], 768)
            flip_low(R_Q // P, gain="q")
            qr_done = latest(UQ[3])
            for half in range(2):
                dve.wait_ge(*qr_done)
                for t in range(TT):
                    rotate(qrope[:, t, 4 * half:4 * half + 4, :],
                           ps[:, 6 + half, t * 256:t * 256 + 256].rearrange("p (h r) -> p h r", h=4),
                           rcos[:, t, :], rsin[:, t, :], 4, rope_t)
                settle()
                nc.vector.memset(st(f"rotated{half}"), 0.0).then_inc(sem("qrope_ready"), 1)
                if half == 0:
                    lows(UQ[6:8], 768)
                    qr_done = latest(UQ[7])
            lows(WO[0:4])

            def softmax(kind, scale, probs, add_mask, after=None):
                def masked(i):
                    dve.wait_ge(sem(kind + "_scores_full"), i + 1)
                    if i >= 2:
                        dve.wait_ge(sem(kind + "_pt_full"), i - 1)
                    add_mask(i, probs[:, i % 2, :]).then_inc(sem(kind + "_masked"), 1)
                    dve.wait_ge(sem(kind + "_masked"), i + 1)
                    mx = st(f"{kind}_mx{i % 2}", TT)
                    mark(nc.vector.tensor_reduce(mx[:, 0:1], probs[:, i % 2, 0:P], AX_X, ALU.max))
                    mark(nc.vector.tensor_reduce(mx[:, 1:2], probs[:, i % 2, P:3 * P], AX_X, ALU.max))
                    settle()
                    nc.vector.tensor_scalar(st(f"{kind}_nmax{i}", TT), mx, -scale, None, ALU.mult
                                            ).then_inc(sem(kind + "_max_ready"), 1)

                def normed(i):
                    dve.wait_ge(sem(kind + "_exp_done"), i + 1)
                    rcp = st(f"{kind}_rcp{i % 2}", TT)
                    mark(nc.vector.reciprocal(rcp, st(f"{kind}_sum{i % 2}", TT)))
                    settle()
                    nc.vector.tensor_scalar(probs[:, i % 2, 0:P], probs[:, i % 2, 0:P], rcp[:, 0:1], None, ALU.mult)
                    nc.vector.tensor_scalar(probs[:, i % 2, P:3 * P], probs[:, i % 2, P:3 * P], rcp[:, 1:2], None,
                                            ALU.mult).then_inc(sem(kind + "_p_ready"), 1)

                masked(0)
                for i in range(H):
                    if i + 1 < H:
                        masked(i + 1)
                    normed(i)
                    if after and i >= 1:
                        after(i - 1)
                if after:
                    after(H - 1)

            def output_low(i):
                if i % 2:
                    flip_low_pair(i // 2, 0, None, i // 2)

            dve.wait_ge(sem("mask_in"), 16)
            softmax("mla", MLA_SCALE, p_sb,
                    lambda i, dst: nc.vector.tensor_tensor(dst, ps[:, 4 + i % 2, 0:3 * P], mask[:], ALU.add), output_low)
            lows(WO[4:6])
            lows(WO[6:8])
            done = latest(WO[-1])
            lows([2, 3])
            residual("post_mix1", 4, done)
            lows([4, 5, 0, 1])
            flip_low(KC, gain="ffn11")
            dve.wait_ge(*rooted("pre_ffn11"))
            ffn("pre_ffn11")
            done = latest(5)
            lows([0, 1, 2, 3])
            lows([4], 64)
            residual("post_ffn11", 5, done)
            flip_low(KC, gain="mix2")
            wide(3)
            wide(2)
            yr_done = latest(RET_O[3])
            lows(RET_O[0:2])
            dve.wait_ge(sem("wide_read"), 20)
            dve.wait_ge(sem("rope2_in"), 32)
            tmp = st_sb
            for t in range(TT):
                rotate(ro_t[:, t, :].rearrange("p (h r) -> p h r", h=8), z[:, t, 0:512].rearrange("p (h r) -> p h r", h=8),
                       cos2[:, t, :], sin2[:, t, :], 8, tmp)
            settle()
            nc.vector.memset(st("rotated2"), 0.0).then_inc(sem("r_rotated"), 1)
            dve.wait_ge(sem("decay_in"), 16)
            for i in range(HR):
                dve.wait_ge(sem("rst_full"), i + 1)
                if i >= 2:
                    dve.wait_ge(sem("rpv_done"), i - 1)
                nc.vector.tensor_tensor(st_sb[:, i % 2, :], ps[:, 4 + i % 2, 0:3 * P], decay[:, i, :], ALU.mult
                                        ).then_inc(sem("rst_ready"), 1)
            dve.wait_ge(sem("rpv_done"), HR)
            for k in range(TT * HR):
                t, i = divmod(k, HR)
                mark(nc.vector.bn_stats(st("bn", 48)[:, 6 * k:6 * k + 6], ps[:, t, i * P:(i + 1) * P]))
            settle()
            for k in range(TT * HR):
                mark(nc.vector.bn_aggr(st("mv", 16)[:, 2 * k:2 * k + 2], st("bn", 48)[:, 6 * k:6 * k + 6]))
            settle()
            nc.vector.tensor_copy(st("s_ret"), mv[:, :, 1]).then_inc(sem("sum_ready"), 1)
            dve.wait_ge(*rooted("ret"))
            for k in range(TT * HR):
                t, i = divmod(k, HR)
                mark(nc.vector.tensor_scalar(ro_t[:, t, i * P:(i + 1) * P], ps[:, t, i * P:(i + 1) * P], mv[:, k, 0:1],
                                             st("r_ret")[:, k:k + 1], ALU.subtract, ALU.mult))
            settle()
            dve.wait_ge(sem("gret_in"), 16)
            for t in range(TT):
                mark(nc.vector.tensor_tensor(ro_t[:, t, :], ro_t[:, t, :], gpost[:, 1, 0:512], ALU.mult))
            settle()
            dve.wait_ge(sem("gate_ready"), 1)
            nc.vector.tensor_tensor(ro_t, ro_t, z[:, :, Z_GT:Z_GT + 512], ALU.mult).then_inc(sem("ro_ready"), 1)
            flip_low(4)
            dve.wait_ge(sem("f_ready"), 1)
            dve.wait_ge(sem("bfor_in"), 16)
            for t in range(TT):
                mark(nc.vector.tensor_tensor(logf[:, 0, 8 * t:8 * t + 8], z[:, t, Z_F:Z_F + 8], bfor[:], ALU.add))
            settle()
            nc.vector.scalar_tensor_tensor(out=logf[:, 1, :], in0=logf[:, 0, :], scalar=-1.0, in1=logf[:, 0, :],
                                           op0=ALU.mult, op1=ALU.max).then_inc(sem("logf_x"), 1)
            mark(nc.vector.tensor_scalar(logf[:, 2, :], logf[:, 0, :], 0.0, None, ALU.min))
            settle()
            squares = turned.rearrange("p a b -> p (a b)").rearrange("p (t n) -> p t n", t=TT)
            mark(nc.vector.tensor_tensor(squares, z[:, :, Z_QF:Z_QF + 1024], z[:, :, Z_QF:Z_QF + 1024], ALU.mult))
            settle()
            for qk, name in enumerate(("foxq", "foxk")):
                nc.vector.tensor_reduce(st("s_" + name).rearrange("p (t h) -> p t h", t=TT),
                                        squares[:, :, qk * 512:qk * 512 + 512].rearrange("p t (h r) -> p t h r", h=H),
                                        AX_X, ALU.add).then_inc(sem("sum_ready"), 1)
            dve.wait_ge(sem("logf_l"), 1)
            nc.vector.tensor_tensor(logf[:, 0, :], logf[:, 2, :], logf[:, 1, :], ALU.subtract).then_inc(sem("logf_ready"), 1)
            dve.wait_ge(sem("gfox_in"), 16 * 2 * H)
            for qk, name in enumerate(("foxq", "foxk")):
                dve.wait_ge(*rooted(name))
                for t in range(TT):
                    zz = z[:, t, Z_QF + qk * 512:Z_QF + qk * 512 + 512]
                    zh = zz.rearrange("p (h r) -> p h r", h=H)
                    mark(nc.vector.tensor_tensor(zh, zh, st("r_" + name)[:, 8 * t:8 * t + 8].unsqueeze(2)
                                                 .to_broadcast([P, H, 64]), ALU.mult))
            settle()
            for t in range(TT):
                zz = z[:, t, Z_QF:Z_QF + 1024]
                ins = nc.vector.tensor_tensor(zz, zz, gfox[:, 0, :], ALU.mult)
            ins.then_inc(sem("fqk_normed"), 1)
            dve.wait_ge(sem("cum_full"), 1)
            nc.vector.tensor_copy(cum.rearrange("p t h -> p (t h)"), ps[:, 7, 0:16]).then_inc(sem("cum_ready"), 1)
            dve.wait_ge(sem("cumt_full"), 1)
            nc.vector.tensor_scalar(ncumt, ps[0:8, 7, 256:512], -1.0, None, ALU.mult).then_inc(sem("ncumt_ready"), 1)
            dve.wait_ge(*yr_done)
            for t in range(TT):
                ins = nc.vector.tensor_tensor(fg[:, t, :], acc(t), z[:, t, Z_AR:Z_AR + D], ALU.mult)
            ins.then_inc(sem("yr_read"), 1)
            lows(FOX_O[2:4])
            yf_done = latest(FOX_O[3])
            lows(OUT2[0:2])

            def fox_mask(i, dst):
                nc.vector.scalar_tensor_tensor(out=dst[:, 0:P], in0=ps[:, 4 + i % 2, 0:P], scalar=cum[:, 0, i:i + 1],
                                               in1=mask[:, 0:P], op0=ALU.add, op1=ALU.add)
                return nc.vector.scalar_tensor_tensor(out=dst[:, P:3 * P], in0=ps[:, 4 + i % 2, P:3 * P],
                                                      scalar=cum[:, 1, i:i + 1], in1=mask[:, P:3 * P],
                                                      op0=ALU.add, op1=ALU.add)

            dve.wait_ge(sem("cum_ready"), 1)
            softmax("fox", 1.0, st_sb, fox_mask)
            dve.wait_ge(sem("fpv_full"), 1)
            nc.vector.tensor_copy(z[:, :, Z_QF:Z_QF + 512], ps[:, 0:2, :]).then_inc(sem("fo_ready"), 1)
            flip_low(4)
            dve.wait_ge(*yf_done)
            for t in range(TT):
                zf = z[:, t, Z_AF:Z_AF + D]
                mark(nc.vector.tensor_tensor(zf, acc(t), zf, ALU.mult))
            dve.wait_ge(sem("yr_read"), 1)
            settle()
            for t in range(TT):
                ins = nc.vector.tensor_tensor(fg[:, t, :], fg[:, t, :], z[:, t, Z_AF:Z_AF + D], ALU.add)
            ins.then_inc(sem("merged"), 1)
            lows(OUT2[2:6])
            flip_low(KC)
            lows(OUT2[6:8])
            done = latest(OUT2[7])

            def plain_residual(done):
                dve.wait_ge(*done)
                for t in range(TT):
                    ins = nc.vector.tensor_tensor(h[:, t, :], acc(t), h[:, t, :], ALU.add)
                ins.then_inc(sem("h_new"), 1)

            lows([2, 3, 4, 5, 0, 1])
            plain_residual(done)
            flip_low(KC, gain="ffn2")
            dve.wait_ge(*rooted("pre_ffn2"))
            ffn("pre_ffn2")
            plain_residual(latest(5))

        @block.tensor
        def _(pe):
            use = [0] * SLOTS
            seen = {}

            def count(name, by=1):
                seen[name] = seen.get(name, 0) + by
                return seen[name]

            def product(dst, lhs, rhs, first, last):
                nc.tensor.matmul(dst, lhs[0], rhs[0], start=first, stop=False)
                nc.tensor.matmul(dst, lhs[0], rhs[1], start=False, stop=False)
                return nc.tensor.matmul(dst, lhs[1], rhs[0], start=False, stop=last)

            def kt(c, t=None):
                cut = slice(0, S) if t is None else slice(t * P, t * P + P)
                return kthi[:, c, cut], ktlo[:, c, cut]

            def ht(c, t):
                return hthi[:, c, t * P:t * P + P], htlo[:, c, t * P:t * P + P]

            def slot(s, cut):
                return cut(whi[:, s, :]), cut(wlo[:, s, :])

            def made(s, n):
                pe.wait_ge(lo_done[s], n + 1)

            def take(s):
                use[s] += 1
                return use[s] - 1

            def flips(chunks, src, bank=lambda r: 4 + r % 4, start=None, signal="flip_full"):
                base = seen.get("kt_ready", 0)
                for r in range(chunks // 2):
                    if start:
                        start(r)
                    if r >= 4:
                        pe.wait_ge(sem("kt_ready"), base + r - 3)
                    for c in range(2):
                        for t in range(TT):
                            ins = nc.tensor.transpose(ps[:, bank(r), c * S + t * P:c * S + t * P + P], src(2 * r + c, t), ident[:])
                    ins.then_inc(sem(signal), 1)
                if signal == "flip_full":
                    count("kt_ready", chunks // 2)
                return base

            def of_h(c, t):
                return h[:, t, c * P:(c + 1) * P]

            def tile_product(n_of, kt_base, width=BANK, bank=4):
                for s in range(4):
                    made(s, n_of(s))
                    if kt_base is not None:
                        pe.wait_ge(sem("kt_ready"), kt_base + max(s + 1, 2))
                    for c in range(2):
                        k = 2 * s + c
                        for t in range(TT):
                            rhs = slot(s, lambda x: x[:, c * BANK:c * BANK + width])
                            ins = product(ps[:, bank + t, 0:width], kt(k, t), rhs, k == 0, k == KC - 1)
                    ins.then_inc(slot_used[s], 1)

            def sum_rows(slots, chunks, wait):
                for c, s in enumerate(slots):
                    n = take(s)
                    made(s, n)
                    wait(c)
                    for t in range(TT):
                        for half in range(2):
                            rhs = slot(s, lambda x: x[:, half * BANK:(half + 1) * BANK])
                            ins = product(ps[:, 2 * t + half, :], kt(c, t), rhs, c == 0, c == chunks - 1)
                    ins.then_inc(slot_used[s], 1)

            def ffn(kt_base):
                base = list(use)
                b = seen.get("hid_ready", 0)
                for bank in range(4):
                    nc.tensor.matmul(ps[:, bank, :], zero[:], hthi[:], start=True, stop=False)

                def gate_up(j, kt_base):
                    if kt_base is None:
                        pe.wait_ge(sem("hid_ready"), j + b)
                    for s in range(4):
                        made(s, j + base[s])
                        if kt_base is not None:
                            pe.wait_ge(sem("kt_ready"), kt_base + max(s + 1, 2))
                        for c in range(2):
                            k = 2 * s + c
                            for t in range(TT):
                                rhs = slot(s, lambda x: x[:, c * BANK:(c + 1) * BANK])
                                ins = product(ps[:, 4 + t, :], kt(k, t), rhs, k == 0, k == KC - 1)
                        ins.then_inc(slot_used[s], 1)

                def turn(j):
                    pe.wait_ge(sem("hid_ready"), j + (b + 1))
                    for c in range(2):
                        for t in range(TT):
                            ins = nc.tensor.transpose(ps[:, 6, c * S + t * P:c * S + t * P + P],
                                                      hid[:, t, c * P:(c + 1) * P], ident[:])
                    ins.then_inc(sem("hid_full"), 1)

                def down(j, last):
                    pe.wait_ge(sem("ht_low"), j + (b + 1))
                    for f in range(2):
                        s = 4 + f
                        made(s, j + base[s])
                        for t in range(TT):
                            for half in range(2):
                                rhs = slot(s, lambda x: x[:, half * BANK:(half + 1) * BANK])
                                ins = product(ps[:, 2 * t + half, :], ht(f, t), rhs, False, last and f == 1)
                        ins.then_inc(slot_used[s], 1)

                gate_up(0, kt_base)
                turn(0)
                with pe.Fori(1, NF) as j:
                    gate_up(j, None)
                    down(j - 1, False)
                    turn(j)
                down(NF - 1, True)
                for s in range(SLOTS):
                    use[s] += NF
                count("hid_ready", NF)

            def wide(pairs, kt_base=None):
                base, b = list(use), seen.get("wide_read", 0)
                with pe.Fori(0, pairs) as i:
                    for par in range(2):
                        pe.wait_ge(sem("wide_read"), i * 2 + (b + par + 1))
                        if kt_base is not None and par == 0:
                            pe.wait_ge(sem("kt_ready"), kt_base + KC // 2)
                        tile_product(lambda s: i * 2 + (base[s] + par), None, bank=4 + 2 * par)
                for s in range(4):
                    use[s] += 2 * pairs
                count("wide_read", 2 * pairs)

            def flip_h(k):
                if k:
                    pe.wait_ge(sem("h_new"), k)
                return flips(KC, of_h)

            pe.wait_ge(sem("ident_in"), 16)
            pe.wait_ge(sem("grow_in"), 16 * len(gain_rows))
            nc.tensor.transpose(ps[:, 4, 0:row], grow[0:row, :], ident[0:row, 0:row]).then_inc(sem("gcol_full"), 1)
            pe.wait_ge(sem("x_in"), 16)
            pe.wait_ge(sem("gcol_ready"), 1)
            pe.wait_ge(sem("zero_ready"), 2)
            k = flip_h(0)
            pe.wait_ge(sem("kt_ready"), 1)
            ffn(k)
            pe.wait_ge(sem("ws_masked"), 1)
            for r in range(GROUPS // 4):
                for g in range(4):
                    ins = nc.tensor.transpose(ps[:, 4 + r, g * P:(g + 1) * P], ws_sb[:, 4 * r + g, :], ident[:])
                ins.then_inc(sem("wst_full"), 1)
            pe.wait_ge(sem("wst_ready"), 4)
            k = flip_h(1)
            wide(2, k)
            wide(2)
            pe.wait_ge(sem("v_ready"), TT)
            pe.wait_ge(sem("wide_read"), 2 + 8)

            def spatial(r):
                for g in (2 * r, 2 * r + 1):
                    ins = nc.tensor.matmul(ps[:, 4 + r % 2, (g % 2) * S:(g % 2) * S + S], wst[:, g, :],
                                           v_sb[:, :, g * GD:(g + 1) * GD], start=True, stop=True)
                ins.then_inc(sem("spatial_full"), 1)

            def gmlp_out(r):
                pe.wait_ge(sem("kt_ready"), kt_base + r + 1)
                for c in (2 * r, 2 * r + 1):
                    s = W_OUT[c]
                    made(s, take(s))
                    for t in range(TT):
                        for half in range(2):
                            rhs = slot(s, lambda x: x[:, half * BANK:(half + 1) * BANK])
                            ins = product(ps[:, 2 * t + half, :], kt(c, t), rhs, c == 0, c == GROUPS - 1)
                    ins.then_inc(slot_used[s], 1)

            spatial(0)
            spatial(1)
            kt_base = seen["kt_ready"]
            for r in range(GROUPS // 2):
                pe.wait_ge(sem("mixed"), r + 1)
                if r >= 2:
                    pe.wait_ge(sem("kt_ready"), kt_base + r - 1)
                for c in range(2):
                    for t in range(TT):
                        ins = nc.tensor.transpose(ps[:, 6 + r % 2, c * S + t * P:c * S + t * P + P],
                                                  u_sb[:, t, (2 * r + c) * GD:(2 * r + c + 1) * GD], ident[:])
                ins.then_inc(sem("flip_full"), 1)
                if r + 2 < GROUPS // 2:
                    spatial(r + 2)
                if r >= 1:
                    gmlp_out(r - 1)
            gmlp_out(GROUPS // 2 - 1)
            count("kt_ready", GROUPS // 2)
            k = flip_h(2)
            ffn(k)
            k = flip_h(3)
            base = list(use)
            tile_product(lambda s: base[s], k, width=R_KV + ROPE)
            for s in range(4):
                use[s] += 1
            pe.wait_ge(sem("ckv_normed"), 1)
            for c in range(2):
                for t in range(TT):
                    ins = nc.tensor.transpose(ps[:, 6, c * S + t * P:c * S + t * P + P], ckv[:, t, c * P:(c + 1) * P], ident[:])
            ins.then_inc(sem("flip_full"), 1)
            pe.wait_ge(sem("krope_ready"), 1)
            for t in range(TT):
                ins = nc.tensor.transpose(ps[:, 7, t * P:(t + 1) * P], krope2[:, t, :, :].rearrange("p c n -> p (c n)"), ident[:])
            ins.then_inc(sem("krt_full"), 1)
            pe.wait_ge(sem("kt_ready"), count("kt_ready"))
            pe.wait_ge(sem("krt_ready"), 1)
            for half in range(2):
                units = UKV[2 * half:2 * half + 2]
                for s in units:
                    made(s, take(s))
                for b in range(2):
                    if half:
                        pe.wait_ge(sem("knt_ready"), b + 1)
                    for e in range(2):
                        at_ = (2 * b + e) * KVW
                        for c, s in enumerate(units):
                            ins = product(ps[:, 4 + b, e * S:(e + 1) * S], slot(s, lambda x: x[:, at_:at_ + P]), kt(8 + c),
                                          c == 0, c == 1)
                    ins.then_inc(sem("knt_full"), 1)
                if half:
                    pe.wait_ge(sem("v_read"), 1)
                for t in range(TT):
                    for c, s in enumerate(units):
                        ins = product(ps[:, 6 + t, :], kt(8 + c, t),
                                      slot(s, lambda x: x.rearrange("p (h n) -> p h n", h=4)[:, :, P:2 * P]), c == 0, c == 1)
                        if t == TT - 1:
                            ins.then_inc(slot_used[s], 1)
            pe.wait_ge(sem("knt_ready"), 4)
            pe.wait_ge(sem("v_read"), 2)
            k = flips(KC, of_h)
            ffn(k)
            k = flip_h(4)
            base = list(use)
            tile_product(lambda s: base[s], k)
            for s in range(4):
                use[s] += 1
            pe.wait_ge(sem("q_normed"), 1)
            flips(R_Q // P, lambda c, t: qlat[:, t, c * P:(c + 1) * P])
            pe.wait_ge(sem("kt_ready"), seen["kt_ready"])
            for half in range(2):
                units = UQ[4 * half:4 * half + 4]
                for s in units:
                    made(s, take(s))
                for b in range(2):
                    if half:
                        pe.wait_ge(sem("qnt_ready"), b + 1)
                    for e in range(2):
                        at_ = (2 * b + e) * QW
                        for c, s in enumerate(units):
                            ins = product(ps[:, 4 + b, e * S:(e + 1) * S], slot(s, lambda x: x[:, at_:at_ + P]), kt(c),
                                          c == 0, c == 3)
                    ins.then_inc(sem("qnt_full"), 1)
                for t in range(TT):
                    for c, s in enumerate(units):
                        ins = product(ps[:, 6 + half, t * 4 * ROPE:(t + 1) * 4 * ROPE], kt(c, t),
                                      slot(s, lambda x: x[:, 0:4 * QW].rearrange("p (h n) -> p h n", h=4)[:, :, P:QW]),
                                      c == 0, c == 3)
                        if t == TT - 1:
                            ins.then_inc(slot_used[s], 1)
            for half in range(2):
                pe.wait_ge(sem("qrope_ready"), half + 1)
                for c in range(2):
                    for t in range(TT):
                        at_ = 4 * half + 2 * c
                        ins = nc.tensor.transpose(ps[:, half, c * S + t * P:c * S + t * P + P],
                                                  qrope[:, t, at_:at_ + 2, :].rearrange("p h r -> p (h r)"), ident[:])
                ins.then_inc(sem("qrt_full"), 1)

            def attention(kind, scores, output, probs, turned_probs):
                def turn(i):
                    pe.wait_ge(sem(kind + "_p_ready"), i + 1)
                    if i >= 1:
                        pe.wait_ge(sem(kind + "_pt_ready"), i)
                    for b in range(3):
                        ins = nc.tensor.transpose(ps[:, 6, b * P:(b + 1) * P], probs[:, i % 2, b * P:(b + 1) * P], ident[:])
                    ins.then_inc(sem(kind + "_pt_full"), 1)

                for i in range(H + 1):
                    if i < H:
                        if i >= 2:
                            pe.wait_ge(sem(kind + "_masked"), i - 1)
                        scores(i).then_inc(sem(kind + "_scores_full"), 1)
                    if i >= 1:
                        turn(i - 1)
                        pe.wait_ge(sem(kind + "_pt_ready"), i)
                        output(i - 1, turned_probs[:, (i - 1) % 2, :])

            def mla_scores(i):
                bank, e = ps[:, 4 + i % 2, :], ROPE * (i % 2)
                for t in range(TT):
                    dst = bank[:, 0:P] if t == 0 else bank[:, P:3 * P]
                    keys, q = slice(0, (t + 1) * P), slice(t * P, (t + 1) * P)
                    nc.tensor.matmul(dst, qnt[:, i, q], knt[:, i, keys], start=True, stop=False)
                    ins = nc.tensor.matmul(dst, qrt[e:e + ROPE, i // 2, q], krt[e:e + ROPE, keys], start=False, stop=True)
                return ins

            def mla_output(i, pt):
                at_ = (i % 2) * S
                bank, v = i // 2, v_mla[:, :, i * P:(i + 1) * P]
                nc.tensor.matmul(ps[:, bank, at_:at_ + S], v[:, 0, :], pt[:, 0:S], start=True, stop=False)
                ins = nc.tensor.matmul(ps[:, bank, at_ + P:at_ + S], v[:, 1, :], pt[:, S:3 * P], start=False, stop=True)
                if i % 2:
                    ins.then_inc(sem("flip_full"), 1)

            pe.wait_ge(sem("qnt_ready"), 4)
            pe.wait_ge(sem("qrt_ready"), 2)
            attention("mla", mla_scores, mla_output, p_sb, pt_sb)
            pe.wait_ge(sem("kt_ready"), count("kt_ready", H // 2))
            sum_rows(WO, H, lambda c: None)
            k = flip_h(5)
            ffn(k)
            k = flip_h(6)
            wide(3, k)
            made(4, take(4))
            for c in range(KC):
                for t in range(TT):
                    ins = product(ps[:, t, 0:8], kt(c, t), slot(4, lambda x: x[:, 8 * c:8 * c + 8]), c == 0, c == KC - 1)
            ins.then_inc(slot_used[4], 1)
            wide(2)
            pe.wait_ge(sem("r_rotated"), 1)
            pe.wait_ge(sem("wide_read"), 20)
            for r in range(2):
                for c in range(2):
                    for t in range(TT):
                        at_ = (2 * r + c) * P
                        ins = nc.tensor.transpose(ps[:, 6 + r, c * S + t * P:c * S + t * P + P], ro_t[:, t, at_:at_ + P], ident[:])
                ins.then_inc(sem("rqk_full"), 1)
            pe.wait_ge(sem("rqk_ready"), 2)
            pe.wait_ge(sem("f_ready"), 1)
            for i in range(HR + 1):
                if i < HR:
                    e = ROPE * (i % 2)
                    q, key = turned[e:e + ROPE, i // 2, :], turned[e:e + ROPE, 2 + i // 2, :]
                    if i >= 2:
                        pe.wait_ge(sem("rst_ready"), i - 1)
                    nc.tensor.matmul(ps[:, 4 + i % 2, 0:S], key[:, 0:P], q[:, 0:S], start=True, stop=True)
                    nc.tensor.matmul(ps[:, 4 + i % 2, S:3 * P], key[:, P:S], q[:, P:S], start=True, stop=True
                                     ).then_inc(sem("rst_full"), 1)
                if i >= 1:
                    j = i - 1
                    pe.wait_ge(sem("rst_ready"), j + 1)
                    w, v = st_sb[:, j % 2, :], z[:, :, Z_VR + j * P:Z_VR + (j + 1) * P]
                    nc.tensor.matmul(ps[:, 0, j * P:(j + 1) * P], w[:, 0:P], v[:, 0, :], start=True, stop=True)
                    nc.tensor.matmul(ps[:, 1, j * P:(j + 1) * P], w[:, P:S], v[:, 0, :], start=True, stop=False)
                    nc.tensor.matmul(ps[:, 1, j * P:(j + 1) * P], w[:, S:3 * P], v[:, 1, :], start=False, stop=True
                                     ).then_inc(sem("rpv_done"), 1)
            pe.wait_ge(sem("ro_ready"), 1)
            flips(4, lambda c, t: ro_t[:, t, c * P:(c + 1) * P])
            pe.wait_ge(sem("kt_ready"), seen["kt_ready"])
            sum_rows(RET_O, 4, lambda c: None)
            pe.wait_ge(sem("logf_ready"), 1)
            pe.wait_ge(sem("fox_c_in"), 48)
            nc.tensor.matmul(ps[:, 7, 0:8], upto, logf[:, 0, 0:8], start=True, stop=True)
            nc.tensor.matmul(ps[:, 7, 8:16], upto, logf[:, 0, 8:16], start=True, stop=False)
            nc.tensor.matmul(ps[:, 7, 8:16], ones, logf[:, 0, 0:8], start=False, stop=True).then_inc(sem("cum_full"), 1)
            pe.wait_ge(sem("cum_ready"), 1)
            for t in range(TT):
                ins = nc.tensor.transpose(ps[0:8, 7, S + t * P:S + (t + 1) * P], cum[:, t, :], ident[:])
            ins.then_inc(sem("cumt_full"), 1)
            pe.wait_ge(sem("fqk_normed"), 1)
            pe.wait_ge(sem("ncumt_ready"), 1)
            flips(8, lambda c, t: z[:, t, Z_QF + c * P:Z_QF + (c + 1) * P], signal="fqk_full")
            pe.wait_ge(sem("fqk_ready"), 4)
            pe.wait_ge(sem("yr_read"), 1)

            def fox_scores(i):
                bank, e = ps[:, 4 + i % 2, :], 64 * (i % 2)
                q, key = turned[e:e + 64, i // 2, :], turned[e:e + 64, 4 + i // 2, :]
                for t in range(TT):
                    dst = bank[:, 0:P] if t == 0 else bank[:, P:3 * P]
                    keys = slice(0, (t + 1) * P)
                    nc.tensor.matmul(dst, q[:, t * P:(t + 1) * P], key[:, keys], start=True, stop=False)
                    ins = nc.tensor.matmul(dst, sel[0:8, i, :], ncumt[:, keys], start=False, stop=True)
                return ins

            def fox_output(i, pt):
                v, at_ = z[:, :, Z_VF + i * 64:Z_VF + (i + 1) * 64], slice(i * 64, (i + 1) * 64)
                nc.tensor.matmul(ps[:, 0, at_], pt[:, 0:P], v[:, 0, :], start=True, stop=True)
                nc.tensor.matmul(ps[:, 1, at_], pt[:, P:S], v[:, 0, :], start=True, stop=False)
                ins = nc.tensor.matmul(ps[:, 1, at_], pt[:, S:3 * P], v[:, 1, :], start=False, stop=True)
                if i == H - 1:
                    ins.then_inc(sem("fpv_full"), 1)

            attention("fox", fox_scores, fox_output, st_sb, pt2_sb)
            pe.wait_ge(sem("fo_ready"), 1)
            flips(4, lambda c, t: z[:, t, Z_QF + c * P:Z_QF + (c + 1) * P])
            pe.wait_ge(sem("kt_ready"), seen["kt_ready"])
            sum_rows(FOX_O, 4, lambda c: None)
            pe.wait_ge(sem("merged"), 1)
            flips(KC, lambda c, t: fg[:, t, c * P:(c + 1) * P])
            pe.wait_ge(sem("kt_ready"), seen["kt_ready"])
            sum_rows(OUT2, KC, lambda c: None)
            k = flip_h(7)
            ffn(k)


OUT_SHAPE = (1, 256, 1024)


def kernel(**inputs):
    import concourse.bacc as bacc
    from concourse.bass_utils import run_bass_kernel_spmd

    nc = bacc.Bacc("TRN2", target_bir_lowering=False, num_devices=1)
    arrays = {name: np.ascontiguousarray(x) for name, x in inputs.items()}
    rope = arrays["w_dkv"].shape[1] - arrays["kv_a_norm_g"].shape[0]
    arrays.update(shape_constants(arrays["x"].shape[1], rope, 4))
    aps, sent = {}, {}
    for name, x in arrays.items():
        sent["in_" + name] = x
        aps[name] = nc.dram_tensor("in_" + name, x.shape, mybir.dt.from_np(x.dtype), kind="ExternalInput").ap()
    out = nc.dram_tensor("out", OUT_SHAPE, F32, kind="ExternalOutput").ap()
    build(nc, aps, out)
    return run_bass_kernel_spmd(nc, [sent], core_ids=[0]).results[0]["out"]
```

```python
from contextlib import ExitStack
import math

import numpy as np

import concourse.bass as bass
from concourse import mybir

ALU = mybir.AluOpType
ACT = mybir.ActivationFunctionType
AX_X = mybir.AxisListType.X
F32 = mybir.dt.float32
F32R = mybir.dt.float32r
I32 = mybir.dt.int32

P = 128
BANK = 512
SLOTS = 6
UNIT = 1024
RMS_EPS = 1e-6
LN_EPS = 1e-5
ROPE_BASE = 10000.0
NEG = -1e30
TWO_PI = (6.28125, 0.0019350051879882812, 3.0199159819567926e-07)
PI_DOWN = 3.141592502593994
ROUND = 1.5 * 2.0 ** 23


def shape_constants(s, rope, heads_r):
    f = np.float32
    i = np.arange(P)
    causal = np.where(i[None, :] <= i[:, None], 0.0, NEG)
    out = {
        "c_ident": np.eye(P),
        "c_mask": np.concatenate([causal, np.zeros((P, P)), causal], 1),
        "c_upto": (i[:, None] <= i[None, :]).astype(f),
        "c_ones": np.ones((P, P)),
    }
    sel = np.zeros((8, 8, P))
    for h in range(8):
        sel[h, h] = 1.0
    out["c_sel"] = sel.reshape(8, 8 * P)
    half = rope // 2
    out["c_freq"] = np.broadcast_to(ROPE_BASE ** (-np.arange(half) / half), (P, half))
    freq = (1.0 / (ROPE_BASE ** (np.arange(half, dtype=f) / f(half))).astype(f)).astype(f)
    ang = (np.arange(s, dtype=f)[:, None] * freq[None, :]).astype(f).astype(np.float64)
    out["c_cos"], out["c_sin"] = np.cos(ang), np.sin(ang)
    log_g = np.log1p(-(2.0 ** (-5.0 - np.arange(heads_r))))
    diff = np.arange(2 * P)[None, :] - i[:, None]
    d = np.where(diff[None] >= 0, np.exp(np.maximum(diff, 0)[None] * log_g[:, None, None]), 0.0) * rope ** -0.5
    d = np.concatenate([d, d[:, :, :P]], 2)
    out["c_decay"] = np.transpose(d, (1, 0, 2)).reshape(P, heads_r * 3 * P)
    return {k: np.ascontiguousarray(v, dtype=f) for k, v in out.items()}


def build(nc, a, out):
    S, D = a["x"].shape[1:]
    TT = S // P
    KC = D // P
    F = a["ffn_w_gate"].shape[-1]
    FT = 256
    NF = F // FT
    HALF = a["gmlp_ln_g"].shape[-1]
    GROUPS = a["gmlp_w_s"].shape[1]
    GD = HALF // GROUPS
    R_KV = a["kv_a_norm_g"].shape[0]
    R_Q = a["mla_q_norm_g"].shape[1]
    ROPE = a["w_dkv"].shape[1] - R_KV
    H = 8
    NOPE = P
    QW = NOPE + ROPE
    KVW = 2 * P
    HR = 4
    ZW = a["w_in_2"].shape[-1]
    RH = ROPE // 2
    assert TT == 2 and KC == 8 and F % FT == 0 and GD == P and ROPE == 64 and a["w_ukv"].shape[1] == H * KVW
    assert a["mla_w_uq"].shape[2] == H * QW
    Z_QR, Z_KR, Z_VR, Z_GT, Z_QF, Z_KF, Z_VF, Z_F, Z_AR, Z_AF = 0, 256, 512, 1024, 1536, 2048, 2560, 3072, 3080, 4104
    assert ZW == Z_AF + D
    MLA_SCALE = float(QW) ** -0.5

    ctx = ExitStack()
    with ctx:
        def sb(name, shape, dt=F32):
            return ctx.enter_context(nc.sbuf_tensor(name, shape, dt))

        sems = {}

        def sem(name):
            if name not in sems:
                sems[name] = ctx.enter_context(nc.semaphore(name))
            return sems[name]

        raw = sb("raw", [P, SLOTS, UNIT])
        whi = sb("whi", [P, SLOTS, UNIT], F32R)
        wlo = sb("wlo", [P, SLOTS, UNIT], F32R)
        kthi = sb("kthi", [P, 16, S], F32R)
        ktlo = sb("ktlo", [P, 16, S], F32R)
        hthi = sb("hthi", [P, 2, S], F32R)
        htlo = sb("htlo", [P, 2, S], F32R)
        zero = sb("zero", [P, P], F32R)
        h = sb("h", [P, TT, D])
        fg = sb("fg", [P, TT, D])
        gpost = sb("gpost", [P, 2, D])
        hid = sb("hid", [P, TT, FT])
        ident = sb("ident", [P, P])
        mask = sb("mask", [P, 3 * P])
        gcol = sb("gcol", [P, P])
        half_neg = sb("half_neg", [P, 40])
        stat = sb("stat", [P, 400])
        rcos = sb("rcos", [P, TT, RH])
        rsin = sb("rsin", [P, TT, RH])
        arena = sb("arena", [P, 16384])
        sq_out = sb("sq_out", [P, TT, D], mybir.dt.bfloat16)
        ps = ctx.enter_context(nc.psum_tensor("ps", [P, 8, BANK], F32))

        def view(at, *dims):
            n = math.prod(dims)
            v = arena[:, at:at + n]
            names = "abcd"[:len(dims)]
            if len(dims) == 1:
                return v
            return v.rearrange(f"p ({' '.join(names)}) -> p {' '.join(names)}", **dict(zip(names[1:], dims[1:])))

        vu = view(0, TT, 2 * HALF)
        v_sb, u_sb = vu[:, :, 0:HALF], vu[:, :, HALF:2 * HALF]
        ws_sb, wst = view(8192, GROUPS, P), view(10240, GROUPS, P)
        ln_g, ln_b = view(12288, HALF), view(14336, HALF)
        grow, grow_late = view(0, P), view(640, P)
        freq = view(256, RH)
        posf = view(320, TT)
        ang, turns, red, whole = view(384, TT, RH), view(448, TT, RH), view(512, TT, RH), view(576, TT, RH)
        pos_i = sb("pos_i", [P, TT], I32)
        ckv = view(0, TT, R_KV + ROPE)
        krope2 = view(640, TT, 2, ROPE)
        krt = view(896, S)
        knt = view(1152, H, S)
        v_mla = view(3200, TT, H * P)
        qlat = view(5248, TT, R_Q)
        qnt = view(6272, H, S)
        qrope = view(8320, TT, H, ROPE)
        qrt = view(9344, H // 2, S)
        rope_t = view(10368, 2, H * RH)
        p_sb = view(10880, 2, 3 * P)
        pt_sb = view(11648, 2, 3 * P)
        z = view(0, TT, ZW)
        o = TT * ZW
        turned = view(o, 8, S)
        ro_t = view(o + 2048, 2, 512)
        st_sb = view(o + 3072, 2, 3 * P)
        pt2_sb = view(o + 3840, 2, 3 * P)
        decay = view(o + 3840, HR, 3 * P)
        assert o + 5952 <= 16384
        gfox = gpost
        upto = view(o + 2048, P)
        ones = view(o + 2048 + P, P)
        sel = view(o + 4608, 8, P)
        cos2, sin2 = sb("cos2", [P, TT, RH]), sb("sin2", [P, TT, RH])
        bfor = sb("bfor", [P, 8])
        logf, cum = view(o + 5888, 3, TT * 8), view(o + 5936, TT, 8)
        ncumt = view(o + 5632, S)[0:8]

        gain_col = {}
        gain_rows = []
        row = 0
        for names, ap in (
            (("ffn00", "ffn01", "ffn10", "ffn11"), a["ffn_pre_g"].rearrange("l f (c p) -> (l f c) p", p=P)),
            (("mix0", "mix1"), a["mix_pre_g"].rearrange("l (c p) -> (l c) p", p=P)),
            (("kv",), a["kv_norm_g"].rearrange("(c p) -> c p", p=P)),
            (("mix2",), a["g_mix_2"][0].rearrange("(c p) -> c p", p=P)),
            (("ffn2",), a["g_ffn_2"][0].rearrange("(c p) -> c p", p=P)),
            (("kva",), a["kv_a_norm_g"].rearrange("(c p) -> c p", p=P)),
            (("q",), a["mla_q_norm_g"][0].rearrange("(c p) -> c p", p=P)),
            (("bs",), a["gmlp_b_s"][0]),
        ):
            n = ap.shape[0]
            for i, name in enumerate(names):
                gain_col[name] = row + i * (n // len(names))
            gain_rows.append((row, n, ap))
            row += n
        early_rows = gain_rows[0][1]
        assert row <= P

        cols = {}
        at = [0]

        def st(name, n=1):
            if name not in cols:
                cols[name] = (at[0], n)
                at[0] += n
                assert at[0] <= 400
            c, n = cols[name]
            return stat[:, c:c + n]

        roots = []

        def root(name, scale, eps, n=1, signals=1, halves=1):
            st("s_" + name, n * halves)
            st("r_" + name, n)
            roots.append((name, n, scale, eps, signals, halves))

        def pre(k, t):
            root(f"pre_{k}{t}", 1.0 / D, RMS_EPS)

        def post(k, t, by):
            root(f"post_{k}{t}", 1.0 / D / by ** 2, RMS_EPS / by ** 2, signals=2, halves=2)

        def after_ffn(k, following):
            post(k, 0, 0.5); post(k, 1, 0.5); pre(following, 0); pre(following, 1)

        def after_rows(k, following):
            post(k, 0, 1.0); pre(following, 0); post(k, 1, 1.0); pre(following, 1)

        pre("ffn00", 0); pre("ffn00", 1)
        after_ffn("ffn00", "mix0")
        root("ln", 1.0, LN_EPS, n=TT)
        after_rows("mix0", "ffn01")
        after_ffn("ffn01", "kv")
        root("kva", 1.0 / R_KV, RMS_EPS, n=TT)
        after_ffn("ffn10", "mix1")
        root("q0", 1.0 / R_Q, RMS_EPS); root("q1", 1.0 / R_Q, RMS_EPS)
        after_rows("mix1", "ffn11")
        after_ffn("ffn11", "mix2")
        root("ret", 1.0, RMS_EPS, n=TT * HR)
        root("foxq", 1.0, 64 * RMS_EPS, n=TT * H)
        root("foxk", 1.0 / 64, RMS_EPS, n=TT * H)
        pre("ffn2", 0); pre("ffn2", 1)

        sum_before, root_number = {}, {}
        for number, (name, *_) in enumerate(roots):
            sum_before[name] = sum(r[4] for r in roots[:number])
            root_number[name] = number + 1

        def sums(name, signals):
            return sem("sum_ready"), sum_before[name] + signals

        def rooted(name):
            return sem("root_ready"), root_number[name]

        raw_in = [sem(f"raw_in{i}") for i in range(SLOTS)]
        hi_done = [sem(f"hi_done{i}") for i in range(SLOTS)]
        lo_done = [sem(f"lo_done{i}") for i in range(SLOTS)]
        slot_used = [sem(f"slot_used{i}") for i in range(SLOTS)]

        W_OUT = [0, 1, 2, 3, 4, 5] + [i % SLOTS for i in range(10)]
        DKV = [0, 1, 2, 3]
        UKV = [4, 5, 2, 3]
        DQ = [0, 1, 2, 3]
        UQ = [4, 5, 0, 1, 2, 3, 4, 5]
        WO = [0, 1, 2, 3, 4, 5, 0, 1]
        RET_O = [4, 5, 0, 1]
        FOX_O = [2, 3, 4, 5]
        OUT2 = [0, 1, 2, 3, 4, 5, 0, 1]

        block = ctx.enter_context(nc.Block())

        @block.sync
        def _(sp):
            use = [0] * SLOTS

            def take(s):
                use[s] += 1
                return use[s] - 1

            def load(s, n, first, second):
                if not (isinstance(n, int) and n == 0):
                    sp.wait_ge(lo_done[s], n)
                for dst, src in (first, second):
                    sp.dma_start(dst, src).then_inc(raw_in[s], 16)

            def pair(s):
                return raw[:, s, :].rearrange("p (c n) -> p c n", c=2)

            def gate_up(s, n, gate, up, col):
                load(s, n, (pair(s)[:, :, 0:FT], gate[:, 2 * s:2 * s + 2, bass.ds(col, FT)]),
                     (pair(s)[:, :, FT:2 * FT], up[:, 2 * s:2 * s + 2, bass.ds(col, FT)]))

            def rows(s, n, w, c):
                wc = w[:, bass.ds(c, 1), :].rearrange("p c n -> p (c n)")
                load(s, n, (raw[:, s, 0:512], wc[:, 0:512]), (raw[:, s, 512:1024], wc[:, 512:1024]))

            def chunked(w):
                return w.rearrange("(c p) n -> p c n", p=P)

            def ffn_first(w_gate, w_up):
                gate, up = chunked(w_gate), chunked(w_up)
                for s in range(4):
                    gate_up(s, take(s), gate, up, 0)

            def ffn_rest(w_gate, w_up, w_down):
                gate, up, down = chunked(w_gate), chunked(w_up), chunked(w_down)
                for f in range(2):
                    rows(4 + f, take(4 + f), down, f)
                base = [n - 1 for n in use]
                with sp.Fori(1, NF) as j:
                    for s in range(4):
                        gate_up(s, j + base[s], gate, up, j * FT)
                    for f in range(2):
                        rows(4 + f, j + base[4 + f], down, j * 2 + f)
                for s in range(SLOTS):
                    use[s] += NF - 1

            def ffn(w_gate, w_up, w_down):
                ffn_first(w_gate, w_up)
                ffn_rest(w_gate, w_up, w_down)

            def tile512(s, n, w, col):
                load(s, n, (pair(s)[:, 0, :], w[:, 2 * s, bass.ds(col, BANK)]),
                     (pair(s)[:, 1, :], w[:, 2 * s + 1, bass.ds(col, BANK)]))

            def wide(w, col0, pairs):
                base = list(use)
                with sp.Fori(0, pairs) as i:
                    for par in range(2):
                        for s in range(4):
                            tile512(s, i * 2 + (base[s] + par), w, i * 1024 + (col0 + par * BANK))
                for s in range(4):
                    use[s] += 2 * pairs

            def all_rows(slots, w):
                for c, s in enumerate(slots):
                    rows(s, take(s), w, c)

            def tokens(t):
                return a["x"][0, t * P:(t + 1) * P, :]

            sp.dma_start(ident[:], a["c_ident"]).then_inc(sem("ident_in"), 16)
            r, n, ap = gain_rows[0]
            sp.dma_start(grow[r:r + n, :], ap).then_inc(sem("early_in"), 16)
            sp.dma_start(freq, a["c_freq"]).then_inc(sem("pos_in"), 16)
            with nc.allow_non_contiguous_dma(reason="256 positions"):
                sp.dma_start(pos_i[:], a["positions"][0].rearrange("(t p) -> p t", p=P)).then_inc(sem("pos_in"), 16)
            sp.dma_start(h[:, 0, :], tokens(0)).then_inc(sem("x_in0"), 16)
            ffn_first(a["ffn_w_gate"][0, 0], a["ffn_w_up"][0, 0])
            sp.dma_start(h[:, 1, :], tokens(1)).then_inc(sem("x_in1"), 16)
            for i, (r, n, ap) in enumerate(gain_rows[1:]):
                sp.dma_start(grow_late[r - early_rows:r - early_rows + n, :], ap).then_inc(sem("late_in"), 16)
            sp.dma_start(mask[:], a["c_mask"]).then_inc(sem("mask_in"), 16)
            sp.dma_start(cos2[:], a["c_cos"].rearrange("(t p) d -> p t d", p=P)).then_inc(sem("rope2_in"), 16)
            sp.dma_start(sin2[:], a["c_sin"].rearrange("(t p) d -> p t d", p=P)).then_inc(sem("rope2_in"), 16)
            sp.dma_start(bfor[:], a["b_forget_2"][0].partition_broadcast(P)).then_inc(sem("bfor_in"), 16)

            posts = [0]

            def load_post(g):
                k = posts[0]
                if k >= 2:
                    sp.wait_ge(sem("h_new"), 4 * (k - 1))
                sp.dma_start(gpost[:, k % 2, :], g.partition_broadcast(P)).then_inc(sem(f"gpost_in{k % 2}"), 16)
                posts[0] += 1

            ffn_rest(a["ffn_w_gate"][0, 0], a["ffn_w_up"][0, 0], a["ffn_w_down"][0, 0])
            load_post(a["ffn_post_g"][0, 0])
            load_post(a["mix_post_g"][0])
            w_in = chunked(a["gmlp_w_in"][0])
            sp.wait_ge(sem("gcol_ready"), 2)
            sp.wait_ge(sem("rope_ready"), 1)
            sp.dma_start(ws_sb, a["gmlp_w_s"][0].rearrange("g t c -> t g c")).then_inc(sem("ws_in"), 16)
            sp.dma_start(ln_g, a["gmlp_ln_g"][0].partition_broadcast(P)).then_inc(sem("ln_in"), 16)
            sp.dma_start(ln_b, a["gmlp_ln_b"][0].partition_broadcast(P)).then_inc(sem("ln_in"), 16)
            wide(w_in, HALF, 2)
            wide(w_in, 0, 2)
            all_rows(W_OUT, chunked(a["gmlp_w_out"][0]))
            load_post(a["ffn_post_g"][0, 1])
            ffn(a["ffn_w_gate"][0, 1], a["ffn_w_up"][0, 1], a["ffn_w_down"][0, 1])
            load_post(a["ffn_post_g"][1, 0])
            dkv = chunked(a["w_dkv"])
            for c, s in enumerate(DKV):
                load(s, take(s), (pair(s)[:, 0, 0:R_KV + ROPE], dkv[:, 2 * c, :]),
                     (pair(s)[:, 1, 0:R_KV + ROPE], dkv[:, 2 * c + 1, :]))
            ukv = chunked(a["w_ukv"])


            def ukv_unit(i):
                s = UKV[i]
                w = ukv[:, i % 2, (i // 2) * UNIT:(i // 2 + 1) * UNIT]
                load(s, take(s), (raw[:, s, 0:512], w[:, 0:512]), (raw[:, s, 512:1024], w[:, 512:1024]))

            ukv_unit(0)
            ukv_unit(1)
            ffn_first(a["ffn_w_gate"][1, 0], a["ffn_w_up"][1, 0])
            ukv_unit(2)
            ukv_unit(3)
            ffn_rest(a["ffn_w_gate"][1, 0], a["ffn_w_up"][1, 0], a["ffn_w_down"][1, 0])
            load_post(a["mix_post_g"][1])
            dq = chunked(a["mla_w_dq"][0])
            for s in DQ:
                tile512(s, take(s), dq, 0)
            uq = chunked(a["mla_w_uq"][0])
            for i, s in enumerate(UQ):
                w = uq[:, i % 4, (i // 4) * 768:(i // 4 + 1) * 768]
                load(s, take(s), (raw[:, s, 0:384], w[:, 0:384]), (raw[:, s, 384:768], w[:, 384:768]))
            all_rows(WO, chunked(a["mla_w_o"][0]))
            load_post(a["ffn_post_g"][1, 1])
            ffn(a["ffn_w_gate"][1, 1], a["ffn_w_up"][1, 1], a["ffn_w_down"][1, 1])
            w_in2 = chunked(a["w_in_2"][0])
            s = 4
            load(s, take(s), (raw[:, s, 0:32].rearrange("p (c n) -> p c n", c=4), w_in2[:, 0:4, Z_F:Z_F + 8]),
                 (raw[:, s, 32:64].rearrange("p (c n) -> p c n", c=4), w_in2[:, 4:8, Z_F:Z_F + 8]))
            wide(w_in2, 0, 3)
            wide(w_in2, Z_AR, 2)
            sp.wait_ge(sem("h_new"), 24)
            sp.dma_start(decay, a["c_decay"].rearrange("p (h n) -> p h n", h=HR)).then_inc(sem("decay_in"), 16)
            sp.dma_start(gfox[:, 1, 0:512], a["g_ret_norm_2"][0].partition_broadcast(P)).then_inc(sem("gret_in"), 16)
            for qk, g in ((0, a["g_fox_q_2"]), (1, a["g_fox_k_2"])):
                for head in range(H):
                    sp.dma_start(gfox[:, 0, qk * 512 + head * 64:qk * 512 + head * 64 + 64],
                                 g[0].partition_broadcast(P)).then_inc(sem("gfox_in"), 16)
            all_rows(RET_O, chunked(a["w_ret_o_2"][0]))
            ret_done = slot_used[RET_O[-1]], use[RET_O[-1]]
            all_rows(FOX_O, chunked(a["w_fox_o_2"][0]))
            sp.wait_ge(*ret_done)
            sp.dma_start(upto, a["c_upto"]).then_inc(sem("fox_c_in"), 16)
            sp.dma_start(ones, a["c_ones"]).then_inc(sem("fox_c_in"), 16)
            sp.dma_start(sel[0:8], a["c_sel"].rearrange("k (h q) -> k h q", h=8)).then_inc(sem("fox_c_in"), 16)
            all_rows(OUT2, chunked(a["w_out_2"][0]))
            ffn(a["w_gate_2"][0], a["w_up_2"][0], a["w_down_2"][0])
            for t in range(TT):
                sp.wait_ge(sem("h_new"), 30 + 2 * t)
                sp.dma_start(out[0, t * P:(t + 1) * P, :], h[:, t, :]).then_inc(sem("out_done"), 16)
            sp.wait_ge(sem("out_done"), 16 * TT)

        @block.gpsimd
        def _(pool):
            own = [0]

            def step(ins):
                own[0] += 1
                ins.then_inc(sem("pool_own"), 1)
                pool.wait_ge(sem("pool_own"), own[0])

            step(nc.gpsimd.memset(half_neg[:], -0.5))
            for name, n, scale, eps, signals, halves in roots:
                if name == "post_ffn000":
                    pool.wait_ge(sem("ws_in"), 16)
                    nc.gpsimd.affine_select(out=ws_sb, in_=ws_sb, compare_op=ALU.is_ge, fill=0.0, base=0,
                                            pattern=[[0, GROUPS], [-1, P]], channel_multiplier=1
                                            ).then_inc(sem("ws_masked"), 1)
                pool.wait_ge(*sums(name, signals))
                total = st("s_" + name)[:, 0:n]
                if halves == 2:
                    step(nc.gpsimd.tensor_tensor(total, total, st("s_" + name)[:, 1:2], ALU.add))
                step(nc.gpsimd.tensor_scalar(total, total, scale, eps, ALU.mult, ALU.add))
                nc.gpsimd.tensor_tensor(st("r_" + name), total, half_neg[:, 0:n],
                                        ALU.pow).then_inc(sem("root_ready"), 1)
                if name == "ln":
                    pool.wait_ge(sem("ln_in"), 32)
                    for t in range(TT):
                        pool.wait_ge(sem("v_normed"), t + 1)
                        step(nc.gpsimd.tensor_tensor(v_sb[:, t, :], v_sb[:, t, :], ln_g, ALU.mult))
                        nc.gpsimd.tensor_tensor(v_sb[:, t, :], v_sb[:, t, :], ln_b, ALU.add
                                                ).then_inc(sem("v_ready"), 1)

        @block.scalar
        def _(act):
            use = [0] * SLOTS
            seen = {}
            own = [0]

            def count(name, by=1):
                seen[name] = seen.get(name, 0) + by
                return seen[name]

            def high(s, n, gain=None, width=None, each=None):
                act.wait_ge(raw_in[s], n * 32 + 32)
                if not (isinstance(n, int) and n == 0):
                    act.wait_ge(slot_used[s], n)
                if gain is not None:
                    for c in range(2):
                        cut, k = slice(c * BANK, c * BANK + (width or BANK)), gain_col[gain] + 2 * s + c
                        ins = nc.scalar.activation(whi[:, s, cut], raw[:, s, cut], ACT.Copy, scale=gcol[:, k:k + 1])
                elif each is not None:
                    ins = nc.scalar.activation(whi[:, s, 0:width], raw[:, s, 0:width], ACT.Copy, scale=gcol[:, each:each + 1])
                else:
                    ins = nc.scalar.copy(whi[:, s, 0:width or UNIT], raw[:, s, 0:width or UNIT])
                ins.then_inc(hi_done[s], 1)

            def take(s):
                use[s] += 1
                return use[s] - 1

            def highs(slots, gain=None, width=None):
                for s in slots:
                    high(s, take(s), gain, width)

            def following(gain=None, width=None):
                return lambda s: high(s, take(s), gain, width)

            def gated_tile(t, pre):
                nc.scalar.activation(hid[:, t, :], ps[:, 4 + t, 0:FT], ACT.Silu, scale=st(f"r_{pre}{t}")
                                     ).then_inc(sem("silu_done"), 1)

            def tile0():
                act.wait_ge(sem("tile0_done"), count("tile0_done"))

            def ffn_first(name, pre):
                more = following(name)
                act.wait_ge(*rooted(pre + "0"))
                tile0()
                gated_tile(0, pre)
                for s in range(3):
                    more(s)
                act.wait_ge(*rooted(pre + "1"))
                act.wait_ge(slot_used[3], use[3])
                gated_tile(1, pre)
                more(3)

            def ffn_rest(name, pre, then=None):
                base, b = [n - 1 for n in use], seen.get("hid_full", 0)

                def turned_hidden(j):
                    act.wait_ge(sem("hid_full"), j + (b + 1))
                    nc.scalar.copy(hthi[:].rearrange("p c n -> p (c n)"), ps[:, 6, :]).then_inc(sem("ht_high"), 1)

                def turned_tile(t):
                    act.wait_ge(sem("hid_full"), b + NF + t)
                    nc.scalar.copy(hthi[:, :, t * P:(t + 1) * P], ps[:, 6 + t, 0:2 * P].rearrange("p (c n) -> p c n", c=2)
                                   ).then_inc(sem("ht_high"), 1)

                turned_hidden(0)
                with act.Fori(1, NF - 1) as j:
                    for s in range(3):
                        high(s, j + base[s], name)
                    act.wait_ge(slot_used[3], j + base[3])
                    for t in range(TT):
                        gated_tile(t, pre)
                    high(3, j + base[3], name)
                    for s in (4, 5):
                        high(s, j + base[s])
                    turned_hidden(j)
                for s in range(SLOTS):
                    use[s] += NF - 2
                tile0()
                gated_tile(0, pre)
                highs([4])
                turned_tile(0)
                highs([5])
                last = slot_used[3], use[3]
                if then:
                    for s in range(3):
                        then(s)
                act.wait_ge(*last)
                gated_tile(1, pre)
                if then:
                    then(3)
                turned_tile(1)
                count("hid_full", NF + 1)

            def latest(s):
                return slot_used[s], use[s]

            def squares(src, name, t, part):
                if sum_before[name]:
                    act.wait_ge(sem("sum_ready"), sum_before[name])
                nc.scalar.activation(sq_out[:, t, 0:src.shape[-1]] if part is None
                                     else sq_out[:, t, part * BANK:(part + 1) * BANK], src, ACT.Square,
                                     accum_out=st("s_" + name)[:, part or 0:(part or 0) + 1]).then_inc(sem("sum_ready"), 1)

            def acc_squares(name, t, half):
                if half:
                    act.wait_ge(sem("acc_read"), count("acc_read"))
                squares(ps[:, 2 * t + half, :], f"{name}{t}", t, half)

            def h_squares(name, t):
                count("h_new", 2)
                act.wait_ge(sem("h_new"), seen["h_new"])
                squares(h[:, t, :], f"{name}{t}", t, None)

            def flip_high(t, bank, at=0):
                act.wait_ge(sem("flip_full"), count("flip_full"))
                nc.scalar.copy(kthi[:, at:at + 4, t * P:(t + 1) * P], ps[:, bank, :].rearrange("p (c n) -> p c n", c=4)
                               ).then_inc(sem("flip_high"), 1)

            def after_ffn(post, pre, done):
                tile0()
                acc_squares(post, 0, 0)
                acc_squares(post, 0, 1)
                act.wait_ge(*done)
                acc_squares(post, 1, 0)
                flip_high(0, 6)
                acc_squares(post, 1, 1)
                flip_high(0, 7, 4)
                h_squares(pre, 0)
                flip_high(1, 6)
                flip_high(1, 7, 4)
                h_squares(pre, 1)

            def after_rows(post, pre, done, then, slots0, slots1):
                if not post:
                    count("tile0_done")
                else:
                    tile0()
                    acc_squares(post, 0, 0)
                    acc_squares(post, 0, 1)
                flip_high(0, 6)
                flip_high(0, 7, 4)
                h_squares(pre, 0)
                if post:
                    act.wait_ge(*done)
                    acc_squares(post, 1, 0)
                    acc_squares(post, 1, 1)
                for s in slots0 + slots1:
                    then(s)
                flip_high(1, 6)
                flip_high(1, 7, 4)
                h_squares(pre, 1)

            def wide(pairs, gain, root, func, dst, then, opening):
                base = list(use)

                def tile(i, par, more, first=False):
                    def evacuate(t):
                        return nc.scalar.activation(dst(t, i * 1024 + par * BANK), ps[:, 4 + 2 * par + t, :], func,
                                                    scale=st(f"r_{root}{t}"))
                    if first:
                        act.wait_ge(*rooted(root + "0"))
                        tile0()
                        evacuate(0)
                    for s in range(3):
                        more(s)
                    if first:
                        act.wait_ge(*rooted(root + "1"))
                    act.wait_ge(slot_used[3], i * 2 + (base[3] + par))
                    for t in range(1 if first else 0, TT):
                        ins = evacuate(t)
                    ins.then_inc(sem("wide_read"), 1)
                    more(3)

                def more(i, par):
                    return lambda s: high(s, i * 2 + (base[s] + par), gain)

                tile(0, 0, more(0, 0), opening)
                tile(0, 1, more(0, 1))
                if pairs > 2:
                    with act.Fori(1, pairs - 1) as i:
                        for par in range(2):
                            tile(i, par, more(i, par))
                tile(pairs - 1, 0, more(pairs - 1, 0))
                for s in range(4):
                    use[s] += 2 * pairs - 1
                tile(pairs - 1, 1, then)

            act.wait_ge(sem("x_in0"), 16)
            squares(h[:, 0, :], "pre_ffn000", 0, None)
            flip_high(0, 6)
            flip_high(0, 7, 4)
            act.wait_ge(sem("gcol_ready"), 1)
            highs([0, 1, 2, 3], "ffn00")
            act.wait_ge(sem("x_in1"), 16)
            squares(h[:, 1, :], "pre_ffn001", 1, None)
            flip_high(1, 6)
            flip_high(1, 7, 4)
            ffn_first("ffn00", "pre_ffn00")
            act.wait_ge(sem("ang_ready"), 2)
            nc.scalar.activation(rcos[:], turns, ACT.Sin)
            nc.scalar.activation(rsin[:], red, ACT.Sin).then_inc(sem("rope_ready"), 1)
            highs([4, 5])
            act.wait_ge(sem("gcol_ready"), 2)
            ffn_rest("ffn00", "pre_ffn00", following("mix0"))
            after_ffn("post_ffn00", "pre_mix0", latest(5))
            wide(4, "mix0", "pre_mix0", ACT.Gelu_apprx_tanh, lambda t, c: vu[:, t, bass.ds(c, BANK)], following(), True)
            for r in range(GROUPS // 4):
                act.wait_ge(sem("wst_full"), r + 1)
                nc.scalar.copy(wst[:, 4 * r:4 * r + 4, :].rearrange("p g t -> p (g t)"), ps[:, r, :]
                               ).then_inc(sem("wst_ready"), 1)
            highs([4, 5])
            for r in range(GROUPS // 2):
                act.wait_ge(sem("flip_full"), count("flip_full"))
                nc.scalar.copy(kthi[:, 2 * r:2 * r + 2, :].rearrange("p c n -> p (c n)"), ps[:, 6 + r % 2, :]
                               ).then_inc(sem("flip_high"), 1)
                if r >= 2 and r < 7:
                    highs(W_OUT[2 * r + 2:2 * r + 4])
            done = latest(W_OUT[-1])
            highs([4, 5])
            after_rows("post_mix0", "pre_ffn01", done, following("ffn01"), [0, 1, 2], [3])
            ffn_first("ffn01", "pre_ffn01")
            ffn_rest("ffn01", "pre_ffn01", following("kv", R_KV + ROPE))
            after_ffn("post_ffn01", "pre_kv", latest(5))
            more = following("ffn10")

            def ukv_high(i):
                high(UKV[i], take(UKV[i]), width=UNIT, each=gain_col["kva"] + i % 2)

            def ckv_out(t):
                act.wait_ge(*rooted(f"pre_kv{t}"))
                nc.scalar.activation(ckv[:, t, :], ps[:, 4 + t, 0:R_KV + ROPE], ACT.Copy,
                                     scale=st(f"r_pre_kv{t}")).then_inc(sem("ckv_ready"), 1)

            ckv_done = latest(DKV[-1])
            ukv_high(0)
            ukv_high(1)
            tile0()
            ckv_out(0)
            for s in range(3):
                more(s)
            act.wait_ge(*ckv_done)
            ckv_out(1)
            more(3)
            gate_up_done = latest(3)
            act.wait_ge(sem("flip_full"), count("flip_full"))
            nc.scalar.copy(kthi[:, 8:10, :].rearrange("p c n -> p (c n)"), ps[:, 6, :]).then_inc(sem("flip_high"), 1)
            act.wait_ge(sem("krt_full"), 1)
            nc.scalar.copy(krt, ps[:, 7, 0:S]).then_inc(sem("krt_ready"), 1)
            more(0)
            more(1)
            ukv_high(2)
            act.wait_ge(*gate_up_done)
            for t in range(TT):
                gated_tile(t, "pre_kv")
            ukv_high(3)
            for half in range(2):
                for b in range(2):
                    act.wait_ge(sem("knt_full"), 2 * half + b + 1)
                    nc.scalar.copy(knt[:, 4 * half + 2 * b:4 * half + 2 * b + 2, :].rearrange("p c n -> p (c n)"),
                                   ps[:, 4 + b, :]).then_inc(sem("knt_ready"), 1)
                if half == 0:
                    highs([4, 5])
            more(2)
            more(3)
            ffn_rest("ffn10", "pre_kv", following("mix1"))
            after_ffn("post_ffn10", "pre_mix1", latest(5))

            def uq_high(i):
                high(UQ[i], take(UQ[i]), width=768, each=gain_col["q"] + i % 4)

            def q_out(t):
                act.wait_ge(*rooted(f"pre_mix1{t}"))
                nc.scalar.activation(qlat[:, t, :], ps[:, 4 + t, :], ACT.Copy,
                                     scale=st(f"r_pre_mix1{t}")).then_inc(sem("qlat_ready"), 1)
                act.wait_ge(sem("qlat_ready"), t + 1)
                squares(qlat[:, t, :], f"q{t}", t, None)

            dq_done = latest(DQ[-1])
            uq_high(0)
            uq_high(1)
            tile0()
            q_out(0)
            for i in (2, 3, 4):
                uq_high(i)
            act.wait_ge(*dq_done)
            q_out(1)
            uq_high(5)
            flip_high(0, 6)
            flip_high(1, 7)
            for half in range(2):
                for b in range(2):
                    act.wait_ge(sem("qnt_full"), 2 * half + b + 1)
                    nc.scalar.copy(qnt[:, 4 * half + 2 * b:4 * half + 2 * b + 2, :].rearrange("p c n -> p (c n)"),
                                   ps[:, 4 + b, :]).then_inc(sem("qnt_ready"), 1)
                if half == 0:
                    uq_high(6)
                    uq_high(7)
            for r in range(2):
                act.wait_ge(sem("qrt_full"), r + 1)
                nc.scalar.copy(qrt[:, 2 * r:2 * r + 2, :].rearrange("p c n -> p (c n)"), ps[:, r, :]
                               ).then_inc(sem("qrt_ready"), 1)
            highs(WO[0:4])

            def exponentials(kind, scale, probs, turned_probs, after=None):
                for i in range(H + 1):
                    if i < H:
                        act.wait_ge(sem(kind + "_max_ready"), i + 1)
                        for t in range(TT):
                            blk = probs[:, i % 2, 0:P] if t == 0 else probs[:, i % 2, P:3 * P]
                            ins = nc.scalar.activation(blk, blk, ACT.Exp, bias=st(f"{kind}_nmax{i}", TT)[:, t:t + 1],
                                                       scale=scale, accum_out=st(f"{kind}_sum{i % 2}", TT)[:, t:t + 1])
                        ins.then_inc(sem(kind + "_exp_done"), 1)
                    if i >= 1:
                        act.wait_ge(sem(kind + "_pt_full"), i)
                        nc.scalar.copy(turned_probs[:, (i - 1) % 2, :], ps[:, 6, 0:3 * P]
                                       ).then_inc(sem(kind + "_pt_ready"), 1)
                        if after:
                            after(i - 1)

            def output_high(i):
                if i % 2:
                    act.wait_ge(sem("flip_full"), count("flip_full"))
                    nc.scalar.copy(kthi[:, i - 1:i + 1, :].rearrange("p c n -> p (c n)"), ps[:, i // 2, :]
                                   ).then_inc(sem("flip_high"), 1)

            exponentials("mla", MLA_SCALE, p_sb, pt_sb, output_high)
            highs(WO[4:6])
            highs(WO[6:8])
            done = latest(WO[-1])
            highs([2, 3], "ffn11")
            after_rows("post_mix1", "pre_ffn11", done, following("ffn11"), [0], [1])
            highs([4, 5])
            ffn_first("ffn11", "pre_ffn11")
            ffn_rest("ffn11", "pre_ffn11", following("mix2"))
            after_ffn("post_ffn11", "pre_mix2", latest(5))
            act.wait_ge(sem("f_gained"), 1)
            highs([4], width=64)
            f_done = latest(4)
            wide(3, "mix2", "pre_mix2", ACT.Copy, lambda t, c: z[:, t, bass.ds(c, BANK)], following("mix2"), True)
            act.wait_ge(*f_done)
            for t in range(TT):
                ins = nc.scalar.activation(z[:, t, Z_F:Z_F + 8], ps[:, t, 0:8], ACT.Copy, scale=st(f"r_pre_mix2{t}"))
            ins.then_inc(sem("f_ready"), 1)
            wide(2, "mix2", "pre_mix2", ACT.Sigmoid, lambda t, c: z[:, t, bass.ds(c + Z_AR, BANK)], following(), False)
            highs(RET_O[0:2])
            act.wait_ge(sem("wide_read"), 20)
            for t in range(TT):
                ins = nc.scalar.activation(z[:, t, Z_GT:Z_GT + 512], z[:, t, Z_GT:Z_GT + 512], ACT.Silu)
            ins.then_inc(sem("gate_ready"), 1)
            for r in range(2):
                act.wait_ge(sem("rqk_full"), r + 1)
                nc.scalar.copy(turned[:, 2 * r:2 * r + 2, :].rearrange("p c n -> p (c n)"), ps[:, 6 + r, :]
                               ).then_inc(sem("rqk_ready"), 1)
            flip_high(0, 6)
            flip_high(1, 7)
            act.wait_ge(sem("logf_x"), 1)
            nc.scalar.activation(logf[:, 1, :], logf[:, 1, :], ACT.Exp, scale=-1.0).then_inc(sem("logf_e"), 1)
            act.wait_ge(sem("logf_e"), 1)
            nc.scalar.activation(logf[:, 1, :], logf[:, 1, :], ACT.Ln, bias=1.0).then_inc(sem("logf_l"), 1)
            for r in range(4):
                act.wait_ge(sem("fqk_full"), r + 1)
                nc.scalar.copy(turned[:, 2 * r:2 * r + 2, :].rearrange("p c n -> p (c n)"), ps[:, 4 + r, :]
                               ).then_inc(sem("fqk_ready"), 1)
            highs(FOX_O[2:4])
            highs(OUT2[0:2])
            exponentials("fox", 1.0, st_sb, pt2_sb)
            flip_high(0, 6)
            flip_high(1, 7)
            highs(OUT2[2:6])
            flip_high(0, 4)
            flip_high(0, 5, 4)
            flip_high(1, 6)
            flip_high(1, 7, 4)
            highs(OUT2[6:8])
            highs([2, 3], "ffn2")
            after_rows(None, "pre_ffn2", None, following("ffn2"), [0], [1])
            highs([4, 5])
            ffn_first("ffn2", "pre_ffn2")
            ffn_rest("ffn2", "pre_ffn2")

        @block.vector
        def _(dve):
            use = [0] * SLOTS
            seen = {}
            own = [0]

            def count(name, by=1):
                seen[name] = seen.get(name, 0) + by
                return seen[name]

            def mark(ins):
                own[0] += 1
                ins.then_inc(sem("dve_own"), 1)

            def settle():
                dve.wait_ge(sem("dve_own"), own[0])

            def f32(x):
                return x.bitcast(F32)

            def low(s, n, gain=None, width=None, each=None):
                dve.wait_ge(hi_done[s], n + 1)
                if gain is not None:
                    for c in range(2):
                        cut, k = slice(c * BANK, c * BANK + (width or BANK)), gain_col[gain] + 2 * s + c
                        ins = nc.vector.scalar_tensor_tensor(out=wlo[:, s, cut], in0=raw[:, s, cut], scalar=gcol[:, k:k + 1],
                                                             in1=f32(whi[:, s, cut]), op0=ALU.mult, op1=ALU.subtract)
                elif each is not None:
                    ins = nc.vector.scalar_tensor_tensor(out=wlo[:, s, 0:width], in0=raw[:, s, 0:width],
                                                         scalar=gcol[:, each:each + 1], in1=f32(whi[:, s, 0:width]),
                                                         op0=ALU.mult, op1=ALU.subtract)
                else:
                    w = slice(0, width or UNIT)
                    ins = nc.vector.tensor_tensor(wlo[:, s, w], raw[:, s, w], f32(whi[:, s, w]), ALU.subtract)
                ins.then_inc(lo_done[s], 1)

            def take(s):
                use[s] += 1
                return use[s] - 1

            def lows(slots, gain=None, width=None):
                for s in slots:
                    low(s, take(s), gain, width)

            def following(gain=None, width=None):
                return lambda s: low(s, take(s), gain, width)

            def gated_tile(t, pre, n):
                dve.wait_ge(sem("silu_done"), n)
                nc.vector.scalar_tensor_tensor(out=hid[:, t, :], in0=ps[:, 4 + t, FT:2 * FT], scalar=st(f"r_{pre}{t}"),
                                               in1=hid[:, t, :], op0=ALU.mult, op1=ALU.mult
                                               ).then_inc(sem("hid_ready"), 1)

            def ffn_first(name, pre):
                more = following(name)
                count("tile0_done")
                gated_tile(0, pre, count("silu_done"))
                for s in range(3):
                    more(s)
                gated_tile(1, pre, count("silu_done"))
                more(3)

            def ffn_rest(name, pre, then=None):
                base, b, b_ht = [n - 1 for n in use], seen["silu_done"] - 2, seen.get("ht_high", 0)

                def turned_hidden(j):
                    dve.wait_ge(sem("ht_high"), j + (b_ht + 1))
                    nc.vector.tensor_tensor(htlo[:].rearrange("p c n -> p (c n)"), ps[:, 6, :],
                                            f32(hthi[:]).rearrange("p c n -> p (c n)"), ALU.subtract
                                            ).then_inc(sem("ht_low"), 1)

                def turned_tile(t):
                    dve.wait_ge(sem("ht_high"), b_ht + NF + t)
                    cut = slice(t * P, (t + 1) * P)
                    nc.vector.tensor_tensor(htlo[:, :, cut], ps[:, 6 + t, 0:2 * P].rearrange("p (c n) -> p c n", c=2),
                                            f32(hthi[:, :, cut]), ALU.subtract).then_inc(sem("ht_low"), 1)

                turned_hidden(0)
                with dve.Fori(1, NF - 1) as j:
                    for s in range(3):
                        low(s, j + base[s], name)
                    for t in range(TT):
                        gated_tile(t, pre, j * 2 + (b + t + 1))
                    low(3, j + base[3], name)
                    for s in (4, 5):
                        low(s, j + base[s])
                    turned_hidden(j)
                for s in range(SLOTS):
                    use[s] += NF - 2
                count("silu_done", 2 * (NF - 2))
                count("tile0_done")
                gated_tile(0, pre, count("silu_done"))
                lows([4])
                turned_tile(0)
                lows([5])
                if then:
                    for s in range(3):
                        then(s)
                gated_tile(1, pre, count("silu_done"))
                if then:
                    then(3)
                turned_tile(1)
                count("ht_high", NF + 1)

            def acc(t):
                return ps[:, 2 * t:2 * t + 2, :].rearrange("p a b -> p (a b)")

            def latest(s):
                return slot_used[s], use[s]

            def acc_gained(k, t, half):
                if t == 0 and half == 1:
                    dve.wait_ge(sem(f"gpost_in{k % 2}"), 16 * (k // 2 + 1))
                cut = slice(half * BANK, (half + 1) * BANK)
                ins = nc.vector.tensor_tensor(fg[:, t, cut], ps[:, 2 * t + half, :], gpost[:, k % 2, cut], ALU.mult)
                if half:
                    ins.then_inc(sem("acc_read"), 1)
                else:
                    mark(ins)

            def renew(name, t):
                dve.wait_ge(*rooted(f"{name}{t}"))
                dve.wait_ge(sem("acc_read"), count("acc_read"))
                settle()
                for half in range(2):
                    cut = slice(half * BANK, (half + 1) * BANK)
                    nc.vector.scalar_tensor_tensor(out=h[:, t, cut], in0=fg[:, t, cut], scalar=st(f"r_{name}{t}"),
                                                   in1=h[:, t, cut], op0=ALU.mult, op1=ALU.add).then_inc(sem("h_new"), 1)

            def tile0():
                dve.wait_ge(sem("tile0_done"), count("tile0_done"))

            def flip_low(t, bank, at=0):
                dve.wait_ge(sem("flip_high"), count("flip_high"))
                cut = slice(t * P, (t + 1) * P)
                nc.vector.tensor_tensor(ktlo[:, at:at + 4, cut], ps[:, bank, :].rearrange("p (c n) -> p c n", c=4),
                                        f32(kthi[:, at:at + 4, cut]), ALU.subtract).then_inc(sem("kt_ready"), 1)

            def flip_low_pair(c, bank):
                dve.wait_ge(sem("flip_high"), count("flip_high"))
                nc.vector.tensor_tensor(ktlo[:, c:c + 2, :].rearrange("p c n -> p (c n)"), ps[:, bank, :],
                                        f32(kthi[:, c:c + 2, :]).rearrange("p c n -> p (c n)"), ALU.subtract
                                        ).then_inc(sem("kt_ready"), 1)

            def after_ffn(post, k, done):
                tile0()
                acc_gained(k, 0, 1)
                dve.wait_ge(*sums(post + "0", 1))
                acc_gained(k, 0, 0)
                renew(post, 0)
                dve.wait_ge(*done)
                acc_gained(k, 1, 1)
                flip_low(0, 6)
                dve.wait_ge(*sums(post + "1", 1))
                acc_gained(k, 1, 0)
                flip_low(0, 7, 4)
                renew(post, 1)
                flip_low(1, 6)
                flip_low(1, 7, 4)

            def after_rows(post, k, done, then, slots0, slots1):
                def renewed(t):
                    if post:
                        renew(post, t)
                    else:
                        for half in range(2):
                            cut = slice(half * BANK, (half + 1) * BANK)
                            nc.vector.tensor_tensor(h[:, t, cut], ps[:, 2 * t + half, :], h[:, t, cut], ALU.add
                                                    ).then_inc(sem("h_new"), 1)
                tile0()
                if post:
                    acc_gained(k, 0, 1)
                    dve.wait_ge(*sums(post + "0", 1))
                    acc_gained(k, 0, 0)
                renewed(0)
                flip_low(0, 6)
                flip_low(0, 7, 4)
                dve.wait_ge(*done)
                if post:
                    acc_gained(k, 1, 1)
                    dve.wait_ge(*sums(post + "1", 1))
                    acc_gained(k, 1, 0)
                for s in slots0:
                    then(s)
                renewed(1)
                for s in slots1:
                    then(s)
                flip_low(1, 6)
                flip_low(1, 7, 4)

            def wide(pairs, gain, then):
                base = list(use)
                with dve.Fori(0, pairs - 1) as i:
                    for par in range(2):
                        for s in range(4):
                            low(s, i * 2 + (base[s] + par), gain)
                for s in range(4):
                    use[s] += 2 * pairs - 2
                for s in range(4):
                    low(s, take(s), gain)
                for s in range(4):
                    then(s)

            def over_heads(x, heads):
                return x.unsqueeze(1).to_broadcast([P, heads, RH])

            def rotate(dst, x, cos, sin, heads, tmp):
                x1, x2 = x[:, :, 0:RH], x[:, :, RH:2 * RH]
                c, s = over_heads(cos, heads), over_heads(sin, heads)
                t0 = tmp[:, 0, 0:heads * RH].rearrange("p (h r) -> p h r", h=heads)
                t1 = tmp[:, 1, 0:heads * RH].rearrange("p (h r) -> p h r", h=heads)
                settle()
                mark(nc.vector.tensor_tensor(t0, x1, c, ALU.mult))
                mark(nc.vector.tensor_tensor(t1, x2, s, ALU.mult))
                settle()
                mark(nc.vector.tensor_tensor(dst[:, :, 0:RH], t0, t1, ALU.subtract))
                settle()
                mark(nc.vector.tensor_tensor(t0, x2, c, ALU.mult))
                mark(nc.vector.tensor_tensor(t1, x1, s, ALU.mult))
                settle()
                mark(nc.vector.tensor_tensor(dst[:, :, RH:2 * RH], t0, t1, ALU.add))

            nc.vector.memset(zero[:].bitcast(F32), 0.0).then_inc(sem("zero_ready"), 1)
            nc.vector.memset(hthi[:].bitcast(F32), 0.0).then_inc(sem("zero_ready"), 1)
            for pair in range(2):
                nc.vector.memset(st(f"free{pair}"), 0.0).then_inc(sem("wide_read"), 1)
            dve.wait_ge(sem("gcol_full"), 1)
            nc.vector.tensor_copy(gcol[:, 0:early_rows], ps[:, 5, 0:early_rows]).then_inc(sem("gcol_ready"), 1)
            dve.wait_ge(sem("pos_in"), 32)
            mark(nc.vector.tensor_copy(posf, pos_i[:]))
            settle()
            for t in range(TT):
                mark(nc.vector.tensor_scalar(ang[:, t, :], freq, posf[:, t:t + 1], None, ALU.mult))
            settle()
            for quarter, dst in ((0.25, turns), (0.0, red)):
                mark(nc.vector.tensor_scalar(whole, ang, 1.0 / (2.0 * math.pi), quarter, ALU.mult, ALU.add))
                settle()
                mark(nc.vector.tensor_scalar(whole, whole, ROUND, -ROUND, ALU.add, ALU.add))
                settle()
                src = ang
                for part in TWO_PI:
                    for t in range(TT):
                        mark(nc.vector.scalar_tensor_tensor(out=dst[:, t, :], in0=whole[:, t, :], scalar=-part,
                                                            in1=src[:, t, :], op0=ALU.mult, op1=ALU.add))
                    settle()
                    src = dst
                mark(nc.vector.tensor_scalar(dst, dst, quarter * 2.0 * math.pi, PI_DOWN, ALU.add, ALU.min))
                settle()
                nc.vector.tensor_scalar(dst, dst, -PI_DOWN, None, ALU.max).then_inc(sem("ang_ready"), 1)
            flip_low(0, 6)
            flip_low(0, 7, 4)
            lows([0, 1, 2, 3], "ffn00")
            flip_low(1, 6)
            flip_low(1, 7, 4)
            ffn_first("ffn00", "pre_ffn00")
            dve.wait_ge(sem("gcol_full"), 2)
            nc.vector.tensor_copy(gcol[:, early_rows:row], ps[:, 7, 0:row - early_rows]).then_inc(sem("gcol_ready"), 1)
            lows([4, 5])
            ffn_rest("ffn00", "pre_ffn00", following("mix0"))
            after_ffn("post_ffn00", 0, latest(5))
            count("tile0_done")
            mv = st("mv", 16).rearrange("p (k two) -> p k two", two=2)
            V_TILES = HALF // BANK
            for k in range(2 * V_TILES):
                if k + 1 < 2 * V_TILES:
                    lows([0, 1, 2, 3], "mix0")
                else:
                    lows([0, 1, 2, 3])
                if k < V_TILES:
                    dve.wait_ge(sem("wide_read"), 2 + k + 1)
                    for t in range(TT):
                        mark(nc.vector.bn_stats(st("bn", 48)[:, (4 * t + k) * 6:(4 * t + k) * 6 + 6],
                                                v_sb[:, t, k * BANK:(k + 1) * BANK]))
                if k == V_TILES - 1:
                    settle()
                    for t in range(TT):
                        mark(nc.vector.bn_aggr(st("mv", 16)[:, 2 * t:2 * t + 2], st("bn", 48)[:, 24 * t:24 * t + 24]))
                    settle()
                    nc.vector.tensor_copy(st("s_ln"), mv[:, 0:TT, 1]).then_inc(sem("sum_ready"), 1)
                    dve.wait_ge(*rooted("ln"))
                if V_TILES <= k < V_TILES + TT:
                    t = k - V_TILES
                    nc.vector.tensor_scalar(v_sb[:, t, :], v_sb[:, t, :], mv[:, t, 0:1], st("r_ln")[:, t:t + 1],
                                            ALU.subtract, ALU.mult).then_inc(sem("v_normed"), 1)
            lows([4, 5])

            def mix(r):
                dve.wait_ge(sem("spatial_full"), r + 1)
                for g in (2 * r, 2 * r + 1):
                    k = gain_col["bs"] + g
                    ug = u_sb[:, :, g * GD:(g + 1) * GD]
                    ins = nc.vector.scalar_tensor_tensor(
                        out=ug, in0=ps[:, 4 + r % 2, (g % 2) * S:(g % 2) * S + S].rearrange("p (n d) -> p n d", n=TT),
                        scalar=gcol[:, k:k + 1], in1=ug, op0=ALU.add, op1=ALU.mult)
                ins.then_inc(sem("mixed"), 1)

            dve.wait_ge(sem("wide_read"), 2 + 8)
            mix(0)
            for r in range(GROUPS // 2):
                if r + 1 < GROUPS // 2:
                    mix(r + 1)
                flip_low_pair(2 * r, 6 + r % 2)
                if r >= 2 and r < 7:
                    lows(W_OUT[2 * r + 2:2 * r + 4])
            done = latest(W_OUT[-1])
            lows([4, 5])
            after_rows("post_mix0", 1, done, following("ffn01"), [0, 1, 2], [3])
            ffn_first("ffn01", "pre_ffn01")
            ffn_rest("ffn01", "pre_ffn01", following("kv", R_KV + ROPE))
            after_ffn("post_ffn01", 2, latest(5))
            more = following("ffn10")

            def ukv_low(i):
                low(UKV[i], take(UKV[i]), width=UNIT, each=gain_col["kva"] + i % 2)

            ukv_low(0)
            ukv_low(1)
            count("tile0_done")
            for s in range(3):
                more(s)
            dve.wait_ge(sem("ckv_ready"), TT)
            for t in range(TT):
                ins = nc.vector.tensor_tensor_reduce(out=fg[:, t, 0:R_KV], in0=ckv[:, t, 0:R_KV], in1=ckv[:, t, 0:R_KV],
                                                     scale=1.0, scalar=0.0, op0=ALU.mult, op1=ALU.add,
                                                     accum_out=st("s_kva")[:, t:t + 1])
            ins.then_inc(sem("sum_ready"), 1)
            more(3)
            dve.wait_ge(sem("rope_ready"), 1)
            for t in range(TT):
                rotate(krope2[:, t, 0:1, :], ckv[:, t:t + 1, R_KV:R_KV + ROPE], rcos[:, t, :], rsin[:, t, :], 1, rope_t)
            settle()
            nc.vector.tensor_copy(krope2[:, :, 1, :], krope2[:, :, 0, :]).then_inc(sem("krope_ready"), 1)
            dve.wait_ge(*rooted("kva"))
            for t in range(TT):
                ins = nc.vector.tensor_scalar(ckv[:, t, 0:R_KV], ckv[:, t, 0:R_KV], st("r_kva")[:, t:t + 1], None, ALU.mult)
            ins.then_inc(sem("ckv_normed"), 1)
            flip_low_pair(8, 6)
            v_done = [latest(UKV[1])]
            more(0)
            more(1)
            ukv_low(2)
            for t in range(TT):
                gated_tile(t, "pre_kv", count("silu_done"))
            ukv_low(3)
            v_done.append(latest(UKV[3]))
            for half in range(2):
                dve.wait_ge(*v_done[half])
                nc.vector.tensor_copy(v_mla[:, :, half * 512:(half + 1) * 512], ps[:, 6:8, :]).then_inc(sem("v_read"), 1)
                if half == 0:
                    lows([4, 5])
            more(2)
            more(3)
            ffn_rest("ffn10", "pre_kv", following("mix1"))
            after_ffn("post_ffn10", 3, latest(5))

            def uq_low(i):
                low(UQ[i], take(UQ[i]), width=768, each=gain_col["q"] + i % 4)

            def q_scale(t):
                dve.wait_ge(*rooted(f"q{t}"))
                nc.vector.tensor_scalar(qlat[:, t, :], qlat[:, t, :], st(f"r_q{t}"), None, ALU.mult
                                        ).then_inc(sem("q_normed"), 1)

            uq_low(0)
            uq_low(1)
            count("tile0_done")
            uq_low(2)
            q_scale(0)
            uq_low(3)
            uq_low(4)
            q_scale(1)
            uq_low(5)
            flip_low(0, 6)
            flip_low(1, 7)
            qr_done = latest(UQ[3])
            for half in range(2):
                dve.wait_ge(*qr_done)
                for t in range(TT):
                    rotate(qrope[:, t, 4 * half:4 * half + 4, :],
                           ps[:, 6 + half, t * 256:t * 256 + 256].rearrange("p (h r) -> p h r", h=4),
                           rcos[:, t, :], rsin[:, t, :], 4, rope_t)
                settle()
                nc.vector.memset(st(f"rotated{half}"), 0.0).then_inc(sem("qrope_ready"), 1)
                if half == 0:
                    uq_low(6)
                    uq_low(7)
                    qr_done = latest(UQ[7])
            lows(WO[0:4])

            def softmax(kind, scale, probs, add_mask, after=None):
                def masked(i):
                    dve.wait_ge(sem(kind + "_scores_full"), i + 1)
                    if i >= 2:
                        dve.wait_ge(sem(kind + "_pt_full"), i - 1)
                    add_mask(i, probs[:, i % 2, :]).then_inc(sem(kind + "_masked"), 1)
                    dve.wait_ge(sem(kind + "_masked"), i + 1)
                    mx = st(f"{kind}_mx{i % 2}", TT)
                    mark(nc.vector.tensor_reduce(mx[:, 0:1], probs[:, i % 2, 0:P], AX_X, ALU.max))
                    mark(nc.vector.tensor_reduce(mx[:, 1:2], probs[:, i % 2, P:3 * P], AX_X, ALU.max))
                    settle()
                    nc.vector.tensor_scalar(st(f"{kind}_nmax{i}", TT), mx, -scale, None, ALU.mult
                                            ).then_inc(sem(kind + "_max_ready"), 1)

                def normed(i):
                    dve.wait_ge(sem(kind + "_exp_done"), i + 1)
                    rcp = st(f"{kind}_rcp{i % 2}", TT)
                    mark(nc.vector.reciprocal(rcp, st(f"{kind}_sum{i % 2}", TT)))
                    settle()
                    nc.vector.tensor_scalar(probs[:, i % 2, 0:P], probs[:, i % 2, 0:P], rcp[:, 0:1], None, ALU.mult)
                    nc.vector.tensor_scalar(probs[:, i % 2, P:3 * P], probs[:, i % 2, P:3 * P], rcp[:, 1:2], None,
                                            ALU.mult).then_inc(sem(kind + "_p_ready"), 1)

                masked(0)
                for i in range(H):
                    if i + 1 < H:
                        masked(i + 1)
                    normed(i)
                    if after and i >= 1:
                        after(i - 1)
                if after:
                    after(H - 1)

            def output_low(i):
                if i % 2:
                    flip_low_pair(i - 1, i // 2)

            dve.wait_ge(sem("mask_in"), 16)
            softmax("mla", MLA_SCALE, p_sb,
                    lambda i, dst: nc.vector.tensor_tensor(dst, ps[:, 4 + i % 2, 0:3 * P], mask[:], ALU.add), output_low)
            lows(WO[4:6])
            lows(WO[6:8])
            done = latest(WO[-1])
            lows([2, 3], "ffn11")
            after_rows("post_mix1", 4, done, following("ffn11"), [0], [1])
            lows([4, 5])
            ffn_first("ffn11", "pre_ffn11")
            ffn_rest("ffn11", "pre_ffn11", following("mix2"))
            after_ffn("post_ffn11", 5, latest(5))
            s = 4
            dve.wait_ge(raw_in[s], 32 * use[s] + 32)
            f_raw = raw[:, s, 0:8 * KC].rearrange("p (c n) -> p c n", c=KC)
            k = gain_col["mix2"]
            nc.vector.tensor_tensor(f_raw, f_raw, gcol[:, k:k + KC].unsqueeze(2).to_broadcast([P, KC, 8]), ALU.mult
                                    ).then_inc(sem("f_gained"), 1)
            lows([4], width=64)
            count("tile0_done")
            wide(3, "mix2", following("mix2"))
            wide(2, "mix2", following())
            yr_done = latest(RET_O[3])
            lows(RET_O[0:2])
            dve.wait_ge(sem("wide_read"), 20)
            dve.wait_ge(sem("rope2_in"), 32)
            tmp = st_sb
            for t in range(TT):
                rotate(ro_t[:, t, :].rearrange("p (h r) -> p h r", h=8), z[:, t, 0:512].rearrange("p (h r) -> p h r", h=8),
                       cos2[:, t, :], sin2[:, t, :], 8, tmp)
            settle()
            nc.vector.memset(st("rotated2"), 0.0).then_inc(sem("r_rotated"), 1)
            dve.wait_ge(sem("decay_in"), 16)
            for i in range(HR):
                dve.wait_ge(sem("rst_full"), i + 1)
                if i >= 2:
                    dve.wait_ge(sem("rpv_done"), i - 1)
                nc.vector.tensor_tensor(st_sb[:, i % 2, :], ps[:, 4 + i % 2, 0:3 * P], decay[:, i, :], ALU.mult
                                        ).then_inc(sem("rst_ready"), 1)
            dve.wait_ge(sem("rpv_done"), HR)
            for k in range(TT * HR):
                t, i = divmod(k, HR)
                mark(nc.vector.bn_stats(st("bn", 48)[:, 6 * k:6 * k + 6], ps[:, t, i * P:(i + 1) * P]))
            settle()
            for k in range(TT * HR):
                mark(nc.vector.bn_aggr(st("mv", 16)[:, 2 * k:2 * k + 2], st("bn", 48)[:, 6 * k:6 * k + 6]))
            settle()
            nc.vector.tensor_copy(st("s_ret"), mv[:, :, 1]).then_inc(sem("sum_ready"), 1)
            dve.wait_ge(*rooted("ret"))
            for k in range(TT * HR):
                t, i = divmod(k, HR)
                mark(nc.vector.tensor_scalar(ro_t[:, t, i * P:(i + 1) * P], ps[:, t, i * P:(i + 1) * P], mv[:, k, 0:1],
                                             st("r_ret")[:, k:k + 1], ALU.subtract, ALU.mult))
            settle()
            dve.wait_ge(sem("gret_in"), 16)
            for t in range(TT):
                mark(nc.vector.tensor_tensor(ro_t[:, t, :], ro_t[:, t, :], gpost[:, 1, 0:512], ALU.mult))
            settle()
            dve.wait_ge(sem("gate_ready"), 1)
            nc.vector.tensor_tensor(ro_t, ro_t, z[:, :, Z_GT:Z_GT + 512], ALU.mult).then_inc(sem("ro_ready"), 1)
            flip_low(0, 6)
            flip_low(1, 7)
            dve.wait_ge(sem("f_ready"), 1)
            dve.wait_ge(sem("bfor_in"), 16)
            for t in range(TT):
                mark(nc.vector.tensor_tensor(logf[:, 0, 8 * t:8 * t + 8], z[:, t, Z_F:Z_F + 8], bfor[:], ALU.add))
            settle()
            nc.vector.scalar_tensor_tensor(out=logf[:, 1, :], in0=logf[:, 0, :], scalar=-1.0, in1=logf[:, 0, :],
                                           op0=ALU.mult, op1=ALU.max).then_inc(sem("logf_x"), 1)
            mark(nc.vector.tensor_scalar(logf[:, 2, :], logf[:, 0, :], 0.0, None, ALU.min))
            settle()
            squares = turned.rearrange("p a b -> p (a b)").rearrange("p (t n) -> p t n", t=TT)
            mark(nc.vector.tensor_tensor(squares, z[:, :, Z_QF:Z_QF + 1024], z[:, :, Z_QF:Z_QF + 1024], ALU.mult))
            settle()
            for qk, name in enumerate(("foxq", "foxk")):
                nc.vector.tensor_reduce(st("s_" + name).rearrange("p (t h) -> p t h", t=TT),
                                        squares[:, :, qk * 512:qk * 512 + 512].rearrange("p t (h r) -> p t h r", h=H),
                                        AX_X, ALU.add).then_inc(sem("sum_ready"), 1)
            dve.wait_ge(sem("logf_l"), 1)
            nc.vector.tensor_tensor(logf[:, 0, :], logf[:, 2, :], logf[:, 1, :], ALU.subtract).then_inc(sem("logf_ready"), 1)
            dve.wait_ge(sem("gfox_in"), 16 * 2 * H)
            for qk, name in enumerate(("foxq", "foxk")):
                dve.wait_ge(*rooted(name))
                for t in range(TT):
                    zz = z[:, t, Z_QF + qk * 512:Z_QF + qk * 512 + 512]
                    zh = zz.rearrange("p (h r) -> p h r", h=H)
                    mark(nc.vector.tensor_tensor(zh, zh, st("r_" + name)[:, 8 * t:8 * t + 8].unsqueeze(2)
                                                 .to_broadcast([P, H, 64]), ALU.mult))
            settle()
            for t in range(TT):
                zz = z[:, t, Z_QF:Z_QF + 1024]
                ins = nc.vector.tensor_tensor(zz, zz, gfox[:, 0, :], ALU.mult)
            ins.then_inc(sem("fqk_normed"), 1)
            dve.wait_ge(sem("cum_full"), 1)
            nc.vector.tensor_copy(cum.rearrange("p t h -> p (t h)"), ps[:, 7, 0:16]).then_inc(sem("cum_ready"), 1)
            dve.wait_ge(sem("cumt_full"), 1)
            nc.vector.tensor_scalar(ncumt, ps[0:8, 7, 256:512], -1.0, None, ALU.mult).then_inc(sem("ncumt_ready"), 1)
            dve.wait_ge(*yr_done)
            for t in range(TT):
                ins = nc.vector.tensor_tensor(fg[:, t, :], acc(t), z[:, t, Z_AR:Z_AR + D], ALU.mult)
            ins.then_inc(sem("yr_read"), 1)
            lows(FOX_O[2:4])
            yf_done = latest(FOX_O[3])
            lows(OUT2[0:2])

            def fox_mask(i, dst):
                nc.vector.scalar_tensor_tensor(out=dst[:, 0:P], in0=ps[:, 4 + i % 2, 0:P], scalar=cum[:, 0, i:i + 1],
                                               in1=mask[:, 0:P], op0=ALU.add, op1=ALU.add)
                return nc.vector.scalar_tensor_tensor(out=dst[:, P:3 * P], in0=ps[:, 4 + i % 2, P:3 * P],
                                                      scalar=cum[:, 1, i:i + 1], in1=mask[:, P:3 * P],
                                                      op0=ALU.add, op1=ALU.add)

            dve.wait_ge(sem("cum_ready"), 1)
            softmax("fox", 1.0, st_sb, fox_mask)
            dve.wait_ge(sem("fpv_full"), 1)
            nc.vector.tensor_copy(z[:, :, Z_QF:Z_QF + 512], ps[:, 0:2, :]).then_inc(sem("fo_ready"), 1)
            flip_low(0, 6)
            flip_low(1, 7)
            dve.wait_ge(*yf_done)
            for t in range(TT):
                zf = z[:, t, Z_AF:Z_AF + D]
                mark(nc.vector.tensor_tensor(zf, acc(t), zf, ALU.mult))
            dve.wait_ge(sem("yr_read"), 1)
            settle()
            for t in range(TT):
                ins = nc.vector.tensor_tensor(fg[:, t, :], fg[:, t, :], z[:, t, Z_AF:Z_AF + D], ALU.add)
            ins.then_inc(sem("merged"), 1)
            lows(OUT2[2:6])
            flip_low(0, 4)
            flip_low(0, 5, 4)
            flip_low(1, 6)
            flip_low(1, 7, 4)
            lows(OUT2[6:8])
            done = latest(OUT2[7])
            lows([2, 3], "ffn2")
            after_rows(None, None, done, following("ffn2"), [0], [1])
            lows([4, 5])
            ffn_first("ffn2", "pre_ffn2")
            ffn_rest("ffn2", "pre_ffn2")
            for t, done in enumerate(((sem("tile0_done"), count("tile0_done")), latest(5))):
                dve.wait_ge(*done)
                for half in range(2):
                    cut = slice(half * BANK, (half + 1) * BANK)
                    nc.vector.tensor_tensor(h[:, t, cut], ps[:, 2 * t + half, :], h[:, t, cut], ALU.add
                                            ).then_inc(sem("h_new"), 1)

        @block.tensor
        def _(pe):
            use = [0] * SLOTS
            seen = {}

            def count(name, by=1):
                seen[name] = seen.get(name, 0) + by
                return seen[name]

            def product(dst, lhs, rhs, first, last):
                nc.tensor.matmul(dst, lhs[0], rhs[0], start=first, stop=False)
                nc.tensor.matmul(dst, lhs[0], rhs[1], start=False, stop=False)
                return nc.tensor.matmul(dst, lhs[1], rhs[0], start=False, stop=last)

            def kt(c, t=None):
                cut = slice(0, S) if t is None else slice(t * P, t * P + P)
                return kthi[:, c, cut], ktlo[:, c, cut]

            def ht(c, t):
                return hthi[:, c, t * P:t * P + P], htlo[:, c, t * P:t * P + P]

            def slot(s, cut):
                return cut(whi[:, s, :]), cut(wlo[:, s, :])

            def made(s, n):
                pe.wait_ge(lo_done[s], n + 1)

            def take(s):
                use[s] += 1
                return use[s] - 1

            def turn(bank, src, chunks=4):
                for c in range(chunks):
                    ins = nc.tensor.transpose(ps[:, bank, c * P:(c + 1) * P], src(c), ident[:])
                return ins

            def flip(t, src, banks=(6, 7), ready=None):
                for b, bank in enumerate(banks):
                    if ready:
                        ready(b)
                    turn(bank, lambda c: src(4 * b + c, t)).then_inc(sem("flip_full"), 1)
                    count("kt_ready")

            def flip_h(k, t):
                def renewed(b):
                    if k:
                        pe.wait_ge(sem("h_new"), 4 * (k - 1) + 2 * t + b + 1)
                    elif b == 0:
                        pe.wait_ge(sem(f"x_in{t}"), 16)
                flip(t, lambda c, t: h[:, t, c * P:(c + 1) * P], ready=renewed)

            def tile_product(n_of, bank=4):
                for s in range(4):
                    made(s, n_of(s))
                    for c in range(2):
                        k = 2 * s + c
                        for t in range(TT):
                            rhs = slot(s, lambda x: x[:, c * BANK:(c + 1) * BANK])
                            ins = product(ps[:, bank + t, :], kt(k, t), rhs, k == 0, k == KC - 1)
                    ins.then_inc(slot_used[s], 1)

            def opening(k, n_of, width=BANK):
                base = seen["kt_ready"] - 2
                for t in range(TT):
                    for s in range(4):
                        made(s, n_of(s))
                        if s % 2 == 0:
                            pe.wait_ge(sem("kt_ready"), base + 2 * t + s // 2 + 1)
                        if t == 0 and s == 2:
                            flip_h(k, 1)
                        for c in range(2):
                            kc = 2 * s + c
                            rhs = slot(s, lambda x: x[:, c * BANK:c * BANK + width])
                            ins = product(ps[:, 4 + t, 0:width], kt(kc, t), rhs, kc == 0, kc == KC - 1)
                        if t:
                            ins.then_inc(slot_used[s], 1)
                    if t == 0:
                        ins.then_inc(sem("tile0_done"), 1)

            def row_chunk(s, c, t, first, last):
                for half in range(2):
                    rhs = slot(s, lambda x: x[:, half * BANK:(half + 1) * BANK])
                    ins = product(ps[:, 2 * t + half, :], kt(c, t), rhs, first, last)
                return ins

            def sum_rows(slots, chunks, more=False):
                for c in range(chunks):
                    s = slots[c]
                    made(s, take(s))
                    for t in range(TT):
                        ins = row_chunk(s, c, t, c == 0, c == chunks - 1 and not more)
                    ins.then_inc(slot_used[s], 1)

            def end_rows(slots, chunks, k):
                tail = range(chunks - 4, chunks)
                for c in tail:
                    made(slots[c], take(slots[c]))
                for t in range(TT):
                    for c in tail:
                        if t == 1 and c == chunks - 1:
                            flip_h(k, 0)
                        ins = row_chunk(slots[c], c, t, c == 0, c == chunks - 1)
                        if t:
                            ins.then_inc(slot_used[slots[c]], 1)
                    if t == 0:
                        ins.then_inc(sem("tile0_done"), 1)

            def hid_turn(bank, t, at):
                for c in range(2):
                    ins = nc.tensor.transpose(ps[:, bank, at(c):at(c) + P], hid[:, t, c * P:(c + 1) * P], ident[:])
                return ins

            def ffn_first(k):
                opening(k, lambda s: use[s])
                for s in range(4):
                    take(s)

            def ffn_rest():
                b, b_ht = seen.get("hid_ready", 0), seen.get("hid_full", 0)
                base = [n - 1 for n in use[:4]] + use[4:]
                for bank in range(4):
                    nc.tensor.matmul(ps[:, bank, :], zero[:], hthi[:], start=True, stop=False)

                def hid_flip(j):
                    pe.wait_ge(sem("hid_ready"), j * 2 + (b + 2))
                    for t in range(TT):
                        ins = hid_turn(6, t, lambda c: c * S + t * P)
                    ins.then_inc(sem("hid_full"), 1)

                def down_chunk(f, t, last):
                    for half in range(2):
                        rhs = slot(4 + f, lambda x: x[:, half * BANK:(half + 1) * BANK])
                        ins = product(ps[:, 2 * t + half, :], ht(f, t), rhs, False, last and f == 1)
                    return ins

                def down(j):
                    pe.wait_ge(sem("ht_low"), j + (b_ht + 1))
                    for f in range(2):
                        made(4 + f, j + base[4 + f])
                        for t in range(TT):
                            ins = down_chunk(f, t, False)
                        ins.then_inc(slot_used[4 + f], 1)

                hid_flip(0)
                with pe.Fori(1, NF - 1) as j:
                    tile_product(lambda s: j + base[s])
                    down(j - 1)
                    hid_flip(j)
                last = NF - 1
                for t in range(TT):
                    for s in range(4):
                        made(s, last + base[s])
                        for c in range(2):
                            k = 2 * s + c
                            ins = product(ps[:, 4 + t, :], kt(k, t), slot(s, lambda x: x[:, c * BANK:(c + 1) * BANK]),
                                          k == 0, k == KC - 1)
                        if t:
                            ins.then_inc(slot_used[s], 1)
                    if t == 0:
                        ins.then_inc(sem("tile0_done"), 1)
                        down(last - 1)
                        pe.wait_ge(sem("hid_ready"), b + 2 * last + 1)
                        hid_turn(6, 0, lambda c: c * P).then_inc(sem("hid_full"), 1)
                pe.wait_ge(sem("ht_low"), b_ht + NF)
                for f in range(2):
                    made(4 + f, last + base[4 + f])
                down_chunk(0, 0, True)
                pe.wait_ge(sem("hid_ready"), b + 2 * NF)
                hid_turn(7, 1, lambda c: c * P).then_inc(sem("hid_full"), 1)
                down_chunk(1, 0, True).then_inc(sem("tile0_done"), 1)
                pe.wait_ge(sem("ht_low"), b_ht + NF + 1)
                for f in range(2):
                    down_chunk(f, 1, True).then_inc(slot_used[4 + f], 1)
                for s in range(SLOTS):
                    use[s] += NF - 1 + (s >= 4)
                count("hid_ready", 2 * NF)
                count("hid_full", NF + 1)

            def wide(pairs, k=None):
                base, b = list(use), seen.get("wide_read", 0)

                def tile(i, par, first=False):
                    pe.wait_ge(sem("wide_read"), i * 2 + (b + par + 1))
                    if first:
                        opening(k, lambda s: base[s])
                    else:
                        tile_product(lambda s: i * 2 + (base[s] + par), bank=4 + 2 * par)

                tile(0, 0, k is not None)
                tile(0, 1)
                with pe.Fori(1, pairs) as i:
                    for par in range(2):
                        tile(i, par)
                for s in range(4):
                    use[s] += 2 * pairs
                count("wide_read", 2 * pairs)

            pe.wait_ge(sem("ident_in"), 16)
            pe.wait_ge(sem("early_in"), 16)
            nc.tensor.transpose(ps[:, 5, 0:early_rows], grow[0:early_rows, :], ident[0:early_rows, 0:early_rows]
                                ).then_inc(sem("gcol_full"), 1)
            flip_h(0, 0)
            pe.wait_ge(sem("gcol_ready"), 1)
            ffn_first(0)
            pe.wait_ge(sem("late_in"), 16 * (len(gain_rows) - 1))
            late = row - early_rows
            nc.tensor.transpose(ps[:, 7, 0:late], grow_late[0:late, :], ident[0:late, 0:late]).then_inc(sem("gcol_full"), 1)
            pe.wait_ge(sem("zero_ready"), 2)
            ffn_rest()
            flip_h(1, 0)
            wide(4, 1)
            pe.wait_ge(sem("ws_masked"), 1)
            for r in range(GROUPS // 4):
                turn(r, lambda c: ws_sb[:, 4 * r + c, :]).then_inc(sem("wst_full"), 1)
            pe.wait_ge(sem("v_ready"), TT)
            pe.wait_ge(sem("wide_read"), 2 + 8)
            pe.wait_ge(sem("wst_ready"), 4)

            def spatial(r):
                for g in (2 * r, 2 * r + 1):
                    ins = nc.tensor.matmul(ps[:, 4 + r % 2, (g % 2) * S:(g % 2) * S + S], wst[:, g, :],
                                           v_sb[:, :, g * GD:(g + 1) * GD], start=True, stop=True)
                ins.then_inc(sem("spatial_full"), 1)

            def gmlp_out(r):
                pe.wait_ge(sem("kt_ready"), kt_base + r + 1)
                for c in (2 * r, 2 * r + 1):
                    s = W_OUT[c]
                    made(s, take(s))
                    for t in range(TT):
                        ins = row_chunk(s, c, t, c == 0, False)
                    ins.then_inc(slot_used[s], 1)

            spatial(0)
            spatial(1)
            kt_base = seen["kt_ready"]
            for r in range(GROUPS // 2):
                pe.wait_ge(sem("mixed"), r + 1)
                if r >= 2:
                    pe.wait_ge(sem("kt_ready"), kt_base + r - 1)
                for c in range(2):
                    for t in range(TT):
                        ins = nc.tensor.transpose(ps[:, 6 + r % 2, c * S + t * P:c * S + t * P + P],
                                                  u_sb[:, t, (2 * r + c) * GD:(2 * r + c + 1) * GD], ident[:])
                ins.then_inc(sem("flip_full"), 1)
                if r + 2 < GROUPS // 2:
                    spatial(r + 2)
                if 1 <= r <= 6:
                    gmlp_out(r - 1)
            pe.wait_ge(sem("kt_ready"), kt_base + GROUPS // 2)
            count("kt_ready", GROUPS // 2)
            end_rows(W_OUT, GROUPS, 2)
            ffn_first(2)
            ffn_rest()
            flip_h(3, 0)
            opening(3, lambda s: use[s], width=R_KV + ROPE)
            for s in range(4):
                take(s)
            pe.wait_ge(sem("ckv_ready"), TT)
            tile_product(lambda s: use[s])
            for s in range(4):
                take(s)
            pe.wait_ge(sem("ckv_normed"), 1)
            for c in range(2):
                for t in range(TT):
                    ins = nc.tensor.transpose(ps[:, 6, c * S + t * P:c * S + t * P + P], ckv[:, t, c * P:(c + 1) * P], ident[:])
            ins.then_inc(sem("flip_full"), 1)
            pe.wait_ge(sem("krope_ready"), 1)
            for t in range(TT):
                ins = nc.tensor.transpose(ps[:, 7, t * P:(t + 1) * P], krope2[:, t, :, :].rearrange("p c n -> p (c n)"), ident[:])
            ins.then_inc(sem("krt_full"), 1)
            pe.wait_ge(sem("kt_ready"), count("kt_ready"))
            pe.wait_ge(sem("krt_ready"), 1)
            pe.wait_ge(sem("hid_ready"), seen["hid_ready"] + TT)
            for half in range(2):
                units = UKV[2 * half:2 * half + 2]
                for s in units:
                    made(s, take(s))
                for b in range(2):
                    if half:
                        pe.wait_ge(sem("knt_ready"), b + 1)
                    for e in range(2):
                        at_ = (2 * b + e) * KVW
                        for c, s in enumerate(units):
                            ins = product(ps[:, 4 + b, e * S:(e + 1) * S], slot(s, lambda x: x[:, at_:at_ + P]), kt(8 + c),
                                          c == 0, c == 1)
                    ins.then_inc(sem("knt_full"), 1)
                if half:
                    pe.wait_ge(sem("v_read"), 1)
                for t in range(TT):
                    for c, s in enumerate(units):
                        ins = product(ps[:, 6 + t, :], kt(8 + c, t),
                                      slot(s, lambda x: x.rearrange("p (h n) -> p h n", h=4)[:, :, P:2 * P]), c == 0, c == 1)
                        if t == TT - 1:
                            ins.then_inc(slot_used[s], 1)
            pe.wait_ge(sem("knt_ready"), 4)
            pe.wait_ge(sem("v_read"), 2)
            ffn_rest()
            flip_h(4, 0)
            opening(4, lambda s: use[s])
            for s in range(4):
                take(s)
            for t in range(TT):
                pe.wait_ge(sem("q_normed"), t + 1)
                flip(t, lambda c, t: qlat[:, t, c * P:(c + 1) * P], (6 + t,))
            pe.wait_ge(sem("kt_ready"), seen["kt_ready"])
            for half in range(2):
                units = UQ[4 * half:4 * half + 4]
                for s in units:
                    made(s, take(s))
                for b in range(2):
                    if half:
                        pe.wait_ge(sem("qnt_ready"), b + 1)
                    for e in range(2):
                        at_ = (2 * b + e) * QW
                        for c, s in enumerate(units):
                            ins = product(ps[:, 4 + b, e * S:(e + 1) * S], slot(s, lambda x: x[:, at_:at_ + P]), kt(c),
                                          c == 0, c == 3)
                    ins.then_inc(sem("qnt_full"), 1)
                for t in range(TT):
                    for c, s in enumerate(units):
                        ins = product(ps[:, 6 + half, t * 4 * ROPE:(t + 1) * 4 * ROPE], kt(c, t),
                                      slot(s, lambda x: x[:, 0:4 * QW].rearrange("p (h n) -> p h n", h=4)[:, :, P:QW]),
                                      c == 0, c == 3)
                        if t == TT - 1:
                            ins.then_inc(slot_used[s], 1)
            for half in range(2):
                pe.wait_ge(sem("qrope_ready"), half + 1)
                for c in range(2):
                    for t in range(TT):
                        at_ = 4 * half + 2 * c
                        ins = nc.tensor.transpose(ps[:, half, c * S + t * P:c * S + t * P + P],
                                                  qrope[:, t, at_:at_ + 2, :].rearrange("p h r -> p (h r)"), ident[:])
                ins.then_inc(sem("qrt_full"), 1)

            def attention(kind, scores, output, probs, turned_probs):
                def turn(i):
                    pe.wait_ge(sem(kind + "_p_ready"), i + 1)
                    if i >= 1:
                        pe.wait_ge(sem(kind + "_pt_ready"), i)
                    for b in range(3):
                        ins = nc.tensor.transpose(ps[:, 6, b * P:(b + 1) * P], probs[:, i % 2, b * P:(b + 1) * P], ident[:])
                    ins.then_inc(sem(kind + "_pt_full"), 1)

                for i in range(H + 1):
                    if i < H:
                        if i >= 2:
                            pe.wait_ge(sem(kind + "_masked"), i - 1)
                        scores(i).then_inc(sem(kind + "_scores_full"), 1)
                    if i >= 1:
                        turn(i - 1)
                        pe.wait_ge(sem(kind + "_pt_ready"), i)
                        output(i - 1, turned_probs[:, (i - 1) % 2, :])

            def mla_scores(i):
                bank, e = ps[:, 4 + i % 2, :], ROPE * (i % 2)
                for t in range(TT):
                    dst = bank[:, 0:P] if t == 0 else bank[:, P:3 * P]
                    keys, q = slice(0, (t + 1) * P), slice(t * P, (t + 1) * P)
                    nc.tensor.matmul(dst, qnt[:, i, q], knt[:, i, keys], start=True, stop=False)
                    ins = nc.tensor.matmul(dst, qrt[e:e + ROPE, i // 2, q], krt[e:e + ROPE, keys], start=False, stop=True)
                return ins

            def mla_output(i, pt):
                at_ = (i % 2) * S
                bank, v = i // 2, v_mla[:, :, i * P:(i + 1) * P]
                nc.tensor.matmul(ps[:, bank, at_:at_ + S], v[:, 0, :], pt[:, 0:S], start=True, stop=False)
                ins = nc.tensor.matmul(ps[:, bank, at_ + P:at_ + S], v[:, 1, :], pt[:, S:3 * P], start=False, stop=True)
                if i % 2:
                    ins.then_inc(sem("flip_full"), 1)

            pe.wait_ge(sem("qnt_ready"), 4)
            pe.wait_ge(sem("qrt_ready"), 2)
            attention("mla", mla_scores, mla_output, p_sb, pt_sb)
            pe.wait_ge(sem("kt_ready"), count("kt_ready", H // 2))
            sum_rows(WO, 4, more=True)
            end_rows(WO, H, 5)
            ffn_first(5)
            ffn_rest()
            flip_h(6, 0)
            wide(3, 6)
            made(4, take(4))
            for c in range(KC):
                for t in range(TT):
                    ins = product(ps[:, t, 0:8], kt(c, t), slot(4, lambda x: x[:, 8 * c:8 * c + 8]), c == 0, c == KC - 1)
            ins.then_inc(slot_used[4], 1)
            wide(2)
            pe.wait_ge(sem("r_rotated"), 1)
            pe.wait_ge(sem("wide_read"), 20)
            for r in range(2):
                for c in range(2):
                    for t in range(TT):
                        at_ = (2 * r + c) * P
                        ins = nc.tensor.transpose(ps[:, 6 + r, c * S + t * P:c * S + t * P + P], ro_t[:, t, at_:at_ + P], ident[:])
                ins.then_inc(sem("rqk_full"), 1)
            pe.wait_ge(sem("rqk_ready"), 2)
            pe.wait_ge(sem("f_ready"), 1)
            for i in range(HR + 1):
                if i < HR:
                    e = ROPE * (i % 2)
                    q, key = turned[e:e + ROPE, i // 2, :], turned[e:e + ROPE, 2 + i // 2, :]
                    if i >= 2:
                        pe.wait_ge(sem("rst_ready"), i - 1)
                    nc.tensor.matmul(ps[:, 4 + i % 2, 0:S], key[:, 0:P], q[:, 0:S], start=True, stop=True)
                    nc.tensor.matmul(ps[:, 4 + i % 2, S:3 * P], key[:, P:S], q[:, P:S], start=True, stop=True
                                     ).then_inc(sem("rst_full"), 1)
                if i >= 1:
                    j = i - 1
                    pe.wait_ge(sem("rst_ready"), j + 1)
                    w, v = st_sb[:, j % 2, :], z[:, :, Z_VR + j * P:Z_VR + (j + 1) * P]
                    nc.tensor.matmul(ps[:, 0, j * P:(j + 1) * P], w[:, 0:P], v[:, 0, :], start=True, stop=True)
                    nc.tensor.matmul(ps[:, 1, j * P:(j + 1) * P], w[:, P:S], v[:, 0, :], start=True, stop=False)
                    nc.tensor.matmul(ps[:, 1, j * P:(j + 1) * P], w[:, S:3 * P], v[:, 1, :], start=False, stop=True
                                     ).then_inc(sem("rpv_done"), 1)
            pe.wait_ge(sem("ro_ready"), 1)
            for t in range(TT):
                flip(t, lambda c, t: ro_t[:, t, c * P:(c + 1) * P], (6 + t,))
            pe.wait_ge(sem("kt_ready"), seen["kt_ready"])
            sum_rows(RET_O, 4)
            pe.wait_ge(sem("logf_ready"), 1)
            pe.wait_ge(sem("fox_c_in"), 48)
            nc.tensor.matmul(ps[:, 7, 0:8], upto, logf[:, 0, 0:8], start=True, stop=True)
            nc.tensor.matmul(ps[:, 7, 8:16], upto, logf[:, 0, 8:16], start=True, stop=False)
            nc.tensor.matmul(ps[:, 7, 8:16], ones, logf[:, 0, 0:8], start=False, stop=True).then_inc(sem("cum_full"), 1)
            pe.wait_ge(sem("cum_ready"), 1)
            for t in range(TT):
                ins = nc.tensor.transpose(ps[0:8, 7, S + t * P:S + (t + 1) * P], cum[:, t, :], ident[:])
            ins.then_inc(sem("cumt_full"), 1)
            pe.wait_ge(sem("fqk_normed"), 1)
            pe.wait_ge(sem("ncumt_ready"), 1)
            for r in range(4):
                for t in range(TT):
                    for c in range(2):
                        at_ = Z_QF + (2 * r + c) * P
                        ins = nc.tensor.transpose(ps[:, 4 + r, c * S + t * P:c * S + (t + 1) * P], z[:, t, at_:at_ + P], ident[:])
                ins.then_inc(sem("fqk_full"), 1)
            pe.wait_ge(sem("fqk_ready"), 4)
            pe.wait_ge(sem("yr_read"), 1)

            def fox_scores(i):
                bank, e = ps[:, 4 + i % 2, :], 64 * (i % 2)
                q, key = turned[e:e + 64, i // 2, :], turned[e:e + 64, 4 + i // 2, :]
                for t in range(TT):
                    dst = bank[:, 0:P] if t == 0 else bank[:, P:3 * P]
                    keys = slice(0, (t + 1) * P)
                    nc.tensor.matmul(dst, q[:, t * P:(t + 1) * P], key[:, keys], start=True, stop=False)
                    ins = nc.tensor.matmul(dst, sel[0:8, i, :], ncumt[:, keys], start=False, stop=True)
                return ins

            def fox_output(i, pt):
                v, at_ = z[:, :, Z_VF + i * 64:Z_VF + (i + 1) * 64], slice(i * 64, (i + 1) * 64)
                nc.tensor.matmul(ps[:, 0, at_], pt[:, 0:P], v[:, 0, :], start=True, stop=True)
                nc.tensor.matmul(ps[:, 1, at_], pt[:, P:S], v[:, 0, :], start=True, stop=False)
                ins = nc.tensor.matmul(ps[:, 1, at_], pt[:, S:3 * P], v[:, 1, :], start=False, stop=True)
                if i == H - 1:
                    ins.then_inc(sem("fpv_full"), 1)

            attention("fox", fox_scores, fox_output, st_sb, pt2_sb)
            pe.wait_ge(sem("fo_ready"), 1)
            for t in range(TT):
                flip(t, lambda c, t: z[:, t, Z_QF + c * P:Z_QF + (c + 1) * P], (6 + t,))
            pe.wait_ge(sem("kt_ready"), seen["kt_ready"])
            sum_rows(FOX_O, 4)
            pe.wait_ge(sem("merged"), 1)
            for t in range(TT):
                flip(t, lambda c, t: fg[:, t, c * P:(c + 1) * P], (4 + 2 * t, 5 + 2 * t))
            pe.wait_ge(sem("kt_ready"), seen["kt_ready"])
            sum_rows(OUT2, 4, more=True)
            end_rows(OUT2, KC, 7)
            ffn_first(7)
            ffn_rest()


OUT_SHAPE = (1, 256, 1024)


def kernel(**inputs):
    import concourse.bacc as bacc
    from concourse.bass_utils import run_bass_kernel_spmd

    nc = bacc.Bacc("TRN2", target_bir_lowering=False, num_devices=1)
    arrays = {name: np.ascontiguousarray(x) for name, x in inputs.items()}
    rope = arrays["w_dkv"].shape[1] - arrays["kv_a_norm_g"].shape[0]
    arrays.update(shape_constants(arrays["x"].shape[1], rope, 4))
    aps, sent = {}, {}
    for name, x in arrays.items():
        sent["in_" + name] = x
        aps[name] = nc.dram_tensor("in_" + name, x.shape, mybir.dt.from_np(x.dtype), kind="ExternalInput").ap()
    out = nc.dram_tensor("out", OUT_SHAPE, F32, kind="ExternalOutput").ap()
    build(nc, aps, out)
    return run_bass_kernel_spmd(nc, [sent], core_ids=[0]).results[0]["out"]
```

```python
from contextlib import ExitStack
import math

import numpy as np

import concourse.bass as bass
from concourse import mybir

ALU = mybir.AluOpType
ACT = mybir.ActivationFunctionType
AX_X = mybir.AxisListType.X
F32 = mybir.dt.float32
F32R = mybir.dt.float32r
I32 = mybir.dt.int32

P = 128
BANK = 512
SLOTS = 6
UNIT = 1024
RMS_EPS = 1e-6
LN_EPS = 1e-5
ROPE_BASE = 10000.0
NEG = -1e30
TWO_PI = (6.28125, 0.0019350051879882812, 3.0199159819567926e-07)
PI_DOWN = 3.141592502593994
ROUND = 1.5 * 2.0 ** 23


def shape_constants(s, rope, heads_r):
    f = np.float32
    i = np.arange(P)
    causal = np.where(i[None, :] <= i[:, None], 0.0, NEG)
    out = {
        "c_ident": np.eye(P),
        "c_mask": np.concatenate([causal, np.zeros((P, P)), causal], 1),
        "c_upto": (i[:, None] <= i[None, :]).astype(f),
        "c_ones": np.ones((P, P)),
    }
    sel = np.zeros((8, 8, P))
    for h in range(8):
        sel[h, h] = 1.0
    out["c_sel"] = sel.reshape(8, 8 * P)
    half = rope // 2
    out["c_freq"] = np.broadcast_to(ROPE_BASE ** (-np.arange(half) / half), (P, half))
    freq = (1.0 / (ROPE_BASE ** (np.arange(half, dtype=f) / f(half))).astype(f)).astype(f)
    ang = (np.arange(s, dtype=f)[:, None] * freq[None, :]).astype(f).astype(np.float64)
    out["c_cos"], out["c_sin"] = np.cos(ang), np.sin(ang)
    log_g = np.log1p(-(2.0 ** (-5.0 - np.arange(heads_r))))
    diff = np.arange(2 * P)[None, :] - i[:, None]
    d = np.where(diff[None] >= 0, np.exp(np.maximum(diff, 0)[None] * log_g[:, None, None]), 0.0) * rope ** -0.5
    d = np.concatenate([d, d[:, :, :P]], 2)
    out["c_decay"] = np.transpose(d, (1, 0, 2)).reshape(P, heads_r * 3 * P)
    return {k: np.ascontiguousarray(v, dtype=f) for k, v in out.items()}


def build(nc, a, out):
    S, D = a["x"].shape[1:]
    TT = S // P
    KC = D // P
    F = a["ffn_w_gate"].shape[-1]
    FT = 256
    NF = F // FT
    HALF = a["gmlp_ln_g"].shape[-1]
    GROUPS = a["gmlp_w_s"].shape[1]
    GD = HALF // GROUPS
    R_KV = a["kv_a_norm_g"].shape[0]
    R_Q = a["mla_q_norm_g"].shape[1]
    ROPE = a["w_dkv"].shape[1] - R_KV
    H = 8
    NOPE = P
    QW = NOPE + ROPE
    KVW = 2 * P
    HR = 4
    ZW = a["w_in_2"].shape[-1]
    RH = ROPE // 2
    assert TT == 2 and KC == 8 and F % FT == 0 and GD == P and ROPE == 64 and a["w_ukv"].shape[1] == H * KVW
    assert a["mla_w_uq"].shape[2] == H * QW
    Z_QR, Z_KR, Z_VR, Z_GT, Z_QF, Z_KF, Z_VF, Z_F, Z_AR, Z_AF = 0, 256, 512, 1024, 1536, 2048, 2560, 3072, 3080, 4104
    assert ZW == Z_AF + D
    MLA_SCALE = float(QW) ** -0.5

    ctx = ExitStack()
    with ctx:
        def sb(name, shape, dt=F32):
            return ctx.enter_context(nc.sbuf_tensor(name, shape, dt))

        sems = {}

        def sem(name):
            if name not in sems:
                sems[name] = ctx.enter_context(nc.semaphore(name))
            return sems[name]

        raw = sb("raw", [P, SLOTS, UNIT])
        whi = sb("whi", [P, SLOTS, UNIT], F32R)
        wlo = sb("wlo", [P, SLOTS, UNIT], F32R)
        kthi = sb("kthi", [P, 16, S], F32R)
        ktlo = sb("ktlo", [P, 16, S], F32R)
        hthi = sb("hthi", [P, 2, S], F32R)
        htlo = sb("htlo", [P, 2, S], F32R)
        h = sb("h", [P, TT, D])
        fg = sb("fg", [P, TT, D])
        gpost = sb("gpost", [P, 2, D])
        hid = sb("hid", [P, TT, FT])
        ident = sb("ident", [P, P])
        mask = sb("mask", [P, 3 * P])
        gcol = sb("gcol", [P, P])
        half_neg = sb("half_neg", [P, 40])
        stat = sb("stat", [P, 400])
        rcos = sb("rcos", [P, TT, RH])
        rsin = sb("rsin", [P, TT, RH])
        arena = sb("arena", [P, 16384])
        sq_out = sb("sq_out", [P, TT, D], mybir.dt.bfloat16)
        ps = ctx.enter_context(nc.psum_tensor("ps", [P, 8, BANK], F32))

        def view(at, *dims):
            n = math.prod(dims)
            v = arena[:, at:at + n]
            names = "abcd"[:len(dims)]
            if len(dims) == 1:
                return v
            return v.rearrange(f"p ({' '.join(names)}) -> p {' '.join(names)}", **dict(zip(names[1:], dims[1:])))

        vu = view(0, TT, 2 * HALF)
        v_sb, u_sb = vu[:, :, 0:HALF], vu[:, :, HALF:2 * HALF]
        ws_sb, wst = view(8192, GROUPS, P), view(10240, GROUPS, P)
        ln_g, ln_b = view(12288, HALF), view(14336, HALF)
        grow, grow_late = view(0, P), view(640, P)
        freq = view(256, RH)
        posf = view(320, TT)
        ang, turns, red, whole = view(384, TT, RH), view(448, TT, RH), view(512, TT, RH), view(576, TT, RH)
        pos_i = sb("pos_i", [P, TT], I32)
        ckv = view(0, TT, R_KV + ROPE)
        krope2 = view(640, TT, 2, ROPE)
        krt = view(896, S)
        knt = view(1152, H, S)
        v_mla = view(3200, TT, H * P)
        qlat = view(5248, TT, R_Q)
        qnt = view(6272, H, S)
        qrope = view(8320, TT, H, ROPE)
        qrt = view(9344, H // 2, S)
        rope_t = view(10368, 2, H * RH)
        p_sb = view(10880, 3, 3 * P)
        pt_sb = view(12032, 2, 3 * P)
        z = view(0, TT, ZW)
        o = TT * ZW
        turned = view(o, 8, S)
        ro_t = view(o + 2048, 2, 512)
        st_sb = view(o + 3072, 2, 3 * P)
        p2_sb = view(0, 3, 3 * P)
        pt2_sb = view(o + 3840, 2, 3 * P)
        decay = view(o + 3840, HR, 3 * P)
        assert o + 5952 <= 16384
        gfox = gpost
        upto, ones = hid[:, 0, 0:P], hid[:, 0, P:2 * P]
        sel = view(o + 4608, 8, P)
        cos2, sin2 = sb("cos2", [P, TT, RH]), sb("sin2", [P, TT, RH])
        bfor = sb("bfor", [P, 8])
        logf, cum = view(o + 5888, 3, TT * 8), view(o + 5936, TT, 8)
        ncumt = view(o + 5632, S)[0:8]

        gain_col = {}
        gain_rows = []
        row = 0
        for names, ap in (
            (("ffn00", "ffn01", "ffn10", "ffn11"), a["ffn_pre_g"].rearrange("l f (c p) -> (l f c) p", p=P)),
            (("mix0", "mix1"), a["mix_pre_g"].rearrange("l (c p) -> (l c) p", p=P)),
            (("kv",), a["kv_norm_g"].rearrange("(c p) -> c p", p=P)),
            (("mix2",), a["g_mix_2"][0].rearrange("(c p) -> c p", p=P)),
            (("ffn2",), a["g_ffn_2"][0].rearrange("(c p) -> c p", p=P)),
            (("kva",), a["kv_a_norm_g"].rearrange("(c p) -> c p", p=P)),
            (("q",), a["mla_q_norm_g"][0].rearrange("(c p) -> c p", p=P)),
            (("bs",), a["gmlp_b_s"][0]),
        ):
            n = ap.shape[0]
            for i, name in enumerate(names):
                gain_col[name] = row + i * (n // len(names))
            gain_rows.append((row, n, ap))
            row += n
        early_rows = gain_rows[0][1]
        assert row <= P

        cols = {}
        at = [0]

        def st(name, n=1):
            if name not in cols:
                cols[name] = (at[0], n)
                at[0] += n
                assert at[0] <= 400
            c, n = cols[name]
            return stat[:, c:c + n]

        roots = []

        def root(name, scale, eps, n=1, signals=1, halves=1):
            st("s_" + name, n * halves)
            st("r_" + name, n)
            roots.append((name, n, scale, eps, signals, halves))

        def pre(k, t):
            root(f"pre_{k}{t}", 1.0 / D, RMS_EPS)

        def post(k, t, by):
            root(f"post_{k}{t}", 1.0 / D / by ** 2, RMS_EPS / by ** 2, signals=2, halves=2)

        def after_ffn(k, following):
            post(k, 0, 0.5); post(k, 1, 0.5); pre(following, 0); pre(following, 1)

        def after_rows(k, following):
            post(k, 0, 1.0); pre(following, 0); post(k, 1, 1.0); pre(following, 1)

        pre("ffn00", 0); pre("ffn00", 1)
        after_ffn("ffn00", "mix0")
        root("ln", 1.0, LN_EPS, n=TT)
        after_rows("mix0", "ffn01")
        after_ffn("ffn01", "kv")
        root("kva", 1.0 / R_KV, RMS_EPS, n=TT)
        after_ffn("ffn10", "mix1")
        root("q0", 1.0 / R_Q, RMS_EPS); root("q1", 1.0 / R_Q, RMS_EPS)
        after_rows("mix1", "ffn11")
        after_ffn("ffn11", "mix2")
        root("foxq", 1.0, 64 * RMS_EPS, n=TT * H)
        root("foxk", 1.0 / 64, RMS_EPS, n=TT * H)
        root("ret", 1.0, RMS_EPS, n=TT * HR)
        pre("ffn2", 0); pre("ffn2", 1)

        sum_before, root_number = {}, {}
        for number, (name, *_) in enumerate(roots):
            sum_before[name] = sum(r[4] for r in roots[:number])
            root_number[name] = number + 1

        def sums(name, signals):
            return sem("sum_ready"), sum_before[name] + signals

        def rooted(name):
            return sem("root_ready"), root_number[name]

        raw_in = [sem(f"raw_in{i}") for i in range(SLOTS)]
        hi_done = [sem(f"hi_done{i}") for i in range(SLOTS)]
        lo_done = [sem(f"lo_done{i}") for i in range(SLOTS)]
        slot_used = [sem(f"slot_used{i}") for i in range(SLOTS)]

        W_OUT = [0, 1, 2, 3, 4, 5] + [2, 3, 4, 5, 0, 1] + [4, 5, 2, 3]
        DKV = [0, 1, 2, 3]
        UKV = [4, 5, 2, 3]
        DQ = [0, 1, 2, 3]
        UQ = [4, 5, 0, 1, 2, 3, 4, 5]
        WO = [0, 1, 2, 3, 4, 5, 2, 3]
        RET_O = [4, 5, 0, 1]
        FOX_O = [2, 3, 4, 5]
        OUT2 = [0, 1, 2, 3, 4, 5, 2, 3]

        ROPE_BANK, NOPE_BANK = (6, 2), ((4, 5), (1, 3))

        block = ctx.enter_context(nc.Block())

        @block.sync
        def _(sp):
            use = [0] * SLOTS

            def take(s):
                use[s] += 1
                return use[s] - 1

            def load(s, n, first, second):
                if not (isinstance(n, int) and n == 0):
                    sp.wait_ge(lo_done[s], n)
                for dst, src in (first, second):
                    sp.dma_start(dst, src).then_inc(raw_in[s], 16)

            def pair(s):
                return raw[:, s, :].rearrange("p (c n) -> p c n", c=2)

            def gate_up(s, n, gate, up, col):
                load(s, n, (pair(s)[:, :, 0:FT], gate[:, 2 * s:2 * s + 2, bass.ds(col, FT)]),
                     (pair(s)[:, :, FT:2 * FT], up[:, 2 * s:2 * s + 2, bass.ds(col, FT)]))

            def rows(s, n, w, c):
                wc = w[:, bass.ds(c, 1), :].rearrange("p c n -> p (c n)")
                load(s, n, (raw[:, s, 0:512], wc[:, 0:512]), (raw[:, s, 512:1024], wc[:, 512:1024]))

            def chunked(w):
                return w.rearrange("(c p) n -> p c n", p=P)

            def ffn_first(w_gate, w_up):
                gate, up = chunked(w_gate), chunked(w_up)
                for s in range(4):
                    gate_up(s, take(s), gate, up, 0)

            def ffn_rest(w_gate, w_up, w_down, between=()):
                gate, up, down = chunked(w_gate), chunked(w_up), chunked(w_down)
                for f in range(2):
                    rows(4 + f, take(4 + f), down, f)
                base = [n - 1 for n in use]
                parts = len(between) + 1
                for part in range(parts):
                    with sp.Fori(1 + part * (NF - 1) // parts, 1 + (part + 1) * (NF - 1) // parts) as j:
                        for s in range(4):
                            gate_up(s, j + base[s], gate, up, j * FT)
                        for f in range(2):
                            rows(4 + f, j + base[4 + f], down, j * 2 + f)
                    if part < len(between):
                        between[part]()
                for s in range(SLOTS):
                    use[s] += NF - 1

            def ffn(w_gate, w_up, w_down, between=()):
                ffn_first(w_gate, w_up)
                ffn_rest(w_gate, w_up, w_down, between)

            def tile512(s, n, w, col):
                load(s, n, (pair(s)[:, 0, :], w[:, 2 * s, bass.ds(col, BANK)]),
                     (pair(s)[:, 1, :], w[:, 2 * s + 1, bass.ds(col, BANK)]))

            def wide(w, col0, tiles):
                base = list(use)
                with sp.Fori(0, tiles) as i:
                    for s in range(4):
                        tile512(s, i + base[s], w, i * BANK + col0)
                for s in range(4):
                    use[s] += tiles

            def all_rows(slots, w):
                for c, s in enumerate(slots):
                    rows(s, take(s), w, c)

            def tokens(t):
                return a["x"][0, t * P:(t + 1) * P, :]

            sp.dma_start(ident[:], a["c_ident"]).then_inc(sem("ident_in"), 16)
            r, n, ap = gain_rows[0]
            sp.dma_start(grow[r:r + n, :], ap).then_inc(sem("early_in"), 16)
            sp.dma_start(freq, a["c_freq"]).then_inc(sem("pos_in"), 16)
            with nc.allow_non_contiguous_dma(reason="256 positions"):
                sp.dma_start(pos_i[:], a["positions"][0].rearrange("(t p) -> p t", p=P)).then_inc(sem("pos_in"), 16)
            sp.dma_start(h[:, 0, :], tokens(0)).then_inc(sem("x_in0"), 16)
            ffn_first(a["ffn_w_gate"][0, 0], a["ffn_w_up"][0, 0])
            sp.dma_start(h[:, 1, :], tokens(1)).then_inc(sem("x_in1"), 16)

            posts = [0]

            def load_post(g):
                k = posts[0]
                if k >= 2:
                    sp.wait_ge(sem("h_new"), 4 * (k - 1))
                sp.dma_start(gpost[:, k % 2, :], g.partition_broadcast(P)).then_inc(sem(f"gpost_in{k % 2}"), 16)
                posts[0] += 1

            def load_ws(half):
                sp.wait_ge(sem("gcol_ready"), 2)
                sp.wait_ge(sem("rope_ready"), 1)
                g = slice(half * GROUPS // 2, (half + 1) * GROUPS // 2)
                sp.dma_start(ws_sb[:, g, :], a["gmlp_w_s"][0, g].rearrange("g t c -> t g c")).then_inc(sem("ws_in"), 16)

            def load_constants():
                sp.dma_start(mask[:], a["c_mask"]).then_inc(sem("mask_in"), 16)
                sp.dma_start(cos2[:], a["c_cos"].rearrange("(t p) d -> p t d", p=P)).then_inc(sem("rope2_in"), 16)
                sp.dma_start(sin2[:], a["c_sin"].rearrange("(t p) d -> p t d", p=P)).then_inc(sem("rope2_in"), 16)
                sp.dma_start(bfor[:], a["b_forget_2"][0].partition_broadcast(P)).then_inc(sem("bfor_in"), 16)

            def load_ln(dst, src, half):
                cut = slice(half * HALF // 2, (half + 1) * HALF // 2)
                sp.dma_start(dst[:, cut], src[0, cut].partition_broadcast(P)).then_inc(sem("ln_in"), 16)

            ffn_rest(a["ffn_w_gate"][0, 0], a["ffn_w_up"][0, 0], a["ffn_w_down"][0, 0],
                     (lambda: load_ln(ln_g, a["gmlp_ln_g"], 0), lambda: load_post(a["ffn_post_g"][0, 0]),
                      lambda: load_ln(ln_g, a["gmlp_ln_g"], 1), lambda: load_ws(0), lambda: load_ws(1)))
            w_in = chunked(a["gmlp_w_in"][0])
            wide(w_in, HALF, 2)
            load_ln(ln_b, a["gmlp_ln_b"], 0)
            wide(w_in, HALF + UNIT, 2)
            load_ln(ln_b, a["gmlp_ln_b"], 1)
            wide(w_in, 0, 2)
            load_post(a["mix_post_g"][0])
            wide(w_in, UNIT, 2)
            load_constants()
            all_rows(W_OUT, chunked(a["gmlp_w_out"][0]))
            ffn(a["ffn_w_gate"][0, 1], a["ffn_w_up"][0, 1], a["ffn_w_down"][0, 1],
                (lambda: load_post(a["ffn_post_g"][0, 1]), lambda: load_post(a["ffn_post_g"][1, 0])))
            dkv = chunked(a["w_dkv"])
            for c, s in enumerate(DKV):
                load(s, take(s), (pair(s)[:, 0, 0:R_KV + ROPE], dkv[:, 2 * c, :]),
                     (pair(s)[:, 1, 0:R_KV + ROPE], dkv[:, 2 * c + 1, :]))
            ukv = chunked(a["w_ukv"])


            def ukv_unit(i):
                s = UKV[i]
                w = ukv[:, i % 2, (i // 2) * UNIT:(i // 2 + 1) * UNIT]
                load(s, take(s), (raw[:, s, 0:512], w[:, 0:512]), (raw[:, s, 512:1024], w[:, 512:1024]))

            ukv_unit(0)
            ukv_unit(1)
            ffn_first(a["ffn_w_gate"][1, 0], a["ffn_w_up"][1, 0])
            ukv_unit(2)
            ukv_unit(3)
            ffn_rest(a["ffn_w_gate"][1, 0], a["ffn_w_up"][1, 0], a["ffn_w_down"][1, 0],
                     (lambda: load_post(a["mix_post_g"][1]),))
            dq = chunked(a["mla_w_dq"][0])
            for s in DQ:
                tile512(s, take(s), dq, 0)
            uq = chunked(a["mla_w_uq"][0])
            for i, s in enumerate(UQ):
                w = uq[:, i % 4, (i // 4) * 768:(i // 4 + 1) * 768]
                load(s, take(s), (raw[:, s, 0:384], w[:, 0:384]), (raw[:, s, 384:768], w[:, 384:768]))
            all_rows(WO, chunked(a["mla_w_o"][0]))
            ffn(a["ffn_w_gate"][1, 1], a["ffn_w_up"][1, 1], a["ffn_w_down"][1, 1],
                (lambda: load_post(a["ffn_post_g"][1, 1]),))
            w_in2 = chunked(a["w_in_2"][0])
            for s in range(4):
                tile512(s, take(s), w_in2, 0)
            s = 4
            load(s, take(s), (raw[:, s, 0:32].rearrange("p (c n) -> p c n", c=4), w_in2[:, 0:4, Z_F:Z_F + 8]),
                 (raw[:, s, 32:64].rearrange("p (c n) -> p c n", c=4), w_in2[:, 4:8, Z_F:Z_F + 8]))
            wide(w_in2, BANK, 5)
            sp.wait_ge(sem("h_new"), 24)
            for qk, g in ((0, a["g_fox_q_2"]), (1, a["g_fox_k_2"])):
                for head in range(H):
                    sp.dma_start(gfox[:, 0, qk * 512 + head * 64:qk * 512 + head * 64 + 64],
                                 g[0].partition_broadcast(P)).then_inc(sem("gfox_in"), 16)
            sp.dma_start(upto, a["c_upto"]).then_inc(sem("cum_c_in"), 16)
            sp.dma_start(ones, a["c_ones"]).then_inc(sem("cum_c_in"), 16)
            wide(w_in2, Z_AR, 4)
            sp.dma_start(decay, a["c_decay"].rearrange("p (h n) -> p h n", h=HR)).then_inc(sem("decay_in"), 16)
            sp.dma_start(gfox[:, 1, 0:512], a["g_ret_norm_2"][0].partition_broadcast(P)).then_inc(sem("gret_in"), 16)
            all_rows(RET_O, chunked(a["w_ret_o_2"][0]))
            all_rows(FOX_O, chunked(a["w_fox_o_2"][0]))
            sp.wait_ge(sem("rst_ready"), HR)
            sp.dma_start(sel[0:8], a["c_sel"].rearrange("k (h q) -> k h q", h=8)).then_inc(sem("sel_in"), 16)
            all_rows(OUT2, chunked(a["w_out_2"][0]))
            ffn(a["w_gate_2"][0], a["w_up_2"][0], a["w_down_2"][0])
            for t in range(TT):
                for half in range(2):
                    sp.wait_ge(sem("h_new"), 29 + 2 * t + half)
                    cut = slice(half * BANK, (half + 1) * BANK)
                    sp.dma_start(out[0, t * P:(t + 1) * P, cut], h[:, t, cut]).then_inc(sem("out_done"), 16)
            sp.wait_ge(sem("out_done"), 16 * 2 * TT)

        @block.gpsimd
        def _(pool):
            own = [0]

            def step(ins):
                own[0] += 1
                ins.then_inc(sem("pool_own"), 1)
                pool.wait_ge(sem("pool_own"), own[0])

            step(nc.gpsimd.memset(half_neg[:], -0.5))
            for name, n, scale, eps, signals, halves in roots:
                if name == "post_ffn000":
                    pool.wait_ge(sem("ws_in"), 32)
                    nc.gpsimd.affine_select(out=ws_sb, in_=ws_sb, compare_op=ALU.is_ge, fill=0.0, base=0,
                                            pattern=[[0, GROUPS], [-1, P]], channel_multiplier=1
                                            ).then_inc(sem("ws_masked"), 1)
                pool.wait_ge(*sums(name, signals))
                total = st("s_" + name)[:, 0:n]
                if halves == 2:
                    step(nc.gpsimd.tensor_tensor(total, total, st("s_" + name)[:, 1:2], ALU.add))
                step(nc.gpsimd.tensor_scalar(total, total, scale, eps, ALU.mult, ALU.add))
                nc.gpsimd.tensor_tensor(st("r_" + name), total, half_neg[:, 0:n],
                                        ALU.pow).then_inc(sem("root_ready"), 1)
                if name == "ln":
                    pool.wait_ge(sem("ln_in"), 64)
                    for t in range(TT):
                        pool.wait_ge(sem("v_normed"), t + 1)
                        step(nc.gpsimd.tensor_tensor(v_sb[:, t, :], v_sb[:, t, :], ln_g, ALU.mult))
                        nc.gpsimd.tensor_tensor(v_sb[:, t, :], v_sb[:, t, :], ln_b, ALU.add
                                                ).then_inc(sem("v_ready"), 1)

        @block.scalar
        def _(act):
            use = [0] * SLOTS
            seen = {}
            own = [0]

            def count(name, by=1):
                seen[name] = seen.get(name, 0) + by
                return seen[name]

            def high(s, n, gain=None, width=None, each=None):
                act.wait_ge(raw_in[s], n * 32 + 32)
                if not (isinstance(n, int) and n == 0):
                    act.wait_ge(slot_used[s], n)
                if gain is not None:
                    for c in range(2):
                        cut, k = slice(c * BANK, c * BANK + (width or BANK)), gain_col[gain] + 2 * s + c
                        ins = nc.scalar.activation(whi[:, s, cut], raw[:, s, cut], ACT.Copy, scale=gcol[:, k:k + 1])
                elif each is not None:
                    ins = nc.scalar.activation(whi[:, s, 0:width], raw[:, s, 0:width], ACT.Copy, scale=gcol[:, each:each + 1])
                else:
                    ins = nc.scalar.copy(whi[:, s, 0:width or UNIT], raw[:, s, 0:width or UNIT])
                ins.then_inc(hi_done[s], 1)

            def take(s):
                use[s] += 1
                return use[s] - 1

            def highs(slots, gain=None, width=None):
                for s in slots:
                    high(s, take(s), gain, width)

            def following(gain=None, width=None):
                return lambda s: high(s, take(s), gain, width)

            def gated_tile(t, pre):
                nc.scalar.activation(hid[:, t, :], ps[:, 4 + t, 0:FT], ACT.Silu, scale=st(f"r_{pre}{t}")
                                     ).then_inc(sem("silu_done"), 1)

            def tile0():
                act.wait_ge(sem("tile0_done"), count("tile0_done"))

            def ffn_first(name, pre):
                more = following(name)
                act.wait_ge(*rooted(pre + "0"))
                tile0()
                gated_tile(0, pre)
                for s in range(3):
                    more(s)
                act.wait_ge(*rooted(pre + "1"))
                act.wait_ge(slot_used[3], use[3])
                gated_tile(1, pre)
                more(3)

            def ffn_rest(name, pre, then=None):
                base, b = [n - 1 for n in use], seen.get("hid_full", 0)

                def turned_hidden(j):
                    act.wait_ge(sem("hid_full"), j + (b + 1))
                    nc.scalar.copy(hthi[:].rearrange("p c n -> p (c n)"), ps[:, 6, :]).then_inc(sem("ht_high"), 1)

                def turned_tile(t):
                    act.wait_ge(sem("hid_full"), b + NF + t)
                    nc.scalar.copy(hthi[:, :, t * P:(t + 1) * P], ps[:, 6 + t, 0:2 * P].rearrange("p (c n) -> p c n", c=2)
                                   ).then_inc(sem("ht_high"), 1)

                turned_hidden(0)
                with act.Fori(1, NF - 1) as j:
                    for s in range(3):
                        high(s, j + base[s], name)
                    act.wait_ge(slot_used[3], j + base[3])
                    for t in range(TT):
                        gated_tile(t, pre)
                    high(3, j + base[3], name)
                    for s in (4, 5):
                        high(s, j + base[s])
                    turned_hidden(j)
                for s in range(SLOTS):
                    use[s] += NF - 2
                tile0()
                gated_tile(0, pre)
                highs([4])
                turned_tile(0)
                highs([5])
                last = slot_used[3], use[3]
                if then:
                    for s in range(3):
                        then(s)
                act.wait_ge(*last)
                gated_tile(1, pre)
                if then:
                    then(3)
                turned_tile(1)
                count("hid_full", NF + 1)

            def latest(s):
                return slot_used[s], use[s]

            def squares(src, name, t, part):
                if sum_before[name]:
                    act.wait_ge(sem("sum_ready"), sum_before[name])
                nc.scalar.activation(sq_out[:, t, 0:src.shape[-1]] if part is None
                                     else sq_out[:, t, part * BANK:(part + 1) * BANK], src, ACT.Square,
                                     accum_out=st("s_" + name)[:, part or 0:(part or 0) + 1]).then_inc(sem("sum_ready"), 1)

            def acc_squares(name, t, half):
                if half:
                    act.wait_ge(sem("acc_read"), count("acc_read"))
                squares(ps[:, 2 * t + half, :], f"{name}{t}", t, half)

            def h_squares(name, t):
                count("h_new", 2)
                act.wait_ge(sem("h_new"), seen["h_new"])
                squares(h[:, t, :], f"{name}{t}", t, None)

            def flip_high(t, bank, at=0):
                act.wait_ge(sem("flip_full"), count("flip_full"))
                nc.scalar.copy(kthi[:, at:at + 4, t * P:(t + 1) * P], ps[:, bank, :].rearrange("p (c n) -> p c n", c=4)
                               ).then_inc(sem("flip_high"), 1)

            def after_ffn(post, pre, done):
                tile0()
                acc_squares(post, 0, 0)
                acc_squares(post, 0, 1)
                act.wait_ge(*done)
                acc_squares(post, 1, 0)
                flip_high(0, 6)
                acc_squares(post, 1, 1)
                flip_high(0, 7, 4)
                h_squares(pre, 0)
                flip_high(1, 6)
                flip_high(1, 7, 4)
                h_squares(pre, 1)

            def after_rows(post, pre, done, then):
                then(0)
                then(1)
                if not post:
                    count("tile0_done")
                else:
                    tile0()
                    acc_squares(post, 0, 0)
                    acc_squares(post, 0, 1)
                flip_high(0, 6)
                flip_high(0, 7, 4)
                h_squares(pre, 0)
                if post:
                    act.wait_ge(*done)
                    acc_squares(post, 1, 0)
                    acc_squares(post, 1, 1)
                then(2)
                then(3)
                flip_high(1, 6)
                flip_high(1, 7, 4)
                h_squares(pre, 1)

            def wide(pairs, gain, root, func, dst, then, opening, between=None):
                base = list(use)

                def tile(i, par, more, first=False):
                    def evacuate(t):
                        return nc.scalar.activation(dst(t, i * 1024 + par * BANK), ps[:, 4 + 2 * par + t, :], func,
                                                    scale=st(f"r_{root}{t}"))
                    if first:
                        act.wait_ge(*rooted(root + "0"))
                        tile0()
                        evacuate(0)
                    for s in range(3):
                        more(s)
                    if first:
                        act.wait_ge(*rooted(root + "1"))
                    act.wait_ge(slot_used[3], i * 2 + (base[3] + par))
                    for t in range(1 if first else 0, TT):
                        ins = evacuate(t)
                    ins.then_inc(sem("wide_read"), 1)
                    more(3)

                def more(i, par):
                    return lambda s: high(s, i * 2 + (base[s] + par), gain)

                tile(0, 0, more(0, 0), opening)
                tile(0, 1, more(0, 1))
                if between:
                    between()
                if pairs > 2:
                    with act.Fori(1, pairs - 1) as i:
                        for par in range(2):
                            tile(i, par, more(i, par))
                tile(pairs - 1, 0, more(pairs - 1, 0))
                for s in range(4):
                    use[s] += 2 * pairs - 1
                tile(pairs - 1, 1, then)

            for r, n, ap in gain_rows[1:]:
                act.dma_start(grow_late[r - early_rows:r - early_rows + n, :], ap).then_inc(sem("late_in"), 16)
            act.wait_ge(sem("x_in0"), 16)
            squares(h[:, 0, :], "pre_ffn000", 0, None)
            flip_high(0, 6)
            flip_high(0, 7, 4)
            act.wait_ge(sem("gcol_ready"), 1)
            highs([0, 1, 2, 3], "ffn00")
            act.wait_ge(sem("x_in1"), 16)
            squares(h[:, 1, :], "pre_ffn001", 1, None)
            flip_high(1, 6)
            flip_high(1, 7, 4)
            highs([4, 5])
            ffn_first("ffn00", "pre_ffn00")
            act.wait_ge(sem("ang_ready"), 2)
            nc.scalar.activation(rcos[:], turns, ACT.Sin)
            nc.scalar.activation(rsin[:], red, ACT.Sin).then_inc(sem("rope_ready"), 1)
            act.wait_ge(sem("gcol_ready"), 2)
            ffn_rest("ffn00", "pre_ffn00", following("mix0"))
            after_ffn("post_ffn00", "pre_mix0", latest(5))
            def spatial_weights():
                for r in range(GROUPS // 4):
                    act.wait_ge(sem("wst_full"), r + 1)
                    nc.scalar.copy(wst[:, 4 * r:4 * r + 4, :].rearrange("p g t -> p (g t)"), ps[:, r, :]
                                   ).then_inc(sem("wst_ready"), 1)

            wide(4, "mix0", "pre_mix0", ACT.Gelu_apprx_tanh, lambda t, c: vu[:, t, bass.ds(c, BANK)], following(), True,
                 spatial_weights)
            highs([4, 5])
            for r in range(GROUPS // 2):
                act.wait_ge(sem("flip_full"), count("flip_full"))
                nc.scalar.copy(kthi[:, 2 * r:2 * r + 2, :].rearrange("p c n -> p (c n)"), ps[:, 6 + r % 2, :]
                               ).then_inc(sem("flip_high"), 1)
                if r >= 2 and r < 7:
                    highs(W_OUT[2 * r + 2:2 * r + 4])
            done = latest(W_OUT[-1])
            after_rows("post_mix0", "pre_ffn01", done, following("ffn01"))
            highs([4, 5])
            ffn_first("ffn01", "pre_ffn01")
            ffn_rest("ffn01", "pre_ffn01", following("kv", R_KV + ROPE))
            after_ffn("post_ffn01", "pre_kv", latest(5))
            more = following("ffn10")

            def ukv_high(i):
                high(UKV[i], take(UKV[i]), width=UNIT, each=gain_col["kva"] + i % 2)

            def ckv_out(t):
                act.wait_ge(*rooted(f"pre_kv{t}"))
                nc.scalar.activation(ckv[:, t, :], ps[:, 4 + t, 0:R_KV + ROPE], ACT.Copy,
                                     scale=st(f"r_pre_kv{t}")).then_inc(sem("ckv_ready"), 1)

            ckv_done = latest(DKV[-1])
            tile0()
            ckv_out(0)
            for s in range(3):
                more(s)
            act.wait_ge(*ckv_done)
            ckv_out(1)
            more(3)
            ukv_high(0)
            ukv_high(1)
            gate_up_done = latest(3)
            act.wait_ge(sem("flip_full"), count("flip_full"))
            nc.scalar.copy(kthi[:, 8:10, :].rearrange("p c n -> p (c n)"), ps[:, 6, :]).then_inc(sem("flip_high"), 1)
            act.wait_ge(sem("krt_full"), 1)
            nc.scalar.copy(krt, ps[:, 7, 0:S]).then_inc(sem("krt_ready"), 1)
            act.wait_ge(*gate_up_done)
            for t in range(TT):
                gated_tile(t, "pre_kv")
            ukv_high(2)
            more(0)
            ukv_high(3)
            more(1)
            for half in range(2):
                for b in range(2):
                    act.wait_ge(sem("knt_full"), 2 * half + b + 1)
                    nc.scalar.copy(knt[:, 4 * half + 2 * b:4 * half + 2 * b + 2, :].rearrange("p c n -> p (c n)"),
                                   ps[:, 4 + b, :]).then_inc(sem("knt_ready"), 1)
                if half == 0:
                    highs([4, 5])
            more(2)
            more(3)
            ffn_rest("ffn10", "pre_kv", following("mix1"))
            after_ffn("post_ffn10", "pre_mix1", latest(5))

            def uq_high(i):
                high(UQ[i], take(UQ[i]), width=768, each=gain_col["q"] + i % 4)

            def q_out(t):
                act.wait_ge(*rooted(f"pre_mix1{t}"))
                nc.scalar.activation(qlat[:, t, :], ps[:, 4 + t, :], ACT.Copy,
                                     scale=st(f"r_pre_mix1{t}")).then_inc(sem("qlat_ready"), 1)

            def q_squares(t):
                act.wait_ge(sem("qlat_ready"), t + 1)
                squares(qlat[:, t, :], f"q{t}", t, None)

            dq_done = latest(DQ[-1])
            uq_high(0)
            uq_high(1)
            tile0()
            q_out(0)
            q_squares(0)
            uq_high(2)
            uq_high(3)
            act.wait_ge(*dq_done)
            q_out(1)
            flip_high(0, 6)
            flip_high(1, 7)
            q_squares(1)
            uq_high(4)
            uq_high(5)
            def queries_out(half):
                act.wait_ge(slot_used[UQ[4 * half + 3]], q_uses[half])
                for b in range(2):
                    nc.scalar.copy(qnt[:, 4 * half + 2 * b:4 * half + 2 * b + 2, :].rearrange("p c n -> p (c n)"),
                                   ps[:, NOPE_BANK[half][b], :]).then_inc(sem("qnt_ready"), 1)

            q_uses = [use[UQ[3]], use[UQ[7]] + 1]
            queries_out(0)

            def queries_turned(r):
                act.wait_ge(sem("qrt_full"), r + 1)
                nc.scalar.copy(qrt[:, 2 * r:2 * r + 2, :].rearrange("p c n -> p (c n)"), ps[:, 0, :]
                               ).then_inc(sem("qrt_ready"), 1)

            queries_turned(0)
            uq_high(6)
            uq_high(7)

            def exponentials(kind, scale, probs, turned_probs, sums_of, after=None):
                for i in range(H + 1):
                    if i < H:
                        act.wait_ge(sem(kind + "_max_ready"), i + 1)
                        for t in range(TT):
                            blk = probs[:, i % 3, 0:P] if t == 0 else probs[:, i % 3, P:3 * P]
                            ins = nc.scalar.activation(blk, blk, ACT.Exp, bias=st(f"{kind}_nmax{i}", TT)[:, t:t + 1],
                                                       scale=scale, accum_out=sums_of(i, t))
                        ins.then_inc(sem(kind + "_exp_done"), 1)
                    if i >= 1:
                        act.wait_ge(sem(kind + "_pt_full"), i)
                        nc.scalar.copy(turned_probs[:, (i - 1) % 2, :], ps[:, 6, 0:3 * P]
                                       ).then_inc(sem(kind + "_pt_ready"), 1)
                        if after:
                            after(i - 1)

            def outputs_high(i):
                act.wait_ge(sem("flip_full"), count("flip_full"))
                nc.scalar.copy(kthi[:, i:i + 2, :].rearrange("p c n -> p (c n)"), ps[:, 7, :]
                               ).then_inc(sem("flip_high"), 1)

            def between_heads(i):
                if i == 1:
                    queries_out(1)
                    queries_turned(1)
                if i in (2, 3, 4):
                    highs(WO[2 * i - 4:2 * i - 2])
                if i in (2, 4, 6):
                    outputs_high(i - 2)
                if i == H - 1:
                    highs(WO[6:8])

            exponentials("mla", MLA_SCALE, p_sb, pt_sb, lambda i, t: st(f"mla_sum{i % 2}", TT)[:, t:t + 1], between_heads)
            outputs_high(H - 2)
            done = latest(WO[-1])
            after_rows("post_mix1", "pre_ffn11", done, following("ffn11"))
            highs([4, 5])
            ffn_first("ffn11", "pre_ffn11")
            ffn_rest("ffn11", "pre_ffn11", following("mix2"))
            after_ffn("post_ffn11", "pre_mix2", latest(5))
            act.wait_ge(sem("f_gained"), 1)
            highs([4], width=64)
            f_done = latest(4)
            wide(3, "mix2", "pre_mix2", ACT.Copy, lambda t, c: z[:, t, bass.ds(c, BANK)], following("mix2"), True)
            act.wait_ge(*f_done)
            for t in range(TT):
                ins = nc.scalar.activation(z[:, t, Z_F:Z_F + 8], ps[:, t, 0:8], ACT.Copy, scale=st(f"r_pre_mix2{t}"))
            ins.then_inc(sem("f_ready"), 1)
            act.wait_ge(sem("logf_x"), 1)
            nc.scalar.activation(logf[:, 1, :], logf[:, 1, :], ACT.Exp, scale=-1.0).then_inc(sem("logf_e"), 1)
            act.wait_ge(sem("logf_e"), 1)
            nc.scalar.activation(logf[:, 1, :], logf[:, 1, :], ACT.Ln, bias=1.0).then_inc(sem("logf_l"), 1)
            wide(2, "mix2", "pre_mix2", ACT.Sigmoid, lambda t, c: z[:, t, bass.ds(c + Z_AR, BANK)], following(), False)
            for r in range(2):
                act.wait_ge(sem("rqk_full"), r + 1)
                nc.scalar.copy(turned[:, 2 * r:2 * r + 2, :].rearrange("p c n -> p (c n)"), ps[:, 6 + r, :]
                               ).then_inc(sem("rqk_ready"), 1)
            act.wait_ge(sem("wide_read"), 20)
            for t in range(TT):
                ins = nc.scalar.activation(z[:, t, Z_GT:Z_GT + 512], z[:, t, Z_GT:Z_GT + 512], ACT.Silu)
            ins.then_inc(sem("gate_ready"), 1)
            highs(RET_O[0:2])
            for r in range(4):
                act.wait_ge(sem("fqk_full"), r + 1)
                nc.scalar.copy(turned[:, 2 * r:2 * r + 2, :].rearrange("p c n -> p (c n)"), ps[:, 4 + r, :]
                               ).then_inc(sem("fqk_ready"), 1)
            flip_high(0, 6)
            flip_high(1, 7)

            def between_heads(i):
                if i == 4:
                    highs(FOX_O[2:4])

            exponentials("fox", 1.0, p2_sb, pt2_sb, lambda i, t: st("fox_sums", TT * H)[:, t * H + i:t * H + i + 1],
                         between_heads)
            flip_high(0, 6)
            flip_high(1, 7)
            highs(OUT2[0:4])
            count("tile0_done")
            flip_high(0, 4)
            flip_high(0, 5, 4)
            flip_high(1, 6)
            flip_high(1, 7, 4)
            highs(OUT2[4:6])
            highs(OUT2[6:8])
            after_rows(None, "pre_ffn2", None, following("ffn2"))
            highs([4, 5])
            ffn_first("ffn2", "pre_ffn2")
            ffn_rest("ffn2", "pre_ffn2")

        @block.vector
        def _(dve):
            use = [0] * SLOTS
            seen = {}
            own = [0]

            def count(name, by=1):
                seen[name] = seen.get(name, 0) + by
                return seen[name]

            def mark(ins):
                own[0] += 1
                ins.then_inc(sem("dve_own"), 1)

            def settle():
                dve.wait_ge(sem("dve_own"), own[0])

            def f32(x):
                return x.bitcast(F32)

            def low(s, n, gain=None, width=None, each=None):
                dve.wait_ge(hi_done[s], n + 1)
                if gain is not None:
                    for c in range(2):
                        cut, k = slice(c * BANK, c * BANK + (width or BANK)), gain_col[gain] + 2 * s + c
                        ins = nc.vector.scalar_tensor_tensor(out=wlo[:, s, cut], in0=raw[:, s, cut], scalar=gcol[:, k:k + 1],
                                                             in1=f32(whi[:, s, cut]), op0=ALU.mult, op1=ALU.subtract)
                elif each is not None:
                    ins = nc.vector.scalar_tensor_tensor(out=wlo[:, s, 0:width], in0=raw[:, s, 0:width],
                                                         scalar=gcol[:, each:each + 1], in1=f32(whi[:, s, 0:width]),
                                                         op0=ALU.mult, op1=ALU.subtract)
                else:
                    w = slice(0, width or UNIT)
                    ins = nc.vector.tensor_tensor(wlo[:, s, w], raw[:, s, w], f32(whi[:, s, w]), ALU.subtract)
                ins.then_inc(lo_done[s], 1)

            def take(s):
                use[s] += 1
                return use[s] - 1

            def lows(slots, gain=None, width=None):
                for s in slots:
                    low(s, take(s), gain, width)

            def following(gain=None, width=None):
                return lambda s: low(s, take(s), gain, width)

            def gated_tile(t, pre, n):
                dve.wait_ge(sem("silu_done"), n)
                nc.vector.scalar_tensor_tensor(out=hid[:, t, :], in0=ps[:, 4 + t, FT:2 * FT], scalar=st(f"r_{pre}{t}"),
                                               in1=hid[:, t, :], op0=ALU.mult, op1=ALU.mult
                                               ).then_inc(sem("hid_ready"), 1)

            def ffn_first(name, pre):
                more = following(name)
                count("tile0_done")
                gated_tile(0, pre, count("silu_done"))
                for s in range(3):
                    more(s)
                gated_tile(1, pre, count("silu_done"))
                more(3)

            def ffn_rest(name, pre, then=None):
                base, b, b_ht = [n - 1 for n in use], seen["silu_done"] - 2, seen.get("ht_high", 0)

                def turned_hidden(j):
                    dve.wait_ge(sem("ht_high"), j + (b_ht + 1))
                    nc.vector.tensor_tensor(htlo[:].rearrange("p c n -> p (c n)"), ps[:, 6, :],
                                            f32(hthi[:]).rearrange("p c n -> p (c n)"), ALU.subtract
                                            ).then_inc(sem("ht_low"), 1)

                def turned_tile(t):
                    dve.wait_ge(sem("ht_high"), b_ht + NF + t)
                    cut = slice(t * P, (t + 1) * P)
                    nc.vector.tensor_tensor(htlo[:, :, cut], ps[:, 6 + t, 0:2 * P].rearrange("p (c n) -> p c n", c=2),
                                            f32(hthi[:, :, cut]), ALU.subtract).then_inc(sem("ht_low"), 1)

                turned_hidden(0)
                with dve.Fori(1, NF - 1) as j:
                    for s in range(3):
                        low(s, j + base[s], name)
                    for t in range(TT):
                        gated_tile(t, pre, j * 2 + (b + t + 1))
                    low(3, j + base[3], name)
                    for s in (4, 5):
                        low(s, j + base[s])
                    turned_hidden(j)
                for s in range(SLOTS):
                    use[s] += NF - 2
                count("silu_done", 2 * (NF - 2))
                count("tile0_done")
                gated_tile(0, pre, count("silu_done"))
                lows([4])
                turned_tile(0)
                lows([5])
                if then:
                    for s in range(3):
                        then(s)
                gated_tile(1, pre, count("silu_done"))
                if then:
                    then(3)
                turned_tile(1)
                count("ht_high", NF + 1)

            def acc(t):
                return ps[:, 2 * t:2 * t + 2, :].rearrange("p a b -> p (a b)")

            def latest(s):
                return slot_used[s], use[s]

            def acc_gained(k, t, half):
                if t == 0 and half == 1:
                    dve.wait_ge(sem(f"gpost_in{k % 2}"), 16 * (k // 2 + 1))
                cut = slice(half * BANK, (half + 1) * BANK)
                ins = nc.vector.tensor_tensor(fg[:, t, cut], ps[:, 2 * t + half, :], gpost[:, k % 2, cut], ALU.mult)
                if half:
                    ins.then_inc(sem("acc_read"), 1)
                else:
                    mark(ins)

            def renew(name, t):
                dve.wait_ge(*rooted(f"{name}{t}"))
                dve.wait_ge(sem("acc_read"), count("acc_read"))
                settle()
                for half in range(2):
                    cut = slice(half * BANK, (half + 1) * BANK)
                    nc.vector.scalar_tensor_tensor(out=h[:, t, cut], in0=fg[:, t, cut], scalar=st(f"r_{name}{t}"),
                                                   in1=h[:, t, cut], op0=ALU.mult, op1=ALU.add).then_inc(sem("h_new"), 1)

            def tile0():
                dve.wait_ge(sem("tile0_done"), count("tile0_done"))

            def flip_low(t, bank, at=0):
                dve.wait_ge(sem("flip_high"), count("flip_high"))
                cut = slice(t * P, (t + 1) * P)
                nc.vector.tensor_tensor(ktlo[:, at:at + 4, cut], ps[:, bank, :].rearrange("p (c n) -> p c n", c=4),
                                        f32(kthi[:, at:at + 4, cut]), ALU.subtract).then_inc(sem("kt_ready"), 1)

            def flip_low_pair(c, bank):
                dve.wait_ge(sem("flip_high"), count("flip_high"))
                nc.vector.tensor_tensor(ktlo[:, c:c + 2, :].rearrange("p c n -> p (c n)"), ps[:, bank, :],
                                        f32(kthi[:, c:c + 2, :]).rearrange("p c n -> p (c n)"), ALU.subtract
                                        ).then_inc(sem("kt_ready"), 1)

            def after_ffn(post, k, done):
                tile0()
                acc_gained(k, 0, 1)
                dve.wait_ge(*sums(post + "0", 1))
                acc_gained(k, 0, 0)
                renew(post, 0)
                dve.wait_ge(*done)
                acc_gained(k, 1, 1)
                flip_low(0, 6)
                dve.wait_ge(*sums(post + "1", 1))
                acc_gained(k, 1, 0)
                flip_low(0, 7, 4)
                renew(post, 1)
                flip_low(1, 6)
                flip_low(1, 7, 4)

            def after_rows(post, k, done, then):
                def renewed(t):
                    if post:
                        renew(post, t)
                    else:
                        for half in range(2):
                            cut = slice(half * BANK, (half + 1) * BANK)
                            nc.vector.tensor_tensor(h[:, t, cut], ps[:, 2 * t + half, :], h[:, t, cut], ALU.add
                                                    ).then_inc(sem("h_new"), 1)
                then(0)
                then(1)
                tile0()
                if post:
                    acc_gained(k, 0, 1)
                    dve.wait_ge(*sums(post + "0", 1))
                    acc_gained(k, 0, 0)
                renewed(0)
                flip_low(0, 6)
                flip_low(0, 7, 4)
                dve.wait_ge(*done)
                if post:
                    acc_gained(k, 1, 1)
                    dve.wait_ge(*sums(post + "1", 1))
                    acc_gained(k, 1, 0)
                then(2)
                renewed(1)
                then(3)
                flip_low(1, 6)
                flip_low(1, 7, 4)

            def wide(pairs, gain, then):
                base = list(use)
                with dve.Fori(0, pairs - 1) as i:
                    for par in range(2):
                        for s in range(4):
                            low(s, i * 2 + (base[s] + par), gain)
                for s in range(4):
                    use[s] += 2 * pairs - 2
                for s in range(4):
                    low(s, take(s), gain)
                for s in range(4):
                    then(s)

            def over_heads(x, heads):
                return x.unsqueeze(1).to_broadcast([P, heads, RH])

            def rotate(dst, x, cos, sin, heads, tmp):
                x1, x2 = x[:, :, 0:RH], x[:, :, RH:2 * RH]
                c, s = over_heads(cos, heads), over_heads(sin, heads)
                t0 = tmp[:, 0, 0:heads * RH].rearrange("p (h r) -> p h r", h=heads)
                t1 = tmp[:, 1, 0:heads * RH].rearrange("p (h r) -> p h r", h=heads)
                settle()
                mark(nc.vector.tensor_tensor(t0, x1, c, ALU.mult))
                mark(nc.vector.tensor_tensor(t1, x2, s, ALU.mult))
                settle()
                mark(nc.vector.tensor_tensor(dst[:, :, 0:RH], t0, t1, ALU.subtract))
                settle()
                mark(nc.vector.tensor_tensor(t0, x2, c, ALU.mult))
                mark(nc.vector.tensor_tensor(t1, x1, s, ALU.mult))
                settle()
                mark(nc.vector.tensor_tensor(dst[:, :, RH:2 * RH], t0, t1, ALU.add))

            for pair in range(2):
                nc.vector.memset(st(f"free{pair}"), 0.0).then_inc(sem("wide_read"), 1)
            dve.wait_ge(sem("gcol_full"), 1)
            nc.vector.tensor_copy(gcol[:, 0:early_rows], ps[:, 5, 0:early_rows]).then_inc(sem("gcol_ready"), 1)
            dve.wait_ge(sem("pos_in"), 32)
            mark(nc.vector.tensor_copy(posf, pos_i[:]))
            settle()
            for t in range(TT):
                mark(nc.vector.tensor_scalar(ang[:, t, :], freq, posf[:, t:t + 1], None, ALU.mult))
            settle()
            for quarter, dst in ((0.25, turns), (0.0, red)):
                mark(nc.vector.tensor_scalar(whole, ang, 1.0 / (2.0 * math.pi), quarter, ALU.mult, ALU.add))
                settle()
                mark(nc.vector.tensor_scalar(whole, whole, ROUND, -ROUND, ALU.add, ALU.add))
                settle()
                src = ang
                for part in TWO_PI:
                    for t in range(TT):
                        mark(nc.vector.scalar_tensor_tensor(out=dst[:, t, :], in0=whole[:, t, :], scalar=-part,
                                                            in1=src[:, t, :], op0=ALU.mult, op1=ALU.add))
                    settle()
                    src = dst
                mark(nc.vector.tensor_scalar(dst, dst, quarter * 2.0 * math.pi, PI_DOWN, ALU.add, ALU.min))
                settle()
                nc.vector.tensor_scalar(dst, dst, -PI_DOWN, None, ALU.max).then_inc(sem("ang_ready"), 1)
            flip_low(0, 6)
            flip_low(0, 7, 4)
            lows([0, 1, 2, 3], "ffn00")
            flip_low(1, 6)
            flip_low(1, 7, 4)
            lows([4, 5])
            ffn_first("ffn00", "pre_ffn00")
            dve.wait_ge(sem("gcol_full"), 2)
            nc.vector.tensor_copy(gcol[:, early_rows:row], ps[:, 7, 0:row - early_rows]).then_inc(sem("gcol_ready"), 1)
            ffn_rest("ffn00", "pre_ffn00", following("mix0"))
            after_ffn("post_ffn00", 0, latest(5))
            count("tile0_done")
            mv = st("mv", 16).rearrange("p (k two) -> p k two", two=2)
            V_TILES = HALF // BANK
            for k in range(2 * V_TILES):
                if k + 1 < 2 * V_TILES:
                    lows([0, 1, 2, 3], "mix0")
                else:
                    lows([0, 1, 2, 3])
                if k < V_TILES:
                    dve.wait_ge(sem("wide_read"), 2 + k + 1)
                    for t in range(TT):
                        mark(nc.vector.bn_stats(st("bn", 48)[:, (4 * t + k) * 6:(4 * t + k) * 6 + 6],
                                                v_sb[:, t, k * BANK:(k + 1) * BANK]))
                if k == V_TILES - 1:
                    settle()
                    for t in range(TT):
                        mark(nc.vector.bn_aggr(st("mv", 16)[:, 2 * t:2 * t + 2], st("bn", 48)[:, 24 * t:24 * t + 24]))
                    settle()
                    nc.vector.tensor_copy(st("s_ln"), mv[:, 0:TT, 1]).then_inc(sem("sum_ready"), 1)
                    dve.wait_ge(*rooted("ln"))
                if V_TILES <= k < V_TILES + TT:
                    t = k - V_TILES
                    nc.vector.tensor_scalar(v_sb[:, t, :], v_sb[:, t, :], mv[:, t, 0:1], st("r_ln")[:, t:t + 1],
                                            ALU.subtract, ALU.mult).then_inc(sem("v_normed"), 1)
            def mix(r):
                dve.wait_ge(sem("spatial_full"), r + 1)
                for g in (2 * r, 2 * r + 1):
                    k = gain_col["bs"] + g
                    ug = u_sb[:, :, g * GD:(g + 1) * GD]
                    ins = nc.vector.scalar_tensor_tensor(
                        out=ug, in0=ps[:, 4 + r % 2, (g % 2) * S:(g % 2) * S + S].rearrange("p (n d) -> p n d", n=TT),
                        scalar=gcol[:, k:k + 1], in1=ug, op0=ALU.add, op1=ALU.mult)
                ins.then_inc(sem("mixed"), 1)

            dve.wait_ge(sem("wide_read"), 2 + 8)
            mix(0)
            for r in range(GROUPS // 2):
                if r + 1 < GROUPS // 2:
                    mix(r + 1)
                flip_low_pair(2 * r, 6 + r % 2)
                if r == 0:
                    lows([4, 5])
                if r >= 2 and r < 7:
                    lows(W_OUT[2 * r + 2:2 * r + 4])
            done = latest(W_OUT[-1])
            after_rows("post_mix0", 1, done, following("ffn01"))
            lows([4, 5])
            ffn_first("ffn01", "pre_ffn01")
            ffn_rest("ffn01", "pre_ffn01", following("kv", R_KV + ROPE))
            after_ffn("post_ffn01", 2, latest(5))
            more = following("ffn10")

            def ukv_low(i):
                low(UKV[i], take(UKV[i]), width=UNIT, each=gain_col["kva"] + i % 2)

            count("tile0_done")
            for s in range(3):
                more(s)
            dve.wait_ge(sem("ckv_ready"), TT)
            for t in range(TT):
                ins = nc.vector.tensor_tensor_reduce(out=fg[:, t, 0:R_KV], in0=ckv[:, t, 0:R_KV], in1=ckv[:, t, 0:R_KV],
                                                     scale=1.0, scalar=0.0, op0=ALU.mult, op1=ALU.add,
                                                     accum_out=st("s_kva")[:, t:t + 1])
            ins.then_inc(sem("sum_ready"), 1)
            more(3)
            dve.wait_ge(sem("rope_ready"), 1)
            for t in range(TT):
                rotate(krope2[:, t, 0:1, :], ckv[:, t:t + 1, R_KV:R_KV + ROPE], rcos[:, t, :], rsin[:, t, :], 1, rope_t)
            settle()
            nc.vector.tensor_copy(krope2[:, :, 1, :], krope2[:, :, 0, :]).then_inc(sem("krope_ready"), 1)
            dve.wait_ge(*rooted("kva"))
            for t in range(TT):
                ins = nc.vector.tensor_scalar(ckv[:, t, 0:R_KV], ckv[:, t, 0:R_KV], st("r_kva")[:, t:t + 1], None, ALU.mult)
            ins.then_inc(sem("ckv_normed"), 1)
            ukv_low(0)
            ukv_low(1)
            flip_low_pair(8, 6)
            v_done = [latest(UKV[1])]
            for t in range(TT):
                gated_tile(t, "pre_kv", count("silu_done"))
            ukv_low(2)
            more(0)
            ukv_low(3)
            more(1)
            v_done.append(latest(UKV[3]))
            for half in range(2):
                dve.wait_ge(*v_done[half])
                nc.vector.tensor_copy(v_mla[:, :, half * 512:(half + 1) * 512], ps[:, 6:8, :]).then_inc(sem("v_read"), 1)
                if half == 0:
                    lows([4, 5])
            more(2)
            more(3)
            ffn_rest("ffn10", "pre_kv", following("mix1"))
            after_ffn("post_ffn10", 3, latest(5))

            def uq_low(i):
                low(UQ[i], take(UQ[i]), width=768, each=gain_col["q"] + i % 4)

            uq_low(0)
            uq_low(1)
            count("tile0_done")
            uq_low(2)
            uq_low(3)
            flip_low(0, 6)
            flip_low(1, 7)
            uq_low(4)
            uq_low(5)

            def rotate_queries(half):
                dve.wait_ge(sem("qrope_full"), half + 1)
                for t in range(TT):
                    rotate(qrope[:, t, 4 * half:4 * half + 4, :],
                           ps[:, ROPE_BANK[half], t * 256:t * 256 + 256].rearrange("p (h r) -> p h r", h=4),
                           rcos[:, t, :], rsin[:, t, :], 4, rope_t)
                settle()
                nc.vector.memset(st(f"rotated{half}"), 0.0).then_inc(sem("qrope_ready"), 1)

            rotate_queries(0)
            uq_low(6)
            uq_low(7)

            def softmax(kind, scale, probs, add_mask, after, normalise=True):
                def masked(i):
                    dve.wait_ge(sem(kind + "_scores_full"), i + 1)
                    if i >= 3:
                        dve.wait_ge(sem(kind + "_pt_full"), i - 2)
                    add_mask(i, probs[:, i % 3, :]).then_inc(sem(kind + "_masked"), 1)
                    dve.wait_ge(sem(kind + "_masked"), i + 1)
                    mx = st(f"{kind}_mx{i % 2}", TT)
                    mark(nc.vector.tensor_reduce(mx[:, 0:1], probs[:, i % 3, 0:P], AX_X, ALU.max))
                    mark(nc.vector.tensor_reduce(mx[:, 1:2], probs[:, i % 3, P:3 * P], AX_X, ALU.max))
                    settle()
                    nc.vector.tensor_scalar(st(f"{kind}_nmax{i}", TT), mx, -scale, None, ALU.mult
                                            ).then_inc(sem(kind + "_max_ready"), 1)

                def normed(i):
                    dve.wait_ge(sem(kind + "_exp_done"), i + 1)
                    rcp = st(f"{kind}_rcp{i % 2}", TT)
                    mark(nc.vector.reciprocal(rcp, st(f"{kind}_sum{i % 2}", TT)))
                    settle()
                    nc.vector.tensor_scalar(probs[:, i % 3, 0:P], probs[:, i % 3, 0:P], rcp[:, 0:1], None, ALU.mult)
                    nc.vector.tensor_scalar(probs[:, i % 3, P:3 * P], probs[:, i % 3, P:3 * P], rcp[:, 1:2], None,
                                            ALU.mult).then_inc(sem(kind + "_p_ready"), 1)

                masked(0)
                for i in range(H):
                    if i + 1 < H:
                        masked(i + 1)
                    if normalise:
                        normed(i)
                    if i >= 1:
                        after(i - 1)
                after(H - 1)

            def between_heads(i):
                if i == 0:
                    rotate_queries(1)
                if i in (2, 4, 6):
                    flip_low_pair(i - 2, 7)
                if i in (2, 3, 4):
                    lows(WO[2 * i - 4:2 * i - 2])
                if i == H - 1:
                    lows(WO[6:8])

            dve.wait_ge(sem("mask_in"), 16)
            dve.wait_ge(*rooted("q0"))
            dve.wait_ge(*rooted("q1"))

            def mla_mask(i, dst):
                nc.vector.scalar_tensor_tensor(out=dst[:, 0:P], in0=ps[:, 4 + i % 2, 0:P], scalar=st("r_q0"),
                                               in1=mask[:, 0:P], op0=ALU.mult, op1=ALU.add)
                return nc.vector.scalar_tensor_tensor(out=dst[:, P:3 * P], in0=ps[:, 4 + i % 2, P:3 * P],
                                                      scalar=st("r_q1"), in1=mask[:, P:3 * P],
                                                      op0=ALU.mult, op1=ALU.add)

            softmax("mla", MLA_SCALE, p_sb, mla_mask, between_heads)
            flip_low_pair(H - 2, 7)
            done = latest(WO[-1])
            after_rows("post_mix1", 4, done, following("ffn11"))
            lows([4, 5])
            ffn_first("ffn11", "pre_ffn11")
            ffn_rest("ffn11", "pre_ffn11", following("mix2"))
            after_ffn("post_ffn11", 5, latest(5))
            s = 4
            dve.wait_ge(raw_in[s], 32 * use[s] + 32)
            f_raw = raw[:, s, 0:8 * KC].rearrange("p (c n) -> p c n", c=KC)
            k = gain_col["mix2"]
            nc.vector.tensor_tensor(f_raw, f_raw, gcol[:, k:k + KC].unsqueeze(2).to_broadcast([P, KC, 8]), ALU.mult
                                    ).then_inc(sem("f_gained"), 1)
            lows([4], width=64)
            count("tile0_done")
            wide(3, "mix2", following("mix2"))
            dve.wait_ge(sem("f_ready"), 1)
            dve.wait_ge(sem("bfor_in"), 16)
            for t in range(TT):
                mark(nc.vector.tensor_tensor(logf[:, 0, 8 * t:8 * t + 8], z[:, t, Z_F:Z_F + 8], bfor[:], ALU.add))
            settle()
            nc.vector.scalar_tensor_tensor(out=logf[:, 1, :], in0=logf[:, 0, :], scalar=-1.0, in1=logf[:, 0, :],
                                           op0=ALU.mult, op1=ALU.max).then_inc(sem("logf_x"), 1)
            mark(nc.vector.tensor_scalar(logf[:, 2, :], logf[:, 0, :], 0.0, None, ALU.min))
            settle()
            for k in range(4):
                if k < 3:
                    lows([0, 1, 2, 3], "mix2")
                else:
                    settle()
                    nc.vector.memset(st("rotated2"), 0.0).then_inc(sem("r_rotated"), 1)
                    lows([0, 1, 2, 3])
                if k == 0:
                    dve.wait_ge(sem("wide_read"), 2 + 8 + 6)
                    dve.wait_ge(sem("rope2_in"), 32)
                    for t in range(TT):
                        rotate(ro_t[:, t, :].rearrange("p (h r) -> p h r", h=8),
                               z[:, t, 0:512].rearrange("p (h r) -> p h r", h=8), cos2[:, t, :], sin2[:, t, :], 8, st_sb)
                if k == 1:
                    squares = turned.rearrange("p a b -> p (a b)").rearrange("p (t n) -> p t n", t=TT)
                    mark(nc.vector.tensor_tensor(squares, z[:, :, Z_QF:Z_QF + 1024], z[:, :, Z_QF:Z_QF + 1024], ALU.mult))
                    settle()
                    for qk, name in enumerate(("foxq", "foxk")):
                        nc.vector.tensor_reduce(st("s_" + name).rearrange("p (t h) -> p t h", t=TT),
                                                squares[:, :, qk * 512:qk * 512 + 512].rearrange("p t (h r) -> p t h r", h=H),
                                                AX_X, ALU.add).then_inc(sem("sum_ready"), 1)
                    dve.wait_ge(sem("logf_l"), 1)
                    nc.vector.tensor_tensor(logf[:, 0, :], logf[:, 2, :], logf[:, 1, :], ALU.subtract
                                            ).then_inc(sem("logf_ready"), 1)
                if k == 2:
                    for qk, name in enumerate(("foxq", "foxk")):
                        dve.wait_ge(*rooted(name))
                        for t in range(TT):
                            zh = z[:, t, Z_QF + qk * 512:Z_QF + qk * 512 + 512].rearrange("p (h r) -> p h r", h=H)
                            mark(nc.vector.tensor_tensor(zh, zh, st("r_" + name)[:, 8 * t:8 * t + 8].unsqueeze(2)
                                                         .to_broadcast([P, H, 64]), ALU.mult))
            yr_done = slot_used[RET_O[3]], use[RET_O[3]]
            dve.wait_ge(sem("cum_full"), 1)
            nc.vector.tensor_copy(cum.rearrange("p t h -> p (t h)"), ps[:, 2, 0:16]).then_inc(sem("cum_ready"), 1)
            dve.wait_ge(sem("cumt_full"), 1)
            nc.vector.tensor_scalar(ncumt, ps[0:8, 3, 0:S], -1.0, None, ALU.mult).then_inc(sem("ncumt_ready"), 1)
            dve.wait_ge(sem("gfox_in"), 16 * 2 * H)
            for t in range(TT):
                zz = z[:, t, Z_QF:Z_QF + 1024]
                ins = nc.vector.tensor_tensor(zz, zz, gfox[:, 0, :], ALU.mult)
            ins.then_inc(sem("fqk_normed"), 1)
            dve.wait_ge(sem("decay_in"), 16)
            for i in range(HR):
                dve.wait_ge(sem("rst_full"), i + 1)
                if i >= 2:
                    dve.wait_ge(sem("rpv_done"), i - 1)
                nc.vector.tensor_tensor(st_sb[:, i % 2, :], ps[:, 4 + i % 2, 0:3 * P], decay[:, i, :], ALU.mult
                                        ).then_inc(sem("rst_ready"), 1)
                if i < 2:
                    lows(RET_O[i:i + 1])
            dve.wait_ge(sem("gret_in"), 16)
            dve.wait_ge(sem("gate_ready"), 1)
            for t in range(TT):
                gate = z[:, t, Z_GT:Z_GT + 512]
                mark(nc.vector.tensor_tensor(gate, gate, gpost[:, 1, 0:512], ALU.mult))
            dve.wait_ge(sem("rpv_done"), HR)
            for k in range(TT * HR):
                t, i = divmod(k, HR)
                mark(nc.vector.bn_stats(st("bn", 48)[:, 6 * k:6 * k + 6], ps[:, t, i * P:(i + 1) * P]))
            settle()
            for k in range(TT * HR):
                mark(nc.vector.bn_aggr(st("mv", 16)[:, 2 * k:2 * k + 2], st("bn", 48)[:, 6 * k:6 * k + 6]))
            settle()
            nc.vector.tensor_copy(st("s_ret"), mv[:, :, 1]).then_inc(sem("sum_ready"), 1)
            for k in range(TT * HR):
                t, i = divmod(k, HR)
                mark(nc.vector.scalar_tensor_tensor(out=ro_t[:, t, i * P:(i + 1) * P], in0=ps[:, t, i * P:(i + 1) * P],
                                                    scalar=mv[:, k, 0:1], in1=z[:, t, Z_GT + i * P:Z_GT + (i + 1) * P],
                                                    op0=ALU.subtract, op1=ALU.mult))
            dve.wait_ge(*rooted("ret"))
            settle()
            for t in range(TT):
                rt = ro_t[:, t, :].rearrange("p (h n) -> p h n", h=HR)
                nc.vector.tensor_tensor(rt, rt, st("r_ret")[:, HR * t:HR * (t + 1)].unsqueeze(2).to_broadcast([P, HR, P]),
                                        ALU.mult).then_inc(sem("ro_ready"), 1)
            flip_low(0, 6)
            flip_low(1, 7)
            yf_done = [None]

            def fox_mask(i, dst):
                nc.vector.scalar_tensor_tensor(out=dst[:, 0:P], in0=ps[:, 4 + i % 2, 0:P], scalar=cum[:, 0, i:i + 1],
                                               in1=mask[:, 0:P], op0=ALU.add, op1=ALU.add)
                return nc.vector.scalar_tensor_tensor(out=dst[:, P:3 * P], in0=ps[:, 4 + i % 2, P:3 * P],
                                                      scalar=cum[:, 1, i:i + 1], in1=mask[:, P:3 * P],
                                                      op0=ALU.add, op1=ALU.add)

            dve.wait_ge(sem("cum_ready"), 1)

            def fox_out(half):
                dve.wait_ge(sem("fpv_full"), half + 1)
                for t in range(TT):
                    k = t * H + half * 4
                    rcp = st("fox_rcp", TT * H)[:, k:k + 4]
                    mark(nc.vector.reciprocal(rcp, st("fox_sums", TT * H)[:, k:k + 4]))
                    settle()
                    nc.vector.tensor_tensor(
                        z[:, t, Z_QF + half * S:Z_QF + (half + 1) * S].rearrange("p (h d) -> p h d", h=4),
                        ps[:, 7, t * S:(t + 1) * S].rearrange("p (h d) -> p h d", h=4),
                        rcp.unsqueeze(2).to_broadcast([P, 4, 64]), ALU.mult).then_inc(sem("fo_ready"), 1)

            def between_heads(i):
                if i == 5:
                    fox_out(0)
                    lows(FOX_O[2:4])
                    yf_done[0] = latest(FOX_O[3])
                if i == 6:
                    dve.wait_ge(*yr_done)
                    for t in range(TT):
                        ins = nc.vector.tensor_tensor(fg[:, t, :], acc(t), z[:, t, Z_AR:Z_AR + D], ALU.mult)
                    ins.then_inc(sem("yr_read"), 1)

            softmax("fox", 1.0, p2_sb, fox_mask, between_heads, normalise=False)
            fox_out(1)
            flip_low(0, 6)
            flip_low(1, 7)
            lows(OUT2[0:2])
            for t in range(TT):
                zf = z[:, t, Z_AF:Z_AF + D]
                if t == 0:
                    tile0()
                    dve.wait_ge(sem("yr_read"), 1)
                else:
                    dve.wait_ge(*yf_done[0])
                mark(nc.vector.tensor_tensor(zf, acc(t), zf, ALU.mult))
                settle()
                nc.vector.tensor_tensor(fg[:, t, :], fg[:, t, :], zf, ALU.add).then_inc(sem("merged"), 1)
                if t == 0:
                    lows(OUT2[2:4])
                    flip_low(0, 4)
                    flip_low(0, 5, 4)
            flip_low(1, 6)
            flip_low(1, 7, 4)
            lows(OUT2[4:6])
            lows(OUT2[6:8])
            done = latest(OUT2[7])
            after_rows(None, None, done, following("ffn2"))
            lows([4, 5])
            ffn_first("ffn2", "pre_ffn2")
            ffn_rest("ffn2", "pre_ffn2")
            for t, done in enumerate(((sem("tile0_done"), count("tile0_done")), latest(5))):
                dve.wait_ge(*done)
                for half in range(2):
                    cut = slice(half * BANK, (half + 1) * BANK)
                    nc.vector.tensor_tensor(h[:, t, cut], ps[:, 2 * t + half, :], h[:, t, cut], ALU.add
                                            ).then_inc(sem("h_new"), 1)

        @block.tensor
        def _(pe):
            use = [0] * SLOTS
            seen = {}

            def count(name, by=1):
                seen[name] = seen.get(name, 0) + by
                return seen[name]

            def product(dst, lhs, rhs, first, last):
                nc.tensor.matmul(dst, lhs[0], rhs[0], start=first, stop=False)
                nc.tensor.matmul(dst, lhs[0], rhs[1], start=False, stop=False)
                return nc.tensor.matmul(dst, lhs[1], rhs[0], start=False, stop=last)

            def kt(c, t=None):
                cut = slice(0, S) if t is None else slice(t * P, t * P + P)
                return kthi[:, c, cut], ktlo[:, c, cut]

            def ht(c, t):
                return hthi[:, c, t * P:t * P + P], htlo[:, c, t * P:t * P + P]

            def slot(s, cut):
                return cut(whi[:, s, :]), cut(wlo[:, s, :])

            def made(s, n):
                pe.wait_ge(lo_done[s], n + 1)

            def take(s):
                use[s] += 1
                return use[s] - 1

            def turn(bank, src, chunks=4):
                for c in range(chunks):
                    ins = nc.tensor.transpose(ps[:, bank, c * P:(c + 1) * P], src(c), ident[:])
                return ins

            def flip(t, src, banks=(6, 7), ready=None):
                for b, bank in enumerate(banks):
                    if ready:
                        ready(b)
                    turn(bank, lambda c: src(4 * b + c, t)).then_inc(sem("flip_full"), 1)
                    count("kt_ready")

            def flip_h(k, t):
                def renewed(b):
                    if k:
                        pe.wait_ge(sem("h_new"), 4 * (k - 1) + 2 * t + b + 1)
                    elif b == 0:
                        pe.wait_ge(sem(f"x_in{t}"), 16)
                flip(t, lambda c, t: h[:, t, c * P:(c + 1) * P], ready=renewed)

            def tile_product(n_of, bank=4):
                for s in range(4):
                    made(s, n_of(s))
                    for c in range(2):
                        k = 2 * s + c
                        for t in range(TT):
                            rhs = slot(s, lambda x: x[:, c * BANK:(c + 1) * BANK])
                            ins = product(ps[:, bank + t, :], kt(k, t), rhs, k == 0, k == KC - 1)
                    ins.then_inc(slot_used[s], 1)

            def opening(k, n_of, width=BANK):
                base = seen["kt_ready"] - 2
                for t in range(TT):
                    for s in range(4):
                        made(s, n_of(s))
                        if s % 2 == 0:
                            pe.wait_ge(sem("kt_ready"), base + 2 * t + s // 2 + 1)
                        if t == 0 and s == 2:
                            flip_h(k, 1)
                        for c in range(2):
                            kc = 2 * s + c
                            rhs = slot(s, lambda x: x[:, c * BANK:c * BANK + width])
                            ins = product(ps[:, 4 + t, 0:width], kt(kc, t), rhs, kc == 0, kc == KC - 1)
                        if t:
                            ins.then_inc(slot_used[s], 1)
                    if t == 0:
                        ins.then_inc(sem("tile0_done"), 1)

            def row_chunk(s, c, t, first, last):
                for half in range(2):
                    rhs = slot(s, lambda x: x[:, half * BANK:(half + 1) * BANK])
                    ins = product(ps[:, 2 * t + half, :], kt(c, t), rhs, first, last)
                return ins

            def row_unit(slots, c, last):
                s = slots[c]
                made(s, take(s))
                for t in range(TT):
                    ins = row_chunk(s, c, t, c == 0, last)
                ins.then_inc(slot_used[s], 1)

            def end_rows(slots, chunks, k):
                tail = range(chunks - 4, chunks)
                for t in range(TT):
                    for c in tail:
                        if t == 0:
                            made(slots[c], take(slots[c]))
                        if t == 1 and c == chunks - 1:
                            flip_h(k, 0)
                        ins = row_chunk(slots[c], c, t, c == 0, c == chunks - 1)
                        if t:
                            ins.then_inc(slot_used[slots[c]], 1)
                    if t == 0:
                        ins.then_inc(sem("tile0_done"), 1)

            def hid_turn(bank, t, at):
                for c in range(2):
                    ins = nc.tensor.transpose(ps[:, bank, at(c):at(c) + P], hid[:, t, c * P:(c + 1) * P], ident[:])
                return ins

            def ffn_first(k):
                opening(k, lambda s: use[s])
                for s in range(4):
                    take(s)

            def ffn_rest():
                b, b_ht = seen.get("hid_ready", 0), seen.get("hid_full", 0)
                base = [n - 1 for n in use[:4]] + use[4:]
                def hid_flip(j):
                    pe.wait_ge(sem("hid_ready"), j * 2 + (b + 2))
                    for t in range(TT):
                        ins = hid_turn(6, t, lambda c: c * S + t * P)
                    ins.then_inc(sem("hid_full"), 1)

                def down_chunk(f, t, last, first=False):
                    for half in range(2):
                        rhs = slot(4 + f, lambda x: x[:, half * BANK:(half + 1) * BANK])
                        ins = product(ps[:, 2 * t + half, :], ht(f, t), rhs, first and f == 0, last and f == 1)
                    return ins

                def down(j, first=False):
                    pe.wait_ge(sem("ht_low"), j + (b_ht + 1))
                    for f in range(2):
                        made(4 + f, j + base[4 + f])
                        for t in range(TT):
                            ins = down_chunk(f, t, False, first)
                        ins.then_inc(slot_used[4 + f], 1)

                def gate_up(j, t):
                    for s in range(4):
                        made(s, j + base[s])
                        for c in range(2):
                            k = 2 * s + c
                            ins = product(ps[:, 4 + t, :], kt(k, t), slot(s, lambda x: x[:, c * BANK:(c + 1) * BANK]),
                                          k == 0, k == KC - 1)
                        if t:
                            ins.then_inc(slot_used[s], 1)
                    return ins

                pe.wait_ge(sem("hid_ready"), b + 1)
                gate_up(1, 0)
                hid_flip(0)
                gate_up(1, 1)
                down(0, first=True)
                hid_flip(1)
                with pe.Fori(2, NF - 1) as j:
                    tile_product(lambda s: j + base[s])
                    down(j - 1)
                    hid_flip(j)
                last = NF - 1
                gate_up(last, 0).then_inc(sem("tile0_done"), 1)
                down(last - 1)
                pe.wait_ge(sem("hid_ready"), b + 2 * last + 1)
                hid_turn(6, 0, lambda c: c * P).then_inc(sem("hid_full"), 1)
                gate_up(last, 1)
                pe.wait_ge(sem("ht_low"), b_ht + NF)
                for f in range(2):
                    made(4 + f, last + base[4 + f])
                down_chunk(0, 0, True)
                pe.wait_ge(sem("hid_ready"), b + 2 * NF)
                hid_turn(7, 1, lambda c: c * P).then_inc(sem("hid_full"), 1)
                down_chunk(1, 0, True).then_inc(sem("tile0_done"), 1)
                pe.wait_ge(sem("ht_low"), b_ht + NF + 1)
                for f in range(2):
                    down_chunk(f, 1, True).then_inc(slot_used[4 + f], 1)
                for s in range(SLOTS):
                    use[s] += NF - 1 + (s >= 4)
                count("hid_ready", 2 * NF)
                count("hid_full", NF + 1)

            def wide(pairs, k=None, between=None):
                base, b = list(use), seen.get("wide_read", 0)

                def tile(i, par, first=False):
                    pe.wait_ge(sem("wide_read"), i * 2 + (b + par + 1))
                    if first:
                        opening(k, lambda s: base[s])
                    else:
                        tile_product(lambda s: i * 2 + (base[s] + par), bank=4 + 2 * par)

                tile(0, 0, k is not None)
                tile(0, 1)
                if between:
                    between()
                with pe.Fori(1, pairs) as i:
                    for par in range(2):
                        tile(i, par)
                for s in range(4):
                    use[s] += 2 * pairs
                count("wide_read", 2 * pairs)

            pe.wait_ge(sem("ident_in"), 16)
            pe.wait_ge(sem("early_in"), 16)
            nc.tensor.transpose(ps[:, 5, 0:early_rows], grow[0:early_rows, :], ident[0:early_rows, 0:early_rows]
                                ).then_inc(sem("gcol_full"), 1)
            flip_h(0, 0)
            pe.wait_ge(sem("gcol_ready"), 1)
            ffn_first(0)
            pe.wait_ge(sem("late_in"), 16 * (len(gain_rows) - 1))
            late = row - early_rows
            nc.tensor.transpose(ps[:, 7, 0:late], grow_late[0:late, :], ident[0:late, 0:late]).then_inc(sem("gcol_full"), 1)
            ffn_rest()
            flip_h(1, 0)

            def spatial_weights():
                pe.wait_ge(sem("ws_masked"), 1)
                for r in range(GROUPS // 4):
                    turn(r, lambda c: ws_sb[:, 4 * r + c, :]).then_inc(sem("wst_full"), 1)

            wide(4, 1, spatial_weights)
            pe.wait_ge(sem("v_ready"), TT)
            pe.wait_ge(sem("wide_read"), 2 + 8)
            pe.wait_ge(sem("wst_ready"), 4)

            def spatial(r):
                for g in (2 * r, 2 * r + 1):
                    ins = nc.tensor.matmul(ps[:, 4 + r % 2, (g % 2) * S:(g % 2) * S + S], wst[:, g, :],
                                           v_sb[:, :, g * GD:(g + 1) * GD], start=True, stop=True)
                ins.then_inc(sem("spatial_full"), 1)

            def gmlp_out(r):
                pe.wait_ge(sem("kt_ready"), kt_base + r + 1)
                for c in (2 * r, 2 * r + 1):
                    s = W_OUT[c]
                    made(s, take(s))
                    for t in range(TT):
                        ins = row_chunk(s, c, t, c == 0, False)
                    ins.then_inc(slot_used[s], 1)

            spatial(0)
            spatial(1)
            kt_base = seen["kt_ready"]
            for r in range(GROUPS // 2):
                pe.wait_ge(sem("mixed"), r + 1)
                if r >= 2:
                    pe.wait_ge(sem("kt_ready"), kt_base + r - 1)
                for c in range(2):
                    for t in range(TT):
                        ins = nc.tensor.transpose(ps[:, 6 + r % 2, c * S + t * P:c * S + t * P + P],
                                                  u_sb[:, t, (2 * r + c) * GD:(2 * r + c + 1) * GD], ident[:])
                ins.then_inc(sem("flip_full"), 1)
                if r + 2 < GROUPS // 2:
                    spatial(r + 2)
                if 1 <= r <= 6:
                    gmlp_out(r - 1)
            pe.wait_ge(sem("kt_ready"), kt_base + GROUPS // 2)
            count("kt_ready", GROUPS // 2)
            end_rows(W_OUT, GROUPS, 2)
            ffn_first(2)
            ffn_rest()
            flip_h(3, 0)
            opening(3, lambda s: use[s], width=R_KV + ROPE)
            for s in range(4):
                take(s)
            pe.wait_ge(sem("ckv_ready"), TT)
            tile_product(lambda s: use[s])
            for s in range(4):
                take(s)
            pe.wait_ge(sem("ckv_normed"), 1)
            for c in range(2):
                for t in range(TT):
                    ins = nc.tensor.transpose(ps[:, 6, c * S + t * P:c * S + t * P + P], ckv[:, t, c * P:(c + 1) * P], ident[:])
            ins.then_inc(sem("flip_full"), 1)
            pe.wait_ge(sem("krope_ready"), 1)
            for t in range(TT):
                ins = nc.tensor.transpose(ps[:, 7, t * P:(t + 1) * P], krope2[:, t, :, :].rearrange("p c n -> p (c n)"), ident[:])
            ins.then_inc(sem("krt_full"), 1)
            pe.wait_ge(sem("kt_ready"), count("kt_ready"))
            pe.wait_ge(sem("krt_ready"), 1)
            pe.wait_ge(sem("hid_ready"), seen["hid_ready"] + TT)
            for half in range(2):
                units = UKV[2 * half:2 * half + 2]
                for s in units:
                    made(s, take(s))
                for b in range(2):
                    if half:
                        pe.wait_ge(sem("knt_ready"), b + 1)
                    for e in range(2):
                        at_ = (2 * b + e) * KVW
                        for c, s in enumerate(units):
                            ins = product(ps[:, 4 + b, e * S:(e + 1) * S], slot(s, lambda x: x[:, at_:at_ + P]), kt(8 + c),
                                          c == 0, c == 1)
                    ins.then_inc(sem("knt_full"), 1)
                if half:
                    pe.wait_ge(sem("v_read"), 1)
                for t in range(TT):
                    for c, s in enumerate(units):
                        ins = product(ps[:, 6 + t, :], kt(8 + c, t),
                                      slot(s, lambda x: x.rearrange("p (h n) -> p h n", h=4)[:, :, P:2 * P]), c == 0, c == 1)
                        if t == TT - 1:
                            ins.then_inc(slot_used[s], 1)
            pe.wait_ge(sem("knt_ready"), 4)
            pe.wait_ge(sem("v_read"), 2)
            ffn_rest()
            flip_h(4, 0)
            opening(4, lambda s: use[s])
            for s in range(4):
                take(s)
            for t in range(TT):
                pe.wait_ge(sem("qlat_ready"), t + 1)
                flip(t, lambda c, t: qlat[:, t, c * P:(c + 1) * P], (6 + t,))
            pe.wait_ge(sem("kt_ready"), seen["kt_ready"])
            def q_rope(half):
                units = UQ[4 * half:4 * half + 4]
                for s in units:
                    made(s, take(s))
                for t in range(TT):
                    for c, s in enumerate(units):
                        ins = product(ps[:, ROPE_BANK[half], t * 4 * ROPE:(t + 1) * 4 * ROPE], kt(c, t),
                                      slot(s, lambda x: x[:, 0:4 * QW].rearrange("p (h n) -> p h n", h=4)[:, :, P:QW]),
                                      c == 0, c == 3)
                ins.then_inc(sem("qrope_full"), 1)

            def q_nope(half, b):
                units = UQ[4 * half:4 * half + 4]
                for e in range(2):
                    at_ = (2 * b + e) * QW
                    for c, s in enumerate(units):
                        ins = product(ps[:, NOPE_BANK[half][b], e * S:(e + 1) * S], slot(s, lambda x: x[:, at_:at_ + P]), kt(c),
                                      c == 0, c == 3)
                        if b and e:
                            ins.then_inc(slot_used[s], 1)

            def turn_queries(half):
                pe.wait_ge(sem("qrope_ready"), half + 1)
                for c in range(2):
                    for t in range(TT):
                        at_ = 4 * half + 2 * c
                        ins = nc.tensor.transpose(ps[:, 0, c * S + t * P:c * S + t * P + P],
                                                  qrope[:, t, at_:at_ + 2, :].rearrange("p h r -> p (h r)"), ident[:])
                ins.then_inc(sem("qrt_full"), 1)

            q_rope(0)
            q_nope(0, 0)
            q_nope(0, 1)
            turn_queries(0)

            def attention(kind, scores, output, probs, probs_ready, turned_probs, filler):
                def turn_probs(i):
                    pe.wait_ge(sem(probs_ready), i + 1)
                    if i >= 1:
                        pe.wait_ge(sem(kind + "_pt_ready"), i)
                    turn(6, lambda b: probs[:, i % 3, b * P:(b + 1) * P], 3).then_inc(sem(kind + "_pt_full"), 1)

                for i in range(H + 3):
                    if i < H:
                        if i >= 2:
                            pe.wait_ge(sem(kind + "_masked"), i - 1)
                        scores(i).then_inc(sem(kind + "_scores_full"), 1)
                    if 2 <= i < H + 2:
                        turn_probs(i - 2)
                    filler(i)
                    if i >= 3:
                        pe.wait_ge(sem(kind + "_pt_ready"), i - 2)
                        output(i - 3, turned_probs[:, (i - 3) % 2, :])

            def mla_scores(i):
                bank, e = ps[:, 4 + i % 2, :], ROPE * (i % 2)
                if i == 4:
                    pe.wait_ge(sem("qnt_ready"), 4)
                    pe.wait_ge(sem("qrt_ready"), 2)
                for t in range(TT):
                    dst = bank[:, 0:P] if t == 0 else bank[:, P:3 * P]
                    keys, q = slice(0, (t + 1) * P), slice(t * P, (t + 1) * P)
                    nc.tensor.matmul(dst, qnt[:, i, q], knt[:, i, keys], start=True, stop=False)
                    ins = nc.tensor.matmul(dst, qrt[e:e + ROPE, i // 2, q], krt[e:e + ROPE, keys], start=False, stop=True)
                return ins

            def mla_output(i, pt):
                at_ = (i % 2) * S
                bank, v = 7, v_mla[:, :, i * P:(i + 1) * P]
                if i % 2 == 0 and i:
                    pe.wait_ge(sem("kt_ready"), kt_mla + i // 2)
                nc.tensor.matmul(ps[:, bank, at_:at_ + S], v[:, 0, :], pt[:, 0:S], start=True, stop=False)
                ins = nc.tensor.matmul(ps[:, bank, at_ + P:at_ + S], v[:, 1, :], pt[:, S:3 * P], start=False, stop=True)
                if i % 2:
                    ins.then_inc(sem("flip_full"), 1)

            pe.wait_ge(sem("qnt_ready"), 2)
            pe.wait_ge(sem("qrt_ready"), 1)
            kt_mla = seen["kt_ready"]

            def mla_out(i):
                if i == 1:
                    q_rope(1)
                if 2 <= i < 4:
                    q_nope(1, i - 2)
                if i == 3:
                    turn_queries(1)
                if 6 <= i < 10:
                    pe.wait_ge(sem("kt_ready"), kt_mla + (i - 6) // 2 + 1)
                    row_unit(WO, i - 6, False)

            attention("mla", mla_scores, mla_output, p_sb, "mla_p_ready", pt_sb, mla_out)
            pe.wait_ge(sem("kt_ready"), count("kt_ready", H // 2))
            end_rows(WO, H, 5)
            ffn_first(5)
            ffn_rest()
            flip_h(6, 0)
            wide(3, 6)
            made(4, take(4))
            for c in range(KC):
                for t in range(TT):
                    ins = product(ps[:, t, 0:8], kt(c, t), slot(4, lambda x: x[:, 8 * c:8 * c + 8]), c == 0, c == KC - 1)
            ins.then_inc(slot_used[4], 1)
            wide(2)
            pe.wait_ge(sem("r_rotated"), 1)
            pe.wait_ge(sem("wide_read"), 20)
            for r in range(2):
                for c in range(2):
                    for t in range(TT):
                        at_ = (2 * r + c) * P
                        ins = nc.tensor.transpose(ps[:, 6 + r, c * S + t * P:c * S + t * P + P], ro_t[:, t, at_:at_ + P], ident[:])
                ins.then_inc(sem("rqk_full"), 1)
            pe.wait_ge(sem("rqk_ready"), 2)
            pe.wait_ge(sem("f_ready"), 1)
            pe.wait_ge(sem("logf_ready"), 1)
            pe.wait_ge(sem("cum_c_in"), 32)
            nc.tensor.matmul(ps[:, 2, 0:8], upto, logf[:, 0, 0:8], start=True, stop=True)
            nc.tensor.matmul(ps[:, 2, 8:16], upto, logf[:, 0, 8:16], start=True, stop=False)
            nc.tensor.matmul(ps[:, 2, 8:16], ones, logf[:, 0, 0:8], start=False, stop=True).then_inc(sem("cum_full"), 1)
            pe.wait_ge(sem("cum_ready"), 1)
            for t in range(TT):
                ins = nc.tensor.transpose(ps[0:8, 3, t * P:(t + 1) * P], cum[:, t, :], ident[:])
            ins.then_inc(sem("cumt_full"), 1)
            for i in range(HR + 1):
                if i < HR:
                    e = ROPE * (i % 2)
                    q, key = turned[e:e + ROPE, i // 2, :], turned[e:e + ROPE, 2 + i // 2, :]
                    if i >= 2:
                        pe.wait_ge(sem("rst_ready"), i - 1)
                    nc.tensor.matmul(ps[:, 4 + i % 2, 0:S], key[:, 0:P], q[:, 0:S], start=True, stop=True)
                    nc.tensor.matmul(ps[:, 4 + i % 2, S:3 * P], key[:, P:S], q[:, P:S], start=True, stop=True
                                     ).then_inc(sem("rst_full"), 1)
                if i >= 1:
                    j = i - 1
                    pe.wait_ge(sem("rst_ready"), j + 1)
                    w, v = st_sb[:, j % 2, :], z[:, :, Z_VR + j * P:Z_VR + (j + 1) * P]
                    nc.tensor.matmul(ps[:, 0, j * P:(j + 1) * P], w[:, 0:P], v[:, 0, :], start=True, stop=True)
                    nc.tensor.matmul(ps[:, 1, j * P:(j + 1) * P], w[:, P:S], v[:, 0, :], start=True, stop=False)
                    nc.tensor.matmul(ps[:, 1, j * P:(j + 1) * P], w[:, S:3 * P], v[:, 1, :], start=False, stop=True
                                     ).then_inc(sem("rpv_done"), 1)
            pe.wait_ge(sem("fqk_normed"), 1)
            for r in range(4):
                for t in range(TT):
                    for c in range(2):
                        at_ = Z_QF + (2 * r + c) * P
                        ins = nc.tensor.transpose(ps[:, 4 + r, c * S + t * P:c * S + (t + 1) * P], z[:, t, at_:at_ + P], ident[:])
                ins.then_inc(sem("fqk_full"), 1)
            pe.wait_ge(sem("fqk_ready"), 4)
            pe.wait_ge(sem("ncumt_ready"), 1)
            pe.wait_ge(sem("sel_in"), 16)

            def fox_scores(i):
                bank, e = ps[:, 4 + i % 2, :], 64 * (i % 2)
                q, key = turned[e:e + 64, i // 2, :], turned[e:e + 64, 4 + i // 2, :]
                for t in range(TT):
                    dst = bank[:, 0:P] if t == 0 else bank[:, P:3 * P]
                    keys = slice(0, (t + 1) * P)
                    nc.tensor.matmul(dst, q[:, t * P:(t + 1) * P], key[:, keys], start=True, stop=False)
                    ins = nc.tensor.matmul(dst, sel[0:8, i, :], ncumt[:, keys], start=False, stop=True)
                return ins

            def fox_output(i, pt):
                v = z[:, :, Z_VF + i * 64:Z_VF + (i + 1) * 64]
                if i == H // 2:
                    pe.wait_ge(sem("fo_ready"), TT)
                at0, at1 = ((4 * t + i % 4) * 64 for t in range(TT))
                nc.tensor.matmul(ps[:, 7, at0:at0 + 64], pt[:, 0:P], v[:, 0, :], start=True, stop=True)
                nc.tensor.matmul(ps[:, 7, at1:at1 + 64], pt[:, P:S], v[:, 0, :], start=True, stop=False)
                ins = nc.tensor.matmul(ps[:, 7, at1:at1 + 64], pt[:, S:3 * P], v[:, 1, :], start=False, stop=True)
                if i % 4 == 3:
                    ins.then_inc(sem("fpv_full"), 1)

            def ret_out(i):
                if i == 1:
                    for t in range(TT):
                        pe.wait_ge(sem("ro_ready"), t + 1)
                        flip(t, lambda c, t: ro_t[:, t, c * P:(c + 1) * P], (6 + t,))
                    pe.wait_ge(sem("kt_ready"), seen["kt_ready"])
                if 2 <= i < 6:
                    row_unit(RET_O, i - 2, i == 5)

            attention("fox", fox_scores, fox_output, p2_sb, "fox_exp_done", pt2_sb, ret_out)
            pe.wait_ge(sem("yr_read"), 1)
            for t in range(TT):
                pe.wait_ge(sem("fo_ready"), TT + t + 1)
                if t:
                    pe.wait_ge(sem("fo_ready"), 2 * TT)
                flip(t, lambda c, t: z[:, t, Z_QF + c * P:Z_QF + (c + 1) * P], (6 + t,))

            def flip_merged(t):
                pe.wait_ge(sem("merged"), t + 1)
                flip(t, lambda c, t: fg[:, t, c * P:(c + 1) * P], (4 + 2 * t, 5 + 2 * t))

            fox_kt = seen["kt_ready"]
            for t in range(TT):
                pe.wait_ge(sem("kt_ready"), fox_kt - 1 + t)
                for c in range(4):
                    if t == 0:
                        made(FOX_O[c], take(FOX_O[c]))
                    elif c == 3:
                        flip_merged(0)
                    ins = row_chunk(FOX_O[c], c, t, c == 0, c == 3)
                    if t:
                        ins.then_inc(slot_used[FOX_O[c]], 1)
                if t == 0:
                    ins.then_inc(sem("tile0_done"), 1)
            for t in range(TT):
                pe.wait_ge(sem("kt_ready"), fox_kt + 2 * t + 1)
                for c in range(4):
                    if t == 0:
                        made(OUT2[c], take(OUT2[c]))
                        if c == 2:
                            flip_merged(1)
                    ins = row_chunk(OUT2[c], c, t, c == 0, False)
                    if t:
                        ins.then_inc(slot_used[OUT2[c]], 1)
            pe.wait_ge(sem("kt_ready"), fox_kt + 4)
            end_rows(OUT2, KC, 7)
            ffn_first(7)
            ffn_rest()


OUT_SHAPE = (1, 256, 1024)


def kernel(**inputs):
    import concourse.bacc as bacc
    from concourse.bass_utils import run_bass_kernel_spmd

    nc = bacc.Bacc("TRN2", target_bir_lowering=False, num_devices=1)
    arrays = {name: np.ascontiguousarray(x) for name, x in inputs.items()}
    rope = arrays["w_dkv"].shape[1] - arrays["kv_a_norm_g"].shape[0]
    arrays.update(shape_constants(arrays["x"].shape[1], rope, 4))
    aps, sent = {}, {}
    for name, x in arrays.items():
        sent["in_" + name] = x
        aps[name] = nc.dram_tensor("in_" + name, x.shape, mybir.dt.from_np(x.dtype), kind="ExternalInput").ap()
    out = nc.dram_tensor("out", OUT_SHAPE, F32, kind="ExternalOutput").ap()
    build(nc, aps, out)
    return run_bass_kernel_spmd(nc, [sent], core_ids=[0]).results[0]["out"]
```
